# Optimizing a Trainium2 kernel written in Bass

```python
import jax
import jax.numpy as jnp
from jax import lax
import numpy as np
import math
import jax, jax.numpy as jnp

D_MODEL = 1024
BATCH = 1
SEQ = 256
DEPTH = 1

HEAD_DIM = 64
MIX_WIDTH = D_MODEL
NSA_HEADS = MIX_WIDTH // 2 // HEAD_DIM
NSA_KV_HEADS = 2
SWA_HEADS = MIX_WIDTH // 2 // HEAD_DIM
SWA_KV_HEADS = 2
CMP_BLOCK = 32
CMP_STRIDE = 16
CMP_HIDDEN = 256
SEL_BLOCK = 64
SEL_TOPK = 16
SEL_Q_CHUNK = 64
NSA_WINDOW = 512
SWA_WINDOW = 128
BAND_BLOCK = 128
N_NSA_BRANCHES = 3
D_FF = 2816
NORM_EPS = 1e-6
NEG_INF = -1e30
FORCE_SCORE = 1e9
ATTN_SCALE = HEAD_DIM ** -0.5
PROJ_SPLITS = (NSA_HEADS * HEAD_DIM, 2 * N_NSA_BRANCHES * NSA_KV_HEADS * HEAD_DIM, N_NSA_BRANCHES * NSA_HEADS, SWA_HEADS * HEAD_DIM, 2 * SWA_KV_HEADS * HEAD_DIM)
PROJ_WIDTH = sum(PROJ_SPLITS)


def alibi_slopes(n_heads, n_groups):
    slopes = 2.0 ** (-8.0 * np.arange(1, n_heads + 1) / n_heads)
    return jnp.asarray(slopes.reshape(n_groups, n_heads // n_groups), jnp.float32)

def rmsnorm(x, g):
    xf = x.astype(jnp.float32)
    y = xf * lax.rsqrt(jnp.mean(xf * xf, axis=-1, keepdims=True) + NORM_EPS)
    return (y * g.astype(jnp.float32)).astype(x.dtype)

def swiglu(x, w_in, w_out):
    gate, up = jnp.split(x @ w_in, 2, axis=-1)
    return (jax.nn.silu(gate) * up) @ w_out

def banded_attention(q, k, v, slopes, window, sinks=None):
    B, T, G, R, D = q.shape
    nb = T // BAND_BLOCK
    n_prev = -(-(window - 1) // BAND_BLOCK)
    pad = n_prev * BAND_BLOCK
    kw_len = (n_prev + 1) * BAND_BLOCK
    kp = jnp.pad(k, ((0, 0), (pad, 0), (0, 0), (0, 0))).reshape(B, nb + n_prev, BAND_BLOCK, G, D)
    vp = jnp.pad(v, ((0, 0), (pad, 0), (0, 0), (0, 0))).reshape(B, nb + n_prev, BAND_BLOCK, G, D)
    kw = jnp.concatenate([kp[:, j:j + nb] for j in range(n_prev + 1)], axis=2)
    vw = jnp.concatenate([vp[:, j:j + nb] for j in range(n_prev + 1)], axis=2)
    qb = q.reshape(B, nb, BAND_BLOCK, G, R, D)
    s = jnp.einsum('bnqgrd,bnkgd->bngrqk', qb, kw) * ATTN_SCALE
    t_pos = np.arange(nb)[:, None] * BAND_BLOCK + np.arange(BAND_BLOCK)[None, :]
    s_pos = np.arange(nb)[:, None] * BAND_BLOCK - pad + np.arange(kw_len)[None, :]
    dist = t_pos[:, :, None] - s_pos[:, None, :]
    mask = jnp.asarray((dist >= 0) & (dist < window) & (s_pos[:, None, :] >= 0))
    bias = -slopes[None, :, :, None, None] * jnp.asarray(dist, jnp.float32)[:, None, None]
    s = jnp.where(mask[:, None, None], s + bias, NEG_INF)
    if sinks is not None:
        sink = jnp.broadcast_to(sinks[None, None, :, :, None, None], s.shape[:-1] + (1,))
        p = jax.nn.softmax(jnp.concatenate([s, sink], axis=-1), axis=-1)[..., :-1]
    else:
        p = jax.nn.softmax(s, axis=-1)
    o = jnp.einsum('bngrqk,bnkgd->bnqgrd', p, vw)
    return o.reshape(B, T, G, R, D)

def compress_blocks(kr, pos, w1, b1, w2):
    B, T, G, D = kr.shape
    nc = (T - CMP_BLOCK) // CMP_STRIDE + 1
    idx = np.arange(nc)[:, None] * CMP_STRIDE + np.arange(CMP_BLOCK)[None, :]
    blk = kr[:, idx] + pos[None, None, :, None, :]
    flat = blk.transpose(0, 1, 3, 2, 4).reshape(B, nc, G, CMP_BLOCK * D)
    return jax.nn.gelu(flat @ w1 + b1) @ w2

def selected_attention(q, k, v, sel_idx, slopes):
    B, T, G, R, D = q.shape
    ns = T // SEL_BLOCK
    n_sel = sel_idx.shape[-1]
    nq = T // SEL_Q_CHUNK
    kb = k.reshape(B, ns, SEL_BLOCK, G, D).transpose(0, 3, 1, 2, 4)
    vb = v.reshape(B, ns, SEL_BLOCK, G, D).transpose(0, 3, 1, 2, 4)
    qc = q.reshape(B, nq, SEL_Q_CHUNK, G, R, D).transpose(1, 0, 2, 3, 4, 5)
    ic = sel_idx.reshape(B, nq, SEL_Q_CHUNK, G, n_sel).transpose(1, 0, 2, 3, 4)
    tc = jnp.arange(T).reshape(nq, SEL_Q_CHUNK)
    b_ix = jnp.arange(B)[:, None, None, None]
    g_ix = jnp.arange(G)[None, None, :, None]

    def chunk(args):
        qx, ix, tx = args
        kg = kb[b_ix, g_ix, ix]
        vg = vb[b_ix, g_ix, ix]
        s = jnp.einsum('bcgrd,bcgkld->bcgrkl', qx, kg) * ATTN_SCALE
        spos = ix[..., None] * SEL_BLOCK + jnp.arange(SEL_BLOCK)
        dist = tx[None, :, None, None, None] - spos
        mask = (dist >= 0)[:, :, :, None]
        bias = -slopes[None, None, :, :, None, None] * dist.astype(jnp.float32)[:, :, :, None]
        s = jnp.where(mask, s + bias, NEG_INF)
        C = qx.shape[1]
        p = jax.nn.softmax(s.reshape(B, C, G, R, n_sel * SEL_BLOCK), axis=-1).reshape(s.shape)
        return jnp.einsum('bcgrkl,bcgkld->bcgrd', p, vg)

    o = lax.map(chunk, (qc, ic, tc))
    return o.transpose(1, 0, 2, 3, 4, 5).reshape(B, T, G, R, D)

def nsa_group(q, kc_raw, vc_raw, ks, vs, kw, vw, gate_logits, ck_pos, ck_w1, ck_b1, ck_w2, cv_pos, cv_w1, cv_b1, cv_w2, slopes):
    B, T, G, R, D = q.shape
    kc = compress_blocks(kc_raw, ck_pos, ck_w1, ck_b1, ck_w2).astype(jnp.float32)
    vc = compress_blocks(vc_raw, cv_pos, cv_w1, cv_b1, cv_w2).astype(jnp.float32)
    nc = kc.shape[1]
    blk_end = np.arange(nc) * CMP_STRIDE + CMP_BLOCK - 1
    dist_c = np.arange(T)[:, None] - blk_end[None, :]
    mask_c = jnp.asarray(dist_c >= 0)
    s = jnp.einsum('btgrd,bcgd->bgrtc', q, kc) * ATTN_SCALE
    s = jnp.where(mask_c, s - slopes[:, :, None, None] * jnp.asarray(dist_c, jnp.float32), NEG_INF)
    p_cmp = jnp.where(mask_c, jax.nn.softmax(s, axis=-1), 0.0)
    o_cmp = jnp.einsum('bgrtc,bcgd->btgrd', p_cmp, vc)
    ns = T // SEL_BLOCK
    c_start = np.arange(nc) * CMP_STRIDE
    s_start = np.arange(ns) * SEL_BLOCK
    overlap = np.clip(np.minimum(c_start[:, None] + CMP_BLOCK, s_start[None, :] + SEL_BLOCK) - np.maximum(c_start[:, None], s_start[None, :]), 0, None) / CMP_BLOCK
    p_slc = jnp.einsum('bgrtc,cs->btgs', p_cmp, jnp.asarray(overlap, jnp.float32))
    cur = np.arange(T) // SEL_BLOCK
    blk = np.arange(ns)
    valid = jnp.asarray(blk[None, :] <= cur[:, None])[None, :, None, :]
    forced = jnp.asarray((blk[None, :] == 0) | (blk[None, :] == cur[:, None]) | (blk[None, :] == cur[:, None] - 1))[None, :, None, :]
    score = jnp.where(forced, FORCE_SCORE, jnp.where(valid, p_slc, NEG_INF))
    _, sel_idx = lax.top_k(score, min(SEL_TOPK, ns))
    o_slc = selected_attention(q, ks, vs, sel_idx, slopes)
    o_win = banded_attention(q, kw, vw, slopes, NSA_WINDOW)
    g = jax.nn.sigmoid(gate_logits)
    return g[..., 0:1] * o_cmp + g[..., 1:2] * o_slc + g[..., 2:3] * o_win

def hybrid_mixer(xn, w_in, ck_pos, ck_w1, ck_b1, ck_w2, cv_pos, cv_w1, cv_b1, cv_w2, sinks, w_out):
    B, T, _ = xn.shape
    D = HEAD_DIM
    ga, ra = NSA_KV_HEADS, NSA_HEADS // NSA_KV_HEADS
    gb, rb = SWA_KV_HEADS, SWA_HEADS // SWA_KV_HEADS
    proj = (xn @ w_in).astype(jnp.float32)
    offsets = [int(o) for o in np.cumsum(PROJ_SPLITS)[:-1]]
    q_a, kv_a, gate_a, q_b, kv_b = jnp.split(proj, offsets, axis=-1)
    q_a = q_a.reshape(B, T, ga, ra, D)
    kc_raw, vc_raw, ks, vs, kw, vw = [t.reshape(B, T, ga, D) for t in jnp.split(kv_a, 2 * N_NSA_BRANCHES, axis=-1)]
    gate_a = gate_a.reshape(B, T, ga, ra, N_NSA_BRANCHES)
    o_a = nsa_group(q_a, kc_raw, vc_raw, ks, vs, kw, vw, gate_a, ck_pos, ck_w1, ck_b1, ck_w2, cv_pos, cv_w1, cv_b1, cv_w2, alibi_slopes(NSA_HEADS, NSA_KV_HEADS))
    q_b = q_b.reshape(B, T, gb, rb, D)
    k_b, v_b = [t.reshape(B, T, gb, D) for t in jnp.split(kv_b, 2, axis=-1)]
    o_b = banded_attention(q_b, k_b, v_b, alibi_slopes(SWA_HEADS, SWA_KV_HEADS), SWA_WINDOW, sinks.astype(jnp.float32).reshape(gb, rb))
    o = jnp.concatenate([o_a.reshape(B, T, NSA_HEADS * D), o_b.reshape(B, T, SWA_HEADS * D)], axis=-1)
    return o.astype(xn.dtype) @ w_out

def first_inputs(seed: int = 0) -> dict:
    key = jax.random.key(seed)
    ks = jax.random.split(key, 24)
    L = DEPTH

    def nrm(k, shape, fan_in):
        return jax.random.normal(k, shape, jnp.float32) * fan_in ** -0.5

    def gain(k, shape):
        return 1.0 + 0.1 * jax.random.normal(k, shape, jnp.float32)

    return {
        'x': jax.random.normal(ks[0], (BATCH, SEQ, D_MODEL), jnp.float32),
        'ffn1_norm': gain(ks[1], (L, D_MODEL)),
        'ffn1_w_in': nrm(ks[2], (L, D_MODEL, 2 * D_FF), D_MODEL),
        'ffn1_w_out': nrm(ks[3], (L, D_FF, D_MODEL), D_FF),
        'mix_norm': gain(ks[4], (L, D_MODEL)),
        'w_mix_in': nrm(ks[5], (L, D_MODEL, PROJ_WIDTH), D_MODEL),
        'cmp_k_pos': 0.5 * jax.random.normal(ks[6], (L, CMP_BLOCK, HEAD_DIM), jnp.float32),
        'cmp_k_w1': nrm(ks[7], (L, CMP_BLOCK * HEAD_DIM, CMP_HIDDEN), CMP_BLOCK * HEAD_DIM),
        'cmp_k_b1': 0.02 * jax.random.normal(ks[8], (L, CMP_HIDDEN), jnp.float32),
        'cmp_k_w2': nrm(ks[9], (L, CMP_HIDDEN, HEAD_DIM), CMP_HIDDEN),
        'cmp_v_pos': 0.5 * jax.random.normal(ks[10], (L, CMP_BLOCK, HEAD_DIM), jnp.float32),
        'cmp_v_w1': nrm(ks[11], (L, CMP_BLOCK * HEAD_DIM, CMP_HIDDEN), CMP_BLOCK * HEAD_DIM),
        'cmp_v_b1': 0.02 * jax.random.normal(ks[12], (L, CMP_HIDDEN), jnp.float32),
        'cmp_v_w2': nrm(ks[13], (L, CMP_HIDDEN, HEAD_DIM), CMP_HIDDEN),
        'swa_sinks': 0.5 * jax.random.normal(ks[14], (L, SWA_HEADS), jnp.float32),
        'w_mix_out': nrm(ks[15], (L, MIX_WIDTH, D_MODEL), MIX_WIDTH),
        'ffn2_norm': gain(ks[16], (L, D_MODEL)),
        'ffn2_w_in': nrm(ks[17], (L, D_MODEL, 2 * D_FF), D_MODEL),
        'ffn2_w_out': nrm(ks[18], (L, D_FF, D_MODEL), D_FF),
        'final_norm': gain(ks[19], (D_MODEL,)),
    }

def first_block(x, ffn1_norm, ffn1_w_in, ffn1_w_out, mix_norm, w_mix_in, cmp_k_pos, cmp_k_w1, cmp_k_b1, cmp_k_w2, cmp_v_pos, cmp_v_w1, cmp_v_b1, cmp_v_w2, swa_sinks, w_mix_out, ffn2_norm, ffn2_w_in, ffn2_w_out, final_norm):
    h = x
    for l in range(DEPTH):
        h = h + 0.5 * swiglu(rmsnorm(h, ffn1_norm[l]), ffn1_w_in[l], ffn1_w_out[l])
        h = h + hybrid_mixer(rmsnorm(h, mix_norm[l]), w_mix_in[l], cmp_k_pos[l], cmp_k_w1[l], cmp_k_b1[l], cmp_k_w2[l], cmp_v_pos[l], cmp_v_w1[l], cmp_v_b1[l], cmp_v_w2[l], swa_sinks[l], w_mix_out[l])
        h = h + 0.5 * swiglu(rmsnorm(h, ffn2_norm[l]), ffn2_w_in[l], ffn2_w_out[l])
    return rmsnorm(h, final_norm)


DEPTH_2 = 2

CHUNK = 64
MEM_LEN = 256
QBLOCK = 128
EPS = 1e-6

DIFF_HEADS = 4
DIFF_DK = 64
DIFF_DV = 2 * DIFF_DK
DIFF_SCALE = DIFF_DK ** -0.5
MLA_HEADS = 4
MLA_NOPE = 128
MLA_ROPE = 64
MLA_DV = 128
MLA_Q_LORA = 256
MLA_KV_LORA = 128
MLA_SCALE = (MLA_NOPE + MLA_ROPE) ** -0.5
ROPE_BASE = 10000.0
EVEN_SPLITS = (DIFF_HEADS * 2 * DIFF_DK, DIFF_HEADS * 2 * DIFF_DK, DIFF_HEADS * DIFF_DV, MLA_Q_LORA, MLA_KV_LORA, MLA_ROPE)
EVEN_IN = sum(EVEN_SPLITS)
EVEN_MIX = DIFF_HEADS * DIFF_DV + MLA_HEADS * MLA_DV
SB_HEADS = 16
SB_DH = 64
SB_WIDTH = SB_HEADS * SB_DH
SB_SCALE = SB_DH ** -0.5
XA_HEADS = 4
XA_DH = D_MODEL // XA_HEADS
D_FF_2 = 4 * D_MODEL

N_EVEN = (DEPTH_2 + 1) // 2
N_ODD = DEPTH_2 // 2


def _rms(x, g):
    xf = x.astype(jnp.float32)
    y = xf * lax.rsqrt(jnp.mean(xf * xf, axis=-1, keepdims=True) + EPS)
    return (y * g.astype(jnp.float32)).astype(x.dtype)

def _heads(x, h):
    b, s, _ = x.shape
    return x.reshape(b, s, h, -1).transpose(0, 2, 1, 3)

def _merge(x):
    b, h, s, d = x.shape
    return x.transpose(0, 2, 1, 3).reshape(b, s, h * d)

def _rope(x, pos):
    half = x.shape[-1] // 2
    inv = ROPE_BASE ** (-jnp.arange(half, dtype=jnp.float32) / half)
    ang = pos.astype(jnp.float32)[:, None] * inv[None, :]
    cos, sin = jnp.cos(ang), jnp.sin(ang)
    xf = x.astype(jnp.float32)
    x1, x2 = xf[..., :half], xf[..., half:]
    return jnp.concatenate([x1 * cos - x2 * sin, x2 * cos + x1 * sin], axis=-1).astype(x.dtype)

def _chunk_mask(t, s):
    return (s // CHUNK)[None, :] <= (t // CHUNK)[:, None]

def _sweep(block_fn, qs):
    b, _, s, _ = qs[0].shape
    nb = s // QBLOCK
    qs_b = tuple(jnp.moveaxis(q.reshape(b, q.shape[1], nb, QBLOCK, q.shape[-1]), 2, 0) for q in qs)
    out = lax.map(lambda a: block_fn(a[0], *a[1]), (jnp.arange(nb), qs_b))
    out = jnp.moveaxis(out, 0, 2)
    return out.reshape(b, out.shape[1], s, out.shape[-1])

def _even_mixer(h, w_in, lq1, lk1, lq2, lk2, g_sub, g_cq, w_uq, g_ckv, w_ukv, w_out, lambda_init):
    b, s, _ = h.shape
    pos = jnp.arange(s)
    proj = h @ w_in
    cuts = np.cumsum(EVEN_SPLITS)[:-1].tolist()
    aq, ak, av, cq, ckv, kr = jnp.split(proj, cuts, axis=-1)

    aq = aq.reshape(b, s, DIFF_HEADS, 2, DIFF_DK)
    ak = ak.reshape(b, s, DIFF_HEADS, 2, DIFF_DK)
    q1 = aq[:, :, :, 0].transpose(0, 2, 1, 3)
    q2 = aq[:, :, :, 1].transpose(0, 2, 1, 3)
    k1 = ak[:, :, :, 0].transpose(0, 2, 1, 3)
    k2 = ak[:, :, :, 1].transpose(0, 2, 1, 3)
    va = _heads(av, DIFF_HEADS)
    lam = (jnp.exp(jnp.sum(lq1.astype(jnp.float32) * lk1.astype(jnp.float32)))
           - jnp.exp(jnp.sum(lq2.astype(jnp.float32) * lk2.astype(jnp.float32))) + lambda_init)
    slopes = 2.0 ** (-8.0 * jnp.arange(1, DIFF_HEADS + 1, dtype=jnp.float32) / DIFF_HEADS)

    def diff_block(i, q1b, q2b):
        t = i * QBLOCK + jnp.arange(QBLOCK)
        mask = _chunk_mask(t, pos)
        dist = jnp.abs(t[:, None] - pos[None, :]).astype(jnp.float32)
        bias = -slopes[:, None, None] * dist[None]

        def probs(qb, kk):
            sc = jnp.einsum('bhqd,bhkd->bhqk', qb, kk).astype(jnp.float32) * DIFF_SCALE + bias
            return jax.nn.softmax(jnp.where(mask, sc, -jnp.inf), axis=-1)

        p = probs(q1b, k1) - lam * probs(q2b, k2)
        return jnp.einsum('bhqk,bhkd->bhqd', p.astype(va.dtype), va)

    o_a = _sweep(diff_block, (q1, q2))
    o_a = _rms(o_a, g_sub) * (1.0 - lambda_init)

    q = _heads(_rms(cq, g_cq) @ w_uq, MLA_HEADS)
    q_nope, q_rope = q[..., :MLA_NOPE], _rope(q[..., MLA_NOPE:], pos)
    kv = _heads(_rms(ckv, g_ckv) @ w_ukv, MLA_HEADS)
    k_nope, vb = kv[..., :MLA_NOPE], kv[..., MLA_NOPE:]
    k_rope = _rope(kr, pos)

    def mla_block(i, qnb, qrb):
        t = i * QBLOCK + jnp.arange(QBLOCK)
        mask = _chunk_mask(t, pos)
        sc = (jnp.einsum('bhqd,bhkd->bhqk', qnb, k_nope)
              + jnp.einsum('bhqr,bkr->bhqk', qrb, k_rope)).astype(jnp.float32) * MLA_SCALE
        p = jax.nn.softmax(jnp.where(mask, sc, -jnp.inf), axis=-1)
        return jnp.einsum('bhqk,bhkd->bhqd', p.astype(vb.dtype), vb)

    o_b = _sweep(mla_block, (q_nope, q_rope))

    return jnp.concatenate([_merge(o_a), _merge(o_b)], axis=-1) @ w_out

def _odd_mixer(h, w_in, w_out):
    s = h.shape[1]
    pos = jnp.arange(s)
    q, k, v = jnp.split(h @ w_in, 3, axis=-1)
    q, k, v = _heads(q, SB_HEADS), _heads(k, SB_HEADS), _heads(v, SB_HEADS)

    def sb_block(i, qb):
        t = i * QBLOCK + jnp.arange(QBLOCK)
        strict = pos[None, :] < t[:, None]
        z = jnp.einsum('bhqd,bhkd->bhqk', qb, k).astype(jnp.float32) * SB_SCALE
        log_beta = jax.nn.log_sigmoid(z)
        log_keep = jnp.where(strict, jax.nn.log_sigmoid(-z), 0.0)
        between = lax.cumsum(log_keep, axis=3, reverse=True) - log_keep
        a = jnp.where(strict, jnp.exp(log_beta + between), 0.0)
        return jnp.einsum('bhqk,bhkd->bhqd', a.astype(v.dtype), v)

    o = _sweep(sb_block, (q,))
    return _merge(o) @ w_out

def _cross(h, mem_n, wq, wkv, wo):
    q = _heads(h @ wq, XA_HEADS)
    k, v = jnp.split(mem_n @ wkv, 2, axis=-1)
    k, v = _heads(k, XA_HEADS), _heads(v, XA_HEADS)
    sc = jnp.einsum('bhqd,bhkd->bhqk', q, k).astype(jnp.float32) * (XA_DH ** -0.5)
    p = jax.nn.softmax(sc, axis=-1)
    return _merge(jnp.einsum('bhqk,bhkd->bhqd', p.astype(v.dtype), v)) @ wo

def _mlp(h, w1, w2):
    return jnp.square(jax.nn.relu(h @ w1)) @ w2

def second_inputs(seed: int = 0) -> dict:
    key = jax.random.key(seed)
    ks = iter(jax.random.split(key, 40))

    def nrm(shape, scale):
        return jax.random.normal(next(ks), shape, jnp.float32) * scale

    def gain(shape):
        return 1.0 + nrm(shape, 0.02)

    L, E, O, D = DEPTH_2, N_EVEN, N_ODD, D_MODEL
    return {
        'x': nrm((BATCH, SEQ, D), 1.0),
        'mem': nrm((BATCH, MEM_LEN, D), 1.0),
        'ev_norm': gain((E, D)),
        'ev_w_in': nrm((E, D, EVEN_IN), D ** -0.5),
        'diff_lq1': nrm((E, DIFF_DK), 0.1),
        'diff_lk1': nrm((E, DIFF_DK), 0.1),
        'diff_lq2': nrm((E, DIFF_DK), 0.1),
        'diff_lk2': nrm((E, DIFF_DK), 0.1),
        'diff_subln': gain((E, DIFF_DV)),
        'mla_g_cq': gain((E, MLA_Q_LORA)),
        'mla_w_uq': nrm((E, MLA_Q_LORA, MLA_HEADS * (MLA_NOPE + MLA_ROPE)), MLA_Q_LORA ** -0.5),
        'mla_g_ckv': gain((E, MLA_KV_LORA)),
        'mla_w_ukv': nrm((E, MLA_KV_LORA, MLA_HEADS * (MLA_NOPE + MLA_DV)), MLA_KV_LORA ** -0.5),
        'ev_w_out': nrm((E, EVEN_MIX, D), EVEN_MIX ** -0.5),
        'od_norm': gain((O, D)),
        'sb_w_in': nrm((O, D, 3 * SB_WIDTH), D ** -0.5),
        'sb_w_out': nrm((O, SB_WIDTH, D), SB_WIDTH ** -0.5),
        'xa_norm': gain((L, D)),
        'xa_mem_norm': gain((L, D)),
        'xa_wq': nrm((L, D, D), D ** -0.5),
        'xa_wkv': nrm((L, D, 2 * D), D ** -0.5),
        'xa_wo': nrm((L, D, D), D ** -0.5),
        'mlp_norm': gain((L, D)),
        'mlp_w1': nrm((L, D, D_FF_2), D ** -0.5),
        'mlp_w2': nrm((L, D_FF_2, D), D_FF_2 ** -0.5),
        'final_norm': gain((D,)),
    }

def second_block(x, mem, ev_norm, ev_w_in, diff_lq1, diff_lk1, diff_lq2, diff_lk2, diff_subln,
              mla_g_cq, mla_w_uq, mla_g_ckv, mla_w_ukv, ev_w_out, od_norm, sb_w_in, sb_w_out,
              xa_norm, xa_mem_norm, xa_wq, xa_wkv, xa_wo, mlp_norm, mlp_w1, mlp_w2, final_norm):
    h = x
    for i in range(DEPTH_2):
        j = i // 2
        if i % 2 == 0:
            lambda_init = 0.8 - 0.6 * math.exp(-0.3 * i)
            h = h + _even_mixer(_rms(h, ev_norm[j]), ev_w_in[j], diff_lq1[j], diff_lk1[j], diff_lq2[j],
                                diff_lk2[j], diff_subln[j], mla_g_cq[j], mla_w_uq[j], mla_g_ckv[j],
                                mla_w_ukv[j], ev_w_out[j], lambda_init)
        else:
            h = h + _odd_mixer(_rms(h, od_norm[j]), sb_w_in[j], sb_w_out[j])
        h = h + _cross(_rms(h, xa_norm[i]), _rms(mem, xa_mem_norm[i]), xa_wq[i], xa_wkv[i], xa_wo[i])
        h = h + _mlp(_rms(h, mlp_norm[i]), mlp_w1[i], mlp_w2[i])
    return _rms(h, final_norm)


def setup_inputs(seed=0):
    out = dict(first_inputs(seed))
    for name, value in second_inputs(seed + 1).items():
        if name != "x":
            out[name + "_2"] = value
    return out


def reference(
    x, ffn1_norm, ffn1_w_in, ffn1_w_out, mix_norm, w_mix_in, cmp_k_pos, cmp_k_w1, cmp_k_b1,
    cmp_k_w2, cmp_v_pos, cmp_v_w1, cmp_v_b1, cmp_v_w2, swa_sinks, w_mix_out, ffn2_norm,
    ffn2_w_in, ffn2_w_out, final_norm, mem_2, ev_norm_2, ev_w_in_2, diff_lq1_2, diff_lk1_2,
    diff_lq2_2, diff_lk2_2, diff_subln_2, mla_g_cq_2, mla_w_uq_2, mla_g_ckv_2, mla_w_ukv_2,
    ev_w_out_2, od_norm_2, sb_w_in_2, sb_w_out_2, xa_norm_2, xa_mem_norm_2, xa_wq_2, xa_wkv_2,
    xa_wo_2, mlp_norm_2, mlp_w1_2, mlp_w2_2, final_norm_2,
):
    x = first_block(
        x, ffn1_norm, ffn1_w_in, ffn1_w_out, mix_norm, w_mix_in, cmp_k_pos, cmp_k_w1, cmp_k_b1,
        cmp_k_w2, cmp_v_pos, cmp_v_w1, cmp_v_b1, cmp_v_w2, swa_sinks, w_mix_out, ffn2_norm,
        ffn2_w_in, ffn2_w_out, final_norm,
    )
    return second_block(
        x, mem_2, ev_norm_2, ev_w_in_2, diff_lq1_2, diff_lk1_2, diff_lq2_2, diff_lk2_2,
        diff_subln_2, mla_g_cq_2, mla_w_uq_2, mla_g_ckv_2, mla_w_ukv_2, ev_w_out_2, od_norm_2,
        sb_w_in_2, sb_w_out_2, xa_norm_2, xa_mem_norm_2, xa_wq_2, xa_wkv_2, xa_wo_2, mlp_norm_2,
        mlp_w1_2, mlp_w2_2, final_norm_2,
    )


_drawn_inputs = setup_inputs


def setup_inputs(seed=0):
    import zlib

    import numpy as np

    out = dict(_drawn_inputs(seed))
    spreads = {}
    factors = {'cmp_k_pos': 3.981,
     'cmp_k_b1': 8.0,
     'cmp_v_b1': 6.001,
     'swa_sinks': 2.835,
     'ev_norm_2': 3.238,
     'diff_lq1_2': 8.0,
     'diff_subln_2': 5.095,
     'mla_g_cq_2': 8.0,
     'mla_g_ckv_2': 8.0,
     'od_norm_2': 6.057,
     'xa_norm_2': 8.0,
     'xa_mem_norm_2': 8.0,
     'final_norm_2': 2.856}
    for name, (base, spread) in spreads.items():
        noise = np.random.default_rng([zlib.crc32(name.encode()), seed]).standard_normal(out[name].shape)
        drawn = base * np.exp(spread * noise) if base else spread * noise
        out[name] = jnp.asarray(drawn.astype(out[name].dtype))
    for name, factor in factors.items():
        out[name] = (out[name] * factor).astype(out[name].dtype)
    return out
```

```python
from contextlib import ExitStack

import numpy as np

import concourse.bass as bass
from concourse import mybir

F32 = mybir.dt.float32
F32R = mybir.dt.float32r
ACT = mybir.ActivationFunctionType
ALU = mybir.AluOpType
AX = mybir.AxisListType

P = 128
T = 256
TT = T // P
D = 1024
KT = D // P
CH = 2048
RING = 3
AHEAD = 2
DH = 64
EPS = 1e-6
NEG = -1e30
D_FF = 2816
FF_TILES = D_FF // P
D_MLP = 4096
MLP_STEPS = D_MLP // (2 * P)
CBLK = 15
CCOLS = 2 * CBLK
JJ = 16
KEYCOLS = P + T
SEG = [(0, P), (P, T)]
ATTN_SCALE = DH ** -0.5
MLA_SCALE = 192 ** -0.5
XA_SCALE = 256 ** -0.5
LAMBDA_INIT = 0.2
BIAS_SLOTS = 4
SB_GROUP = 4

FFN_CHUNKS = FF_TILES + FF_TILES // 2
MIX_F, MIX_V, MIX_C, MIX_O = 8, 2, 4, 4
EV_F, EV_V, EV_M, EV_O = 5, 4, 2, 4
XA_CHUNKS = 16
MLP_CHUNKS = 2 * MLP_STEPS
SB_CHUNKS = 16
N_GAINS = 13
N_CHUNKS = (2 * FFN_CHUNKS + MIX_F + MIX_V + MIX_C + MIX_O + EV_F + EV_V + EV_M + EV_O
            + 2 * XA_CHUNKS + 2 * MLP_CHUNKS + SB_CHUNKS)

KC, VC, KS, KW, KB, QA, QB = 0, 2, 4, 5, 6, 7, 11
VS_COL, VW_COL, VB_COL, GATE_COL, MIXV_W = 0, 128, 256, 384, 408
CQ_W = 384


class Tally:

    def __init__(self):
        self.n = {}

    def __call__(self, sem, k=1):
        self.n[sem.name] = self.n.get(sem.name, 0) + k
        return self.n[sem.name]

    def total(self, sem):
        return self.n.get(sem.name, 0)

    def one(self, sem):
        self(sem)
        return sem, 1


def program(nc, stream, x, mem, gains, cq_gain, sub_gain, lam_vecs, sinks, cmp_pos, cmp_b1, cmp_w2k,
            cmp_w2v, bias_tiles, sb_mask, cmp_bias, cmp_mask, rope, squares_in, out):
    with ExitStack() as ctx:
        def sb(name, shape, dt=F32):
            return ctx.enter_context(nc.sbuf_tensor(name, shape, dt))

        def psum(name, shape):
            return ctx.enter_context(nc.psum_tensor(name, shape, F32))

        def sem(name):
            return ctx.enter_context(nc.semaphore(name))

        raw = sb("raw", [P, RING, CH])
        w_hi = sb("w_hi", [P, RING, CH], F32R)
        w_lo = sb("w_lo", [P, RING, CH], F32R)
        h = sb("h", [P, TT, D])
        xn = sb("xn", [P, TT, D])
        gain = sb("gain", [P, 2, D])
        xT_hi = sb("xT_hi", [P, KT, T], F32R)
        xT_lo = sb("xT_lo", [P, KT, T], F32R)
        g_hi = sb("g_hi", [P, 6, T], F32R)
        g_lo = sb("g_lo", [P, 6, T], F32R)
        proj = sb("proj", [P, 16, T])
        vtok = sb("vtok", [P, TT, D])
        memkT = sb("memkT", [P, KT, T])
        memv = sb("memv", [P, TT, D])
        obuf = sb("obuf", [P, TT, D])
        work = sb("work", [P, 6144])
        bias = sb("bias", [P, BIAS_SLOTS, KEYCOLS])
        ident = sb("ident", [P, P])
        zeros = sb("zeros", [P, T])
        sbm = sb("sbm", [P, 2 * T])
        sinkt = sb("sinkt", [P, 8])
        nsink = sb("nsink", [P, 8])
        tri = sb("tri", [P, P])
        ones = sb("ones", [P, P])
        gate = sb("gate", [P, TT, 24])
        lam = sb("lam", [P, 4])
        sq = sb("sq", [P, 8])
        ms = sb("ms", [P, 8])
        rstd = sb("rstd", [P, 8])
        nhalf = sb("nhalf", [P, 8])
        nmax = sb("nmax", [P, 4, 4])
        rsum = sb("rsum", [P, 4, 4])
        rinv = sb("rinv", [P, 4, 4])
        esink = sb("esink", [P, 4, 2])
        cst = sb("cst", [P, 3, 16])

        def cut(buf, a, *dims):
            n = int(np.prod(dims))
            v = buf.rearrange("p a b -> p (a b)")[:, a:a + n]
            names = "abcd"[:len(dims)]
            if len(dims) == 1:
                return v
            return v.rearrange("p (" + " ".join(names) + ") -> p " + " ".join(names), **dict(zip(names, dims)))

        cbias = cut(memkT, 0, 16, CBLK)
        cmask = cut(memkT, 256, 16, CBLK)
        posT = cut(memkT, 512, 2, JJ)
        b1T = cut(memkT, 544, 2, 2)
        w2k = cut(memkT, 576, 2, P)
        w2v = cut(memkT, 832, 2, DH)
        kcT = cut(memkT, 960, CCOLS)
        vcd = cut(memkT, 1024, 2, 4, DH)
        ropet = cut(memv, 0, 2, T)
        cqg = cut(memv, 512, CQ_W)
        subg = cut(memv, 896, P)
        lamv = cut(memv, 1024, 4, DH)
        blk_hi = g_hi.rearrange("p a b -> p (a b)")
        blk_lo = g_lo.rearrange("p a b -> p (a b)")

        acc = psum("acc", [P, 4, 512])
        mid = psum("mid", [P, 2, 512])
        aux = psum("aux", [P, 2, 512])

        raw_full = [sem(f"raw_full{i}") for i in range(RING)]
        gain_full = [sem(f"gain_full{i}") for i in range(2)]
        bias_full = [sem(f"bias_full{i}") for i in range(BIAS_SLOTS)]
        x_full = sem("x_full")
        ident_full = sem("ident_full")
        mem_full = sem("mem_full")
        const_full = sem("const_full")
        out_full = sem("out_full")
        hi_ready = sem("hi_ready")
        lo_ready = sem("lo_ready")
        chunk_used = sem("chunk_used")
        sq_ready = sem("sq_ready")
        dsq_ready = sem("dsq_ready")
        rstd_ready = sem("rstd_ready")
        xn_ready = sem("xn_ready")
        h_ready = sem("h_ready")
        mid_full = sem("mid_full")
        mid_done = sem("mid_done")
        thi_ready = sem("thi_ready")
        acc_full = sem("acc_full")
        acc_done = sem("acc_done")
        act_ready = sem("act_ready")
        g_ready = sem("g_ready")
        ghi_ready = sem("ghi_ready")
        glo_ready = sem("glo_ready")
        exp_ready = sem("exp_ready")
        pc_ready = sem("pc_ready")
        turned_full = sem("turned_full")
        turned_done = sem("turned_done")
        o_full = sem("o_full")
        o_done = sem("o_done")
        lam_dots = sem("lam_dots")
        lam_exps = sem("lam_exps")
        blk_ready = sem("blk_ready")
        blkhi_ready = sem("blkhi_ready")
        blklo_ready = sem("blklo_ready")
        gelu_ready = sem("gelu_ready")
        hidd_ready = sem("hidd_ready")
        gexp_ready = sem("gexp_ready")
        cs_ready = sem("cs_ready")
        ce_ready = sem("ce_ready")
        cp_ready = sem("cp_ready")
        cpt_full = sem("cpt_full")
        cpt_done = sem("cpt_done")
        co_full = sem("co_full")
        co_done = sem("co_done")
        rope_ready = sem("rope_ready")
        dnorm_ready = sem("dnorm_ready")
        z_full = sem("z_full")
        m_ready = sem("m_ready")
        act_own = sem("act_own")
        ln_ready = sem("ln_ready")
        sp_ready = sem("sp_ready")
        s_full = sem("s_full")
        zs_ready = sem("zs_ready")
        a_ready = sem("a_ready")
        so_full = sem("so_full")
        so_done = sem("so_done")
        dve_own = sem("dve_own")
        pool_own = sem("pool_own")

        n_const = 19
        bias_used_at = []
        obuf_turned_at = []
        last_h = []
        block = ctx.enter_context(nc.Block())

        N_ = work[:, 0:1024].rearrange("p (r c) -> p r c", r=2)
        P_ = work[:, 1024:3072].rearrange("p (r c) -> p r c", r=4)
        PT_ = work[:, 3072:4096].rearrange("p (r c) -> p r c", r=2)
        PC_ = work[:, 4096:5120].rearrange("p (r c) -> p r c", r=2)
        junk = work[:, 5120:6144]
        ff_s = work[:, 0:1536].rearrange("p (r c) -> p r c", r=3)
        ff_g = work[:, 1536:3072].rearrange("p (r c) -> p r c", r=3)
        cqs = work[:, 0:2 * CQ_W].rearrange("p (t c) -> p t c", t=2)
        SBW = SB_GROUP * KEYCOLS
        SB0 = SB_GROUP * T
        sb_m = work[:, 0:2 * SBW].rearrange("p (r c) -> p r c", r=2)
        sb_l = work[:, 2 * SBW:3 * SBW]
        sb_a = work[:, 3 * SBW:4 * SBW]
        blk = work[:, 0:JJ * CCOLS]
        pre = work[:, 1024:1280]
        hid = work[:, 1280:1280 + 4 * CCOLS].rearrange("p (v m c) -> p v m c", v=2, m=2)
        hidg = work[:, 1408:1408 + 4 * CCOLS].rearrange("p (v m c) -> p v m c", v=2, m=2)
        hidd_flat = work[:, 1536:2048]
        hidd = hidd_flat.rearrange("p (m g r c) -> p m g r c", m=2, g=2, r=4)
        cs = work[:, 2048:2288].rearrange("p (a c) -> p a c", a=16)
        ce = work[:, 2304:2544].rearrange("p (a c) -> p a c", a=16)
        cp_flat = work[:, 2560:3072]
        cp = cp_flat.rearrange("p (a c) -> p a c", a=16)
        cpT = work[:, 3072:3584].rearrange("p (a q) -> p a q", a=4)

        def grp(g):
            return slice(DH * g, DH * (g + 1))

        sb_order = (0, 2, 1, 3)

        @block.tensor
        def _(pe):
            sent, due = Tally(), Tally()
            at = [0]
            jobs = [0]
            hidden = [0]
            scored = [0]

            def mid_bank():
                n = jobs[0]
                jobs[0] += 1
                if n >= 2:
                    pe.wait_ge(mid_done, n - 1)
                return mid[:, n % 2, :]

            def three(out_ap, lhs, rhs, start, stop):
                pe.matmul(out_ap, lhs[0], rhs[0], start=start, stop=False)
                pe.matmul(out_ap, lhs[0], rhs[1], start=False, stop=False)
                return pe.matmul(out_ap, lhs[1], rhs[0], start=False, stop=stop)

            def w_pair(slot, a, n):
                return w_hi[:, slot, a:a + n], w_lo[:, slot, a:a + n]

            def xT_pair(k, t):
                return xT_hi[:, k, t * P:(t + 1) * P], xT_lo[:, k, t * P:(t + 1) * P]

            def f_tile(out_ap, slot, kts, width, col):
                for k in range(kts):
                    mm = three(out_ap, w_pair(slot, k * width + col, P), (xT_hi[:, k, :], xT_lo[:, k, :]),
                               k == 0, k == kts - 1)
                return mm

            def f_chunks(n):
                for _ in range(n):
                    c = at[0]
                    bank = mid_bank()
                    pe.wait_ge(lo_ready, c + 1)
                    for m in range(2):
                        mm = f_tile(bank[:, m * T:(m + 1) * T], c % RING, KT, 2 * P, m * P)
                    mm.then_inc(chunk_used, 1)
                    at[0] += 1

            def t_chunk(slot, lhs, kts, width, halves, start, stop):
                for t in range(TT):
                    for k in range(kts):
                        for half in range(halves):
                            w = min(width, 512)
                            mm = three(acc[:, t * halves + half, 0:w], lhs(k, t),
                                       w_pair(slot, k * width + half * 512, w),
                                       start and k == 0, stop and k == kts - 1)
                    if stop and t == 0:
                        mm.then_inc(acc_full, 1)
                mm.then_inc(chunk_used, 1)

            def acc_free():
                if due.total(acc_done):
                    pe.wait_ge(acc_done, due.total(acc_done))
                due(acc_done, TT)

            def t_chunks(width):
                kts, halves = (2, 2) if width == D else (4, 1)
                n = KT // kts
                acc_free()
                for i in range(n):
                    c = at[0]
                    pe.wait_ge(lo_ready, c + 1)
                    t_chunk(c % RING, lambda k, t: xT_pair(i * kts + k, t), kts, width, halves,
                            i == 0, i == n - 1)
                    at[0] += 1

            def turn(src, ready, tiles=KT, per_bank=4):
                for t in range(TT):
                    ready(t)
                    for a in range(0, tiles, per_bank):
                        bank = mid_bank()
                        for k in range(a, min(a + per_bank, tiles)):
                            mm = pe.transpose(bank[:, (k - a) * P:(k - a + 1) * P],
                                              src[:, t, k * P:(k + 1) * P], ident[:])
                        mm.then_inc(*sent.one(mid_full))
                pe.wait_ge(mid_done, jobs[0])

            def normed(t):
                pe.wait_ge(xn_ready, due(xn_ready))

            def heads_out(t):
                pe.wait_ge(o_done, sent.total(o_full))

            def g_pair(j):
                return lambda k, t: (g_hi[:, j * 2 + k, t * P:(t + 1) * P], g_lo[:, j * 2 + k, t * P:(t + 1) * P])

            def ffn():
                base, g0 = at[0], hidden[0]
                pairs = FF_TILES // 2

                def step_in(c, j, slot, r, wait=True):
                    pe.wait_ge(lo_ready, c + 1)
                    if wait:
                        pe.wait_ge(g_ready, j - 1)
                    for m in range(2):
                        mm = f_tile(mid[:, r, m * T:(m + 1) * T], slot, KT, 2 * P, m * P)
                    mm.then_inc(chunk_used, 1)

                def step_out(c, j, slot, pair, start, stop):
                    pe.wait_ge(lo_ready, c + 1)
                    pe.wait_ge(glo_ready, j)
                    t_chunk(slot, g_pair(pair), 2, D, 2, start, stop)

                acc_free()
                for j in range(4):
                    step_in(base + j, g0 + j, (base + j) % RING, j % 2, j >= 2)
                step_out(base + 4, g0 + 2, (base + 4) % RING, 0, True, False)
                first, loops = base + 5, (pairs - 3) // 2
                with pe.Fori(0, loops) as i:
                    for b in range(2):
                        s = first + 3 * b
                        c, j = i * 6 + s, i * 4 + (g0 + 4 + 2 * b)
                        step_in(c, j, s % RING, 0)
                        step_in(c + 1, j + 1, (s + 1) % RING, 1)
                        step_out(c + 2, j, (s + 2) % RING, (1 + b) % 2, False, False)
                c, j = first + 6 * loops, g0 + 4 + 4 * loops
                step_in(c, j, c % RING, 0)
                step_in(c + 1, j + 1, (c + 1) % RING, 1)
                step_out(c + 2, j, (c + 2) % RING, (pairs - 2) % 2, False, False)
                step_out(c + 3, j + 2, (c + 3) % RING, (pairs - 1) % 2, False, True)
                at[0] = c + 4
                hidden[0] += FF_TILES

            def mlp():
                base, s0 = at[0], hidden[0]
                banks = [mid[:, 0, :], mid[:, 1, :], aux[:, 0, :]]

                def step_in(c, j, slot, r, wait=True):
                    pe.wait_ge(lo_ready, c + 1)
                    if wait:
                        pe.wait_ge(act_ready, j - 2)
                    for m in range(2):
                        mm = f_tile(banks[r][:, m * T:(m + 1) * T], slot, KT, 2 * P, m * P)
                    mm.then_inc(chunk_used, 1)

                def step_out(c, j, slot, r, start, stop):
                    pe.wait_ge(lo_ready, c + 1)
                    pe.wait_ge(glo_ready, j + 1)
                    t_chunk(slot, g_pair(r), 2, D, 2, start, stop)

                acc_free()
                step_in(base, s0, base % RING, 0, False)
                for j in range(1, 4):
                    c = base + 2 * j - 1
                    step_in(c, s0 + j, c % RING, j % 3, j >= 3)
                    step_out(c + 1, s0 + j - 1, (c + 1) % RING, (j - 1) % 3, j == 1, False)
                loops = (MLP_STEPS - 4) // 3
                with pe.Fori(0, loops) as i:
                    for b in range(3):
                        s = base + 7 + 2 * b
                        c = i * 6 + s
                        step_in(c, i * 3 + (s0 + 4 + b), s % RING, (4 + b) % 3)
                        step_out(c + 1, i * 3 + (s0 + 3 + b), (s + 1) % RING, (3 + b) % 3, False, False)
                c = base + MLP_CHUNKS - 1
                step_out(c, s0 + MLP_STEPS - 1, c % RING, (MLP_STEPS - 1) % 3, False, True)
                at[0] = c + 1
                hidden[0] += MLP_STEPS

            def attention(n_units, dv, scores, values, full=False, maps=1):
                def score(u):
                    for m in range(maps):
                        scores(u, m, mid_bank()).then_inc(*sent.one(mid_full))

                def turn_probs(u):
                    if maps == 1:
                        pe.wait_ge(exp_ready, scored[0] + 1)
                        src = P_[:, scored[0] % 4, :]
                    else:
                        pe.wait_ge(pc_ready, due(pc_ready))
                        src = PC_[:, u % 2, :]
                    scored[0] += maps
                    n = sent.total(turned_full)
                    if n >= 2:
                        pe.wait_ge(turned_done, n - 1)
                    for b in range(4 if full else 3):
                        mm = pe.transpose(aux[:, n % 2, b * P:(b + 1) * P], src[:, b * P:(b + 1) * P], ident[:])
                    mm.then_inc(*sent.one(turned_full))

                def weigh(u):
                    n = sent.total(o_full)
                    pe.wait_ge(turned_done, n + 1)
                    if n >= 2:
                        pe.wait_ge(o_done, n - 1)
                    bank = acc[:, 2 + n % 2, :]
                    parts = (((0, 0), (1, 1)), ((2, 0), (3, 1))) if full else (((0, 0),), ((1, 0), (2, 1)))
                    for qt in range(TT):
                        for i, (b, kt) in enumerate(parts[qt]):
                            mm = pe.matmul(bank[:, qt * dv:(qt + 1) * dv], PT_[:, n % 2, b * P:(b + 1) * P],
                                           values(u, kt), start=i == 0, stop=i == len(parts[qt]) - 1)
                    mm.then_inc(*sent.one(o_full))

                score(0)
                for u in range(n_units):
                    if u + 1 < n_units:
                        score(u + 1)
                    turn_probs(u)
                    if u >= 1:
                        weigh(u - 1)
                weigh(n_units - 1)

            def head_scores(bank, q, k):
                for qt in range(TT):
                    a, n = SEG[qt]
                    mm = pe.matmul(bank[:, a:a + n], q[:, qt * P:(qt + 1) * P], k[:, 0:n], start=True, stop=True)
                return mm

            def compress():
                for v in range(2):
                    pe.wait_ge(blklo_ready, v + 1)
                    bank = mid_bank()
                    for half in range(2):
                        c = at[0]
                        pe.wait_ge(lo_ready, c + 1)
                        for j in range(8):
                            jj = half * 8 + j
                            lhs = [b[:, jj * CCOLS:jj * CCOLS + P] for b in (blk_hi, blk_lo)]
                            mm = three(bank[:, 0:T], lhs, w_pair(c % RING, j * T, T), jj == 0, jj == JJ - 1)
                        mm.then_inc(chunk_used, 1)
                        at[0] += 1
                    pe.wait_ge(mid_done, jobs[0])
                    bank = mid_bank()
                    for m in range(2):
                        mm = pe.transpose(bank[:, m * CCOLS:(m + 1) * CCOLS], pre[0:CCOLS, m * P:(m + 1) * P],
                                          ident[0:CCOLS, 0:CCOLS])
                    mm.then_inc(*sent.one(mid_full))
                pe.wait_ge(gelu_ready, 1)
                bank = mid_bank()
                for m in range(2):
                    mm = pe.matmul(bank[:, 0:CCOLS], w2k[:, m, :], hidg[:, 0, m, :], start=m == 0, stop=m == 1)
                mm.then_inc(*sent.one(mid_full))
                pe.wait_ge(hidd_ready, 1)
                bank = mid_bank()
                for g in range(2):
                    for m in range(2):
                        mm = pe.matmul(bank[:, g * DH:(g + 1) * DH], hidd_flat[:, (2 * m + g) * P:(2 * m + g + 1) * P],
                                       w2v[:, m, :], start=m == 0, stop=m == 1)
                mm.then_inc(*sent.one(mid_full))

            def compressed_attention():
                pe.wait_ge(mid_done, jobs[0])
                for g in range(2):
                    bank = mid_bank()
                    for qt in range(TT):
                        for r in range(4):
                            a = (qt * 4 + r) * 16
                            mm = pe.matmul(bank[:, a:a + CBLK], proj[grp(g), QA + r, qt * P:(qt + 1) * P],
                                           kcT[grp(g), g * CBLK:(g + 1) * CBLK], start=True, stop=True)
                    mm.then_inc(*sent.one(mid_full))
                pe.wait_ge(cp_ready, 1)
                for a in range(4):
                    mm = pe.transpose(aux[:, 0, a * P:(a + 1) * P], cp_flat[:, a * P:(a + 1) * P], ident[:])
                mm.then_inc(cpt_full, 1)
                pe.wait_ge(cpt_done, 1)
                for qt in range(TT):
                    for g in range(2):
                        mm = pe.matmul(acc[:, 2 + qt, g * T:(g + 1) * T], cpT[:, g * 2 + qt, :],
                                       vcd[:, g, :, :], start=True, stop=True)
                    mm.then_inc(co_full, 1)
                pe.wait_ge(co_done, TT)

            def stick_breaking():
                def z_scores(g):
                    if g >= 1:
                        pe.wait_ge(m_ready, g)
                    for i, r in enumerate(sb_order):
                        hd = g * SB_GROUP + r
                        q, k = proj[grp(hd % 2), hd // 2, :], proj[grp(hd % 2), 8 + hd // 2, :]
                        pe.matmul(acc[:, i // 2, (i % 2) * T:(i % 2 + 1) * T], k[:, 0:P], q, start=True, stop=True)
                        mm = pe.matmul(acc[:, 2 + i // 2, (i % 2) * P:(i % 2 + 1) * P], k[:, P:T], q[:, P:T],
                                       start=True, stop=True)
                    mm.then_inc(z_full, 1)

                z_scores(0)
                for g in range(4):
                    pe.wait_ge(sp_ready, g + 1)
                    for i in range(SB_GROUP):
                        s = mid[:, i // 2, (i % 2) * T:(i % 2 + 1) * T]
                        sp0, sp1 = sb_l[:, i * T:(i + 1) * T], sb_l[:, SB0 + i * P:SB0 + (i + 1) * P]
                        pe.matmul(s[:, 0:P], tri[:], sp0[:, 0:P], start=True, stop=True)
                        pe.matmul(s[:, P:T], tri[:], sp0[:, P:T], start=True, stop=False)
                        pe.matmul(s[:, P:T], ones[:], sp1, start=False, stop=True)
                        mm = pe.matmul(aux[:, 0, i * P:(i + 1) * P], tri[:], sp1, start=True, stop=True)
                    mm.then_inc(s_full, 1)
                    if g + 1 < 4:
                        z_scores(g + 1)
                    pe.wait_ge(a_ready, g + 1)
                    if g >= 1:
                        pe.wait_ge(so_done, g)
                    for i, r in enumerate(sb_order):
                        hd = g * SB_GROUP + r
                        for qt in range(TT):
                            o = aux[:, 1, qt * T + r * DH:qt * T + (r + 1) * DH]
                            mm = pe.matmul(o, sb_a[:, i * T + qt * P:i * T + (qt + 1) * P],
                                           vtok[:, 0, hd * DH:(hd + 1) * DH], start=True, stop=qt == 0)
                            if qt:
                                mm = pe.matmul(o, sb_a[:, SB0 + i * P:SB0 + (i + 1) * P],
                                               vtok[:, 1, hd * DH:(hd + 1) * DH], start=False, stop=True)
                    mm.then_inc(so_full, 1)

            def projected():
                pe.wait_ge(mid_done, jobs[0])
                pe.wait_ge(acc_done, due.total(acc_done))

            def cross():
                turn(xn, normed)
                f_chunks(4)
                t_chunks(D)
                turn(xn, normed)
                f_chunks(4)
                projected()

                def scores(u, m, bank):
                    for qt in range(TT):
                        for i in range(2):
                            mm = pe.matmul(bank[:, qt * T:(qt + 1) * T], proj[:, 2 * u + i, qt * P:(qt + 1) * P],
                                           memkT[:, 2 * u + i, :], start=i == 0, stop=i == 1)
                    return mm

                attention(4, T, scores, lambda u, kt: memv[:, kt, u * T:(u + 1) * T], full=True)
                turn(obuf, heads_out)
                t_chunks(D)

            def mixer():
                turn(xn, normed)
                f_chunks(MIX_F)
                t_chunks(MIXV_W)
                compress()
                compressed_attention()
                projected()
                attention(16, DH, lambda u, m, bank: head_scores(
                    bank, proj[grp(u // 8), QA + u // 2 % 4, :], proj[grp(u // 8), KS + u % 2, :]),
                    lambda u, kt: vtok[:, kt, VS_COL + P * (u % 2) + DH * (u // 8):][:, 0:DH])
                attention(8, DH, lambda u, m, bank: head_scores(
                    bank, proj[grp(u // 4), QB + u % 4, :], proj[grp(u // 4), KB, :]),
                    lambda u, kt: vtok[:, kt, VB_COL + DH * (u // 4):][:, 0:DH])
                turn(obuf, heads_out)
                t_chunks(D)

            def even_mixer():
                turn(xn, normed)
                f_chunks(EV_F)
                t_chunks(512)
                t_chunks(CQ_W)
                turn(xn, normed, CQ_W // P)
                projected()
                attention(4, P, lambda u, m, bank: head_scores(
                    bank, proj[grp(m), u, :], proj[grp(m), 4 + u, :]),
                    lambda u, kt: vtok[:, kt, u * P:(u + 1) * P], maps=2)
                c = at[0]
                pe.wait_ge(lo_ready, c + 1)
                for pair in range(4):
                    bank = mid_bank()
                    for m in range(2):
                        mm = f_tile(bank[:, m * T:(m + 1) * T], c % RING, 2, D, (2 * pair + m) * P)
                    mm.then_inc(*(sent.one(mid_full) if pair < 3 else (chunk_used, 1)))
                c += 1
                pe.wait_ge(lo_ready, c + 1)
                for pair in range(2):
                    bank = mid_bank()
                    for m in range(2):
                        mm = three(bank[:, m * T:(m + 1) * T], w_pair(c % RING, (2 * pair + m) * P, P),
                                   (xT_hi[:, 2, :], xT_lo[:, 2, :]), True, True)
                    mm.then_inc(*sent.one(mid_full))
                acc_free()
                for t in range(TT):
                    mm = three(acc[:, t, :], xT_pair(2, t), w_pair(c % RING, 512, 512), True, True)
                    mm.then_inc(*((acc_full, 1) if t == 0 else (chunk_used, 1)))
                at[0] = c + 1
                projected()
                pe.wait_ge(rope_ready, 1)

                def scores(u, m, bank):
                    rows = grp(u % 2)
                    for qt in range(TT):
                        a, n = SEG[qt]
                        pe.matmul(bank[:, a:a + n], proj[:, u, qt * P:(qt + 1) * P], proj[:, 10 + u, 0:n],
                                  start=True, stop=False)
                        mm = pe.matmul(bank[:, a:a + n], proj[rows, 14 + u // 2, qt * P:(qt + 1) * P],
                                       proj[rows, 8, 0:n], start=False, stop=True)
                    return mm

                attention(4, P, scores, lambda u, kt: vtok[:, kt, 512 + u * P:512 + (u + 1) * P])
                pe.wait_ge(dnorm_ready, 1)
                turn(obuf, heads_out)
                t_chunks(D)

            def odd_mixer():
                turn(xn, normed)
                f_chunks(8)
                t_chunks(D)
                projected()
                stick_breaking()
                turn(obuf, lambda t: pe.wait_ge(so_done, 4))
                t_chunks(D)

            pe.wait_ge(ident_full, 16)
            turn(xn, normed)
            ffn()
            pe.wait_ge(const_full, 16 * n_const)
            mixer()
            turn(xn, normed)
            ffn()
            even_mixer()
            cross()
            turn(xn, normed)
            mlp()
            odd_mixer()
            cross()
            turn(xn, normed)
            mlp()

        @block.vector
        def _(dve):
            sent, due = Tally(), Tally()
            at = [0]
            jobs = [0]
            hidden = [0]
            norms = [0]
            tiles = [0]
            scored = [0]

            def own(ins):
                ins.then_inc(*sent.one(dve_own))
                dve.wait_ge(dve_own, sent.total(dve_own))

            def split(c, slot):
                dve.wait_ge(hi_ready, c + 1)
                dve.tensor_tensor(w_lo[:, slot, :], raw[:, slot, :], w_hi[:, slot, :],
                                  ALU.subtract).then_inc(lo_ready, 1)

            def ahead(n=1):
                for _ in range(n):
                    c = at[0] + AHEAD
                    if c < N_CHUNKS:
                        split(c, c % RING)
                    at[0] += 1

            def job(signalled=True):
                m = jobs[0]
                jobs[0] += 1
                if signalled:
                    dve.wait_ge(mid_full, due(mid_full))
                else:
                    dve.wait_ge(chunk_used, at[0])
                return mid[:, m % 2, :]

            def gained():
                k = norms[0]
                norms[0] += 1
                dve.wait_ge(gain_full[k % 2], 16 * (k // 2 + 1))
                return gain[:, k % 2, :]

            def norm(src):
                g = gained()
                for t in range(TT):
                    dve.wait_ge(rstd_ready, due(rstd_ready))
                    dve.scalar_tensor_tensor(xn[:, t, :], src[:, t, :], rstd[:, t:t + 1], g,
                                             ALU.mult, ALU.mult).then_inc(*sent.one(xn_ready))

            def final_norm():
                g = gained()
                for t in range(TT):
                    dve.wait_ge(rstd_ready, due(rstd_ready))
                    dve.scalar_tensor_tensor(h[:, t, :], h[:, t, :], rstd[:, t:t + 1], g,
                                             ALU.mult, ALU.mult).then_inc(*sent.one(h_ready))
                last_h[:] = [h_ready, sent.total(h_ready)]

            def turned(tiles_=KT, per_bank=4):
                for t in range(TT):
                    for a in range(0, tiles_, per_bank):
                        n = min(per_bank, tiles_ - a)
                        bank = job()
                        dve.wait_ge(thi_ready, due(thi_ready))
                        dve.tensor_tensor(xT_lo[:, a:a + n, t * P:(t + 1) * P],
                                          bank[:, 0:n * P].rearrange("p (k q) -> p k q", q=P),
                                          xT_hi[:, a:a + n, t * P:(t + 1) * P],
                                          ALU.subtract).then_inc(mid_done, 1)

            def f_chunks(n, dst):
                for i in range(n):
                    ahead()
                    bank = job(False)
                    dve.tensor_copy(dst[:, 2 * i:2 * i + 2, :],
                                    bank.rearrange("p (k q) -> p k q", q=T)).then_inc(mid_done, 1)

            def acc_tile(t):
                if t == 0:
                    dve.wait_ge(acc_full, due(acc_full))
                else:
                    dve.wait_ge(chunk_used, at[0])

            def t_values(dst, width, chunks):
                ahead(chunks)
                for t in range(TT):
                    acc_tile(t)
                    if width == D:
                        o, src = dst[:, t, :].rearrange("p (a b) -> p a b", a=2), acc[:, 2 * t:2 * t + 2, :]
                    else:
                        o, src = dst[:, t, 0:width], acc[:, t, 0:width]
                    dve.tensor_copy(o, src).then_inc(*sent.one(acc_done))

            def residual(scale, chunks):
                ahead(chunks)
                for t in range(TT):
                    acc_tile(t)
                    ht = h[:, t, :].rearrange("p (a b) -> p a b", a=2)
                    dve.scalar_tensor_tensor(ht, acc[:, 2 * t:2 * t + 2, :], scale, ht, ALU.mult,
                                             ALU.add).then_inc(*sent.one(acc_done))

            def ffn():
                base, g0 = at[0], hidden[0]

                def step_in(c, j, slot, r, g):
                    split(c + AHEAD, slot)
                    dve.wait_ge(act_ready, j + 1)
                    dve.tensor_tensor(ff_g[:, r, 0:T], ff_s[:, r, 0:T], mid[:, r, T:2 * T],
                                      ALU.mult).then_inc(g_ready, 1)
                    dve.wait_ge(ghi_ready, j + 1)
                    dve.tensor_tensor(g_lo[:, g, :], ff_g[:, r, 0:T], g_hi[:, g, :],
                                      ALU.subtract).then_inc(glo_ready, 1)

                for j in range(4):
                    step_in(base + j, g0 + j, (base + j + AHEAD) % RING, j % 2, j % 4)
                split(base + 4 + AHEAD, (base + 4 + AHEAD) % RING)
                first, loops = base + 5, (FF_TILES // 2 - 3) // 2
                with dve.Fori(0, loops) as i:
                    for b in range(2):
                        s = first + 3 * b
                        for n in range(2):
                            step_in(i * 6 + (s + n), i * 4 + (g0 + 4 + 2 * b + n), (s + n + AHEAD) % RING, n,
                                    2 * b + n)
                        split(i * 6 + (s + 2 + AHEAD), (s + 2 + AHEAD) % RING)
                c, j = first + 6 * loops, 4 + 4 * loops
                for n in range(2):
                    step_in(c + n, g0 + j + n, (c + n + AHEAD) % RING, n, (j + n) % 4)
                hidden[0] += FF_TILES
                at[0] = c + 2
                residual(0.5, 2)

            def mlp():
                base, s0 = at[0], hidden[0]

                def step_in(c, j, slot, r):
                    if slot is not None:
                        split(c + AHEAD, slot)
                    dve.wait_ge(act_ready, j + 1)
                    dve.tensor_tensor(ff_g[:, r, :], ff_s[:, r, :], ff_s[:, r, :], ALU.mult).then_inc(g_ready, 1)
                    dve.wait_ge(ghi_ready, j + 1)
                    dve.wait_ge(g_ready, j + 1)
                    dve.tensor_tensor(g_lo[:, 2 * r:2 * r + 2, :], ff_g[:, r, :].rearrange(
                        "p (k q) -> p k q", k=2), g_hi[:, 2 * r:2 * r + 2, :], ALU.subtract).then_inc(glo_ready, 1)

                def steps(j):
                    c = base + 2 * j - 1
                    step_in(c, s0 + j, (c + AHEAD) % RING if c + AHEAD < N_CHUNKS else None, j % 3)
                    if c + 1 + AHEAD < N_CHUNKS:
                        split(c + 1 + AHEAD, (c + 1 + AHEAD) % RING)

                step_in(base, s0, (base + AHEAD) % RING, 0)
                for j in range(1, 4):
                    steps(j)
                loops = (MLP_STEPS - 4) // 3
                if base + MLP_CHUNKS == N_CHUNKS:
                    loops -= 1
                with dve.Fori(0, loops) as i:
                    for b in range(3):
                        s = base + 7 + 2 * b
                        step_in(i * 6 + s, i * 3 + (s0 + 4 + b), (s + AHEAD) % RING, (4 + b) % 3)
                        split(i * 6 + (s + 1 + AHEAD), (s + 1 + AHEAD) % RING)
                for j in range(4 + 3 * loops, MLP_STEPS):
                    steps(j)
                hidden[0] += MLP_STEPS
                at[0] = base + MLP_CHUNKS - 1
                residual(1.0, 1)

            def attention(n_units, scale, finish, combine=None, tile_of=None, full=False, maps=1, sink=False):
                segs = [(0, T), (T, T)] if full else SEG
                base, e0 = tiles[0], scored[0]
                seen = [-1]

                def unit(u):
                    k = None
                    if tile_of is not None:
                        k = base + tile_of(u)
                        if k != seen[0]:
                            dve.wait_ge(bias_full[k % BIAS_SLOTS], 16 * (k // BIAS_SLOTS + 1))
                            seen[0] = k
                    for _ in range(maps):
                        e = scored[0]
                        scored[0] += 1
                        bank = job()
                        if e >= 2:
                            dve.wait_ge(exp_ready, e - 1)
                        for qt in range(TT):
                            a, n = segs[qt]
                            b = zeros[:, 0:n] if k is None else bias[:, k % BIAS_SLOTS, a:a + n]
                            ins = dve.tensor_tensor_reduce(N_[:, e % 2, a:a + n], bank[:, a:a + n], b, -scale,
                                                           -NEG, ALU.add, ALU.min, nmax[:, e % 4, qt:qt + 1])
                        if sink:
                            own(ins)
                            ins = dve.tensor_scalar(nmax[:, e % 4, 0:2], nmax[:, e % 4, 0:2],
                                                    nsink[:, u:u + 1], None, ALU.min)
                        ins.then_inc(mid_done, 1)
                    if k is not None:
                        while len(bias_used_at) <= k:
                            bias_used_at.append(0)
                        bias_used_at[k] = jobs[0]

                def output(u):
                    s = (e0 + u * maps) % 4
                    if maps == 1:
                        dve.wait_ge(exp_ready, e0 + u + 1)
                        if sink:
                            own(dve.tensor_tensor(rsum[:, s, 0:2], rsum[:, s, 0:2], esink[:, s, :], ALU.add))
                        own(dve.reciprocal(rinv[:, s, 0:2], rsum[:, s, 0:2]))
                    n = sent.total(o_done)
                    dve.wait_ge(o_full, n + 1)
                    finish(u, acc[:, 2 + n % 2, :], rinv[:, s, :]).then_inc(*sent.one(o_done))

                unit(0)
                for u in range(n_units):
                    if u + 1 < n_units:
                        unit(u + 1)
                    if combine is not None:
                        combine(u, e0)
                    if u >= 1:
                        output(u - 1)
                output(n_units - 1)
                if tile_of is not None:
                    tiles[0] = base + tile_of(n_units - 1) + 1

            def plain_out(base, w):
                def finish(u, bank, inv):
                    for qt in range(TT):
                        ins = dve.tensor_scalar(obuf[:, qt, base + u * w:base + (u + 1) * w],
                                                bank[:, qt * w:(qt + 1) * w], inv[:, qt:qt + 1], None, ALU.mult)
                    return ins
                return finish

            def nsa_out(u, bank, inv):
                hd, branch = u // 2, u % 2
                own(dve.tensor_tensor(inv[:, 0:2], inv[:, 0:2], gate[:, :, hd * 3 + 1 + branch], ALU.mult))
                if branch:
                    dve.wait_ge(o_done, sent.total(o_done))
                for qt in range(TT):
                    o = obuf[:, qt, hd * DH:(hd + 1) * DH]
                    ins = dve.scalar_tensor_tensor(o, bank[:, qt * DH:(qt + 1) * DH], inv[:, qt:qt + 1], o,
                                                   ALU.mult, ALU.add)
                return ins

            def diff_combine(u, e0):
                e = e0 + 2 * u
                dve.wait_ge(exp_ready, e + 2)
                a, b = e % 4, (e + 1) % 4
                dve.reciprocal(rinv[:, a, 0:2], rsum[:, a, 0:2])
                own(dve.reciprocal(rinv[:, b, 0:2], rsum[:, b, 0:2]))
                own(dve.tensor_scalar(rinv[:, b, 0:2], rinv[:, b, 0:2], lam[:, 3:4], None, ALU.mult))
                for qt in range(TT):
                    c, n = SEG[qt]
                    ins = dve.tensor_scalar(P_[:, b, c:c + n], P_[:, b, c:c + n], rinv[:, b, qt:qt + 1], None,
                                            ALU.mult)
                own(ins)
                if u >= 2:
                    dve.wait_ge(turned_full, sent.total(o_done) + 1)
                for qt in range(TT):
                    c, n = SEG[qt]
                    ins = dve.scalar_tensor_tensor(PC_[:, u % 2, c:c + n], P_[:, a, c:c + n],
                                                   rinv[:, a, qt:qt + 1], P_[:, b, c:c + n], ALU.mult, ALU.add)
                ins.then_inc(pc_ready, 1)

            def diff_out(u, bank, inv):
                for qt in range(TT):
                    ins = dve.tensor_copy(obuf[:, qt, u * P:(u + 1) * P], bank[:, qt * P:(qt + 1) * P])
                return ins

            def compress():
                for v in range(2):
                    if v:
                        dve.wait_ge(blkhi_ready, v)
                    for g in range(2):
                        for par in range(2):
                            rows = grp(par)
                            src = proj[rows, KC + 2 * v + g, :].rearrange("p (c b) -> p b c", b=16)
                            bl = blk[rows, :].rearrange("p (j c) -> p j c", j=JJ)
                            for nx in range(2):
                                ins = dve.tensor_tensor(
                                    bl[:, nx * 8:nx * 8 + 8, g * CBLK:(g + 1) * CBLK],
                                    src[:, par:16:2, nx:nx + CBLK],
                                    posT[rows, v, nx * 8:nx * 8 + 8].unsqueeze(2).to_broadcast([DH, 8, CBLK]),
                                    ALU.add)
                    ins.then_inc(blk_ready, 1)
                    dve.wait_ge(blkhi_ready, v + 1)
                    dve.tensor_tensor(blk_lo[:, 0:JJ * CCOLS], blk[:], blk_hi[:, 0:JJ * CCOLS],
                                      ALU.subtract).then_inc(blklo_ready, 1)
                    ahead(2)
                    bank = job(False)
                    dve.tensor_copy(pre[0:CCOLS, :], bank[0:CCOLS, 0:T]).then_inc(mid_done, 1)
                    bank = job()
                    for k in range(2):
                        ins = dve.tensor_scalar(hid[:, v, k, :], bank[:, k * CCOLS:(k + 1) * CCOLS],
                                                b1T[:, v, k:k + 1], None, ALU.add)
                    ins.then_inc(mid_done, 1)
                dve.wait_ge(gelu_ready, 1)
                for k in range(2):
                    for g in range(2):
                        ins = dve.tensor_copy(hidd[:, k, g, :, 0:CBLK], hidg[:, 1, k, g * CBLK:(g + 1) * CBLK]
                                              .unsqueeze(1).to_broadcast([P, 4, CBLK]))
                ins.then_inc(hidd_ready, 1)
                bank = job()
                dve.tensor_copy(kcT[:], bank[:, 0:CCOLS]).then_inc(mid_done, 1)
                bank = job()
                for g in range(2):
                    for r in range(4):
                        rows = slice(32 * r, 32 * r + 32)
                        ins = dve.tensor_copy(vcd[rows, g, r, :], bank[rows, g * DH:(g + 1) * DH])
                ins.then_inc(mid_done, 1)

            def compressed_attention():
                dve.wait_ge(gexp_ready, 1)
                own(dve.tensor_scalar(gate[:], gate[:], 1.0, None, ALU.add))
                own(dve.reciprocal(gate[:], gate[:]))
                for g in range(2):
                    sc = job()[:, 0:128].rearrange("p (a c) -> p a c", a=8)[:, :, 0:CBLK]
                    dve.scalar_tensor_tensor(cs[:, 8 * g:8 * g + 8, :], sc, ATTN_SCALE,
                                             cbias[:, 8 * g:8 * g + 8, :], ALU.mult, ALU.add).then_inc(mid_done, 1)
                dve.wait_ge(mid_done, jobs[0])
                own(dve.tensor_reduce(cst[:, 0, :], cs[:], AX.X, ALU.max))
                dve.tensor_tensor(cs[:], cs[:], cst[:, 0, :].unsqueeze(2).to_broadcast([P, 16, CBLK]),
                                  ALU.subtract).then_inc(cs_ready, 1)
                dve.wait_ge(ce_ready, 1)
                own(dve.tensor_reduce(cst[:, 1, :], ce[:], AX.X, ALU.add))
                own(dve.reciprocal(cst[:, 2, :], cst[:, 1, :]))
                for g in range(2):
                    for qt in range(TT):
                        a = (g * 2 + qt) * 4
                        dve.tensor_tensor(cst[:, 2, a:a + 4], cst[:, 2, a:a + 4], gate[:, qt, 12 * g:12 * g + 12:3],
                                          ALU.mult)
                own(dve.tensor_tensor(ce[:], ce[:], cmask[:], ALU.mult))
                dve.tensor_tensor(cp[:, :, 0:CBLK], ce[:], cst[:, 2, :].unsqueeze(2).to_broadcast([P, 16, CBLK]),
                                  ALU.mult).then_inc(cp_ready, 1)
                for qt in range(TT):
                    dve.wait_ge(co_full, qt + 1)
                    dve.tensor_copy(obuf[:, qt, 0:512], acc[:, 2 + qt, :]).then_inc(*sent.one(co_done))
                dve.wait_ge(co_done, TT)

            def mixer():
                dve.wait_ge(const_full, 16 * n_const)
                dve.tensor_scalar(nsink[:], sinkt[:], -1.0, None, ALU.mult)
                dve.tensor_scalar(subg[:], subg[:], 1.0 - LAMBDA_INIT, None, ALU.mult)
                for i in range(2):
                    ins = dve.tensor_tensor_reduce(lamv[:, 2 * i, :], lamv[:, 2 * i, :], lamv[:, 2 * i + 1, :], 1.0,
                                                   0.0, ALU.mult, ALU.add, lam[:, i:i + 1])
                ins.then_inc(lam_dots, 1)
                norm(h)
                turned()
                f_chunks(MIX_F, proj)
                t_values(vtok, MIXV_W, MIX_V)
                dve.memset(blk_hi[:, JJ * CCOLS:JJ * CCOLS + P].bitcast(F32), 0.0)
                dve.memset(blk_lo[:, JJ * CCOLS:JJ * CCOLS + P].bitcast(F32), 0.0)
                dve.memset(vcd[:], 0.0)
                dve.memset(hidd_flat, 0.0)
                own(dve.memset(cp_flat, 0.0))
                dve.wait_ge(lam_exps, 1)
                own(dve.tensor_tensor(lam[:, 2:3], lam[:, 0:1], lam[:, 1:2], ALU.subtract))
                own(dve.tensor_scalar(lam[:, 3:4], lam[:, 2:3], LAMBDA_INIT, -1.0, ALU.add, ALU.mult))
                compress()
                compressed_attention()
                attention(16, ATTN_SCALE, nsa_out, tile_of=lambda u: u // 2)
                attention(8, ATTN_SCALE, plain_out(512, DH), tile_of=lambda u: u, sink=True)
                turned()
                residual(1.0, MIX_O)

            def even_mixer():
                norm(h)
                turned()
                f_chunks(EV_F, proj)
                t_values(vtok, 512, 2)
                t_values(cqs, CQ_W, 2)
                for t in range(TT):
                    dve.wait_ge(rstd_ready, due(rstd_ready))
                    for i, (a, n) in enumerate(((0, 2 * P), (2 * P, P))):
                        ins = dve.scalar_tensor_tensor(xn[:, t, a:a + n], cqs[:, t, a:a + n],
                                                       rstd[:, 2 * t + i:2 * t + i + 1], cqg[:, a:a + n],
                                                       ALU.mult, ALU.mult)
                    ins.then_inc(*sent.one(xn_ready))
                turned(CQ_W // P)
                attention(4, ATTN_SCALE, diff_out, combine=diff_combine, tile_of=lambda u: u, maps=2)
                dve.wait_ge(o_done, sent.total(o_done))
                for qt in range(TT):
                    for u in range(4):
                        k = qt * 4 + u
                        o = obuf[:, qt, u * P:(u + 1) * P]
                        ins = dve.tensor_tensor_reduce(junk[:, k * P:(k + 1) * P], o, o, 1.0, 0.0,
                                                       ALU.mult, ALU.add, sq[:, k:k + 1])
                ins.then_inc(dsq_ready, 1)
                for pair in range(4):
                    if pair == 3:
                        ahead()
                    bank = job(pair < 3)
                    dve.tensor_copy(proj[:, 2 * pair:2 * pair + 2, :],
                                    bank.rearrange("p (k q) -> p k q", q=T)).then_inc(mid_done, 1)
                for pair in range(2):
                    bank = job()
                    dve.tensor_copy(proj[:, 10 + 2 * pair:12 + 2 * pair, :],
                                    bank.rearrange("p (k q) -> p k q", q=T)).then_inc(mid_done, 1)
                t_values(vtok[:, :, 512:1024], 512, 1)
                dve.wait_ge(mid_done, jobs[0])
                for a in (4, 5, 8):
                    dve.tensor_tensor(proj[:, a, :], proj[:, a, :], ropet[:, 0, :], ALU.mult)
                for b in (6, 7, 9):
                    ins = dve.tensor_tensor(proj[:, b, :], proj[:, b, :], ropet[:, 1, :], ALU.mult)
                own(ins)
                dve.tensor_tensor(proj[:, 14, :], proj[:, 4, :], proj[:, 6, :], ALU.add)
                dve.tensor_tensor(proj[:, 15, :], proj[:, 5, :], proj[:, 7, :], ALU.add)
                dve.tensor_tensor(proj[:, 8, :], proj[:, 8, :], proj[:, 9, :], ALU.add).then_inc(rope_ready, 1)
                attention(4, MLA_SCALE, plain_out(512, P), tile_of=lambda u: 0)
                dve.wait_ge(rstd_ready, due(rstd_ready))
                for qt in range(TT):
                    for u in range(4):
                        o = obuf[:, qt, u * P:(u + 1) * P]
                        k = qt * 4 + u
                        ins = dve.scalar_tensor_tensor(o, o, rstd[:, k:k + 1], subg[:], ALU.mult, ALU.mult)
                ins.then_inc(dnorm_ready, 1)
                turned()
                obuf_turned_at.append(jobs[0])
                residual(1.0, EV_O)

            def cross():
                norm(obuf)
                turned()
                f_chunks(4, memkT)
                t_values(memv, D, 4)
                norm(h)
                turned()
                f_chunks(4, proj)
                attention(4, XA_SCALE, plain_out(0, T), full=True)
                turned()
                residual(1.0, 4)

            def odd_mixer():
                norm(h)
                turned()
                f_chunks(8, proj)
                t_values(vtok, D, 4)
                mask0 = sbm[:, 0:T].unsqueeze(1).to_broadcast([P, SB_GROUP, T])
                mask1 = sbm[:, T:2 * T].unsqueeze(1).to_broadcast([P, 2, T])
                for g in range(4):
                    m0 = sb_m[:, g % 2, 0:SB0]
                    m1 = sb_m[:, g % 2, SB0:SBW].rearrange("p (a b) -> p a b", a=2)
                    dve.wait_ge(z_full, g + 1)
                    dve.scalar_tensor_tensor(m0.rearrange("p (a b) -> p a b", b=T),
                                             acc[:, 0:2, :].rearrange("p a (c b) -> p (a c) b", b=T), ATTN_SCALE,
                                             mask0, ALU.mult, ALU.add)
                    dve.scalar_tensor_tensor(m1, acc[:, 2:4, 0:T], ATTN_SCALE, mask1, ALU.mult,
                                             ALU.add).then_inc(m_ready, 1)
                    dve.wait_ge(ln_ready, g + 1)
                    dve.scalar_tensor_tensor(sb_l[:], sb_m[:, g % 2, :], 0.0, sb_l[:], ALU.max,
                                             ALU.add).then_inc(sp_ready, 1)
                    dve.wait_ge(s_full, g + 1)
                    m0 = m0.rearrange("p (a b) -> p a b", a=2)
                    dve.tensor_tensor(m0, m0, mid[:, :, :], ALU.subtract)
                    m1 = sb_m[:, g % 2, SB0:SBW]
                    dve.tensor_tensor(m1, m1, aux[:, 0, :], ALU.subtract).then_inc(zs_ready, 1)
                    dve.wait_ge(so_full, g + 1)
                    dve.tensor_copy(obuf[:, :, g * T:(g + 1) * T],
                                    aux[:, 1, :].rearrange("p (t c) -> p t c", t=2)).then_inc(so_done, 1)
                turned()
                obuf_turned_at.append(jobs[0])
                residual(1.0, 4)

            
            for c in range(AHEAD):
                split(c, c % RING)
            norm(h)
            turned()
            ffn()
            mixer()
            norm(h)
            turned()
            ffn()
            final_norm()
            even_mixer()
            cross()
            norm(h)
            turned()
            mlp()
            odd_mixer()
            cross()
            norm(h)
            turned()
            mlp()
            final_norm()

        @block.scalar
        def _(act):
            sent, due = Tally(), Tally()
            at = [0]
            jobs = [0]
            hidden = [0]
            scored = [0]
            units = [0]

            def split(c, slot, chunk_waits):
                used, arrived = chunk_waits
                if used is not None:
                    act.wait_ge(chunk_used, used)
                act.wait_ge(raw_full[slot], arrived)
                act.activation(w_hi[:, slot, :], raw[:, slot, :], ACT.Copy).then_inc(hi_ready, 1)

            def split_at(c):
                if c < N_CHUNKS:
                    split(c, c % RING, (c - RING + 1 if c >= RING else None, 16 * (c // RING + 1)))

            def split_in_loop(c, i, per):
                split(c, c % RING, (i * per + (c - RING + 1), i * (16 * per // RING) + 16 * (c // RING + 1)))

            def ahead(n=1):
                for _ in range(n):
                    split_at(at[0] + AHEAD)
                    at[0] += 1

            def squares(src, ready):
                for t in range(TT):
                    ready(t)
                    if sent.total(sq_ready):
                        act.wait_ge(sq_ready, sent.total(sq_ready))
                    act.activation(junk, src[:, t, :], ACT.Square,
                                   accum_out=sq[:, t:t + 1]).then_inc(*sent.one(sq_ready))

            def h_summed(t):
                act.wait_ge(acc_done, due.total(acc_done) - 1 + t)

            def h_normed(t):
                act.wait_ge(h_ready, due(h_ready))

            def turned(tiles_=KT, per_bank=4):
                for t in range(TT):
                    for a in range(0, tiles_, per_bank):
                        n = min(per_bank, tiles_ - a)
                        m = jobs[0]
                        jobs[0] += 1
                        act.wait_ge(mid_full, due(mid_full))
                        act.activation(xT_hi[:, a:a + n, t * P:(t + 1) * P],
                                       mid[:, m % 2, 0:n * P].rearrange("p (k q) -> p k q", q=P),
                                       ACT.Copy).then_inc(thi_ready, 1)

            def mids(n, signalled):
                jobs[0] += n
                due(mid_full, signalled)

            def f_chunks(n):
                ahead(n)
                mids(n, 0)

            def t_chunks(n):
                ahead(n)
                due(acc_done, TT)

            def ffn():
                base, g0 = at[0], hidden[0]

                def step(c, j, r, g):
                    act.wait_ge(chunk_used, c + 1)
                    act.activation(ff_s[:, r, 0:T], mid[:, r, 0:T], ACT.Silu).then_inc(act_ready, 1)
                    act.wait_ge(g_ready, j + 1)
                    act.activation(g_hi[:, g, :], ff_g[:, r, 0:T], ACT.Copy).then_inc(ghi_ready, 1)

                for j in range(4):
                    split_at(base + j + AHEAD)
                    step(base + j, g0 + j, j % 2, j % 4)
                split_at(base + 4 + AHEAD)
                first, loops = base + 5, (FF_TILES // 2 - 3) // 2
                with act.Fori(0, loops) as i:
                    for b in range(2):
                        s = first + 3 * b
                        for n in range(2):
                            split_in_loop(s + n + AHEAD, i, 6)
                            step(i * 6 + (s + n), i * 4 + (g0 + 4 + 2 * b + n), n, 2 * b + n)
                        split_in_loop(s + 2 + AHEAD, i, 6)
                c, j = first + 6 * loops, 4 + 4 * loops
                for n in range(2):
                    split_at(c + n + AHEAD)
                    step(c + n, g0 + j + n, n, (j + n) % 4)
                hidden[0] += FF_TILES
                at[0] = c + 2
                t_chunks(2)

            def mlp():
                base, s0 = at[0], hidden[0]
                banks = [mid[:, 0, :], mid[:, 1, :], aux[:, 0, :]]

                def step(c, j, r, wait=True):
                    act.wait_ge(chunk_used, c + 1)
                    if wait:
                        act.wait_ge(glo_ready, j - 2)
                    act.activation(ff_s[:, r, :], banks[r], ACT.Relu).then_inc(act_ready, 1)
                    act.wait_ge(act_ready, j + 1)
                    act.activation(g_hi[:, 2 * r:2 * r + 2, :], ff_s[:, r, :].rearrange("p (k q) -> p k q", k=2),
                                   ACT.Square).then_inc(ghi_ready, 1)

                def steps(j):
                    c = base + 2 * j - 1
                    split_at(c + AHEAD)
                    step(c, s0 + j, j % 3, j >= 3)
                    split_at(c + 1 + AHEAD)

                split_at(base + AHEAD)
                step(base, s0, 0, False)
                for j in range(1, 4):
                    steps(j)
                loops = (MLP_STEPS - 4) // 3
                if base + MLP_CHUNKS == N_CHUNKS:
                    loops -= 1
                with act.Fori(0, loops) as i:
                    for b in range(3):
                        s = base + 7 + 2 * b
                        split_in_loop(s + AHEAD, i, 6)
                        step(i * 6 + s, i * 3 + (s0 + 4 + b), (4 + b) % 3)
                        split_in_loop(s + 1 + AHEAD, i, 6)
                for j in range(4 + 3 * loops, MLP_STEPS):
                    steps(j)
                hidden[0] += MLP_STEPS
                at[0] = base + MLP_CHUNKS - 1
                t_chunks(1)

            def attention(n_units, full=False, maps=1, sink=False):
                segs = [(0, T), (T, T)] if full else SEG
                width = 2 * T if full else KEYCOLS

                def unit(u):
                    for _ in range(maps):
                        m, e = jobs[0], scored[0]
                        jobs[0] += 1
                        scored[0] += 1
                        due(mid_full)
                        act.wait_ge(mid_done, m + 1)
                        if u >= 2:
                            act.wait_ge(turned_full, u0 + u - 1) if maps == 1 else act.wait_ge(pc_ready, u - 1)
                        for qt in range(TT):
                            a, n = segs[qt]
                            if sink:
                                act.activation(esink[:, e % 4, qt:qt + 1], sinkt[:, u:u + 1], ACT.Exp,
                                               bias=nmax[:, e % 4, qt:qt + 1])
                            ins = act.activation(P_[:, e % 4, a:a + n], N_[:, e % 2, a:a + n], ACT.Exp,
                                                 bias=nmax[:, e % 4, qt:qt + 1], scale=-1.0,
                                                 accum_out=rsum[:, e % 4, qt:qt + 1])
                        ins.then_inc(exp_ready, 1)

                def copied(u):
                    n = u0 + u
                    act.wait_ge(turned_full, n + 1)
                    if n >= 2:
                        act.wait_ge(o_full, n - 1)
                    act.activation(PT_[:, n % 2, 0:width], aux[:, n % 2, 0:width],
                                   ACT.Copy).then_inc(turned_done, 1)

                u0 = units[0]
                unit(0)
                for u in range(n_units):
                    if u + 1 < n_units:
                        unit(u + 1)
                    copied(u)
                units[0] += n_units

            def mixer():
                squares(h, h_summed)
                turned()
                f_chunks(MIX_F)
                t_chunks(MIX_V)
                act.wait_ge(lam_dots, 1)
                act.activation(lam[:, 0:2], lam[:, 0:2], ACT.Exp).then_inc(lam_exps, 1)
                for v in range(2):
                    act.wait_ge(blk_ready, v + 1)
                    if v:
                        act.wait_ge(chunk_used, at[0])
                    act.activation(blk_hi[:, 0:JJ * CCOLS], blk, ACT.Copy).then_inc(blkhi_ready, 1)
                    ahead(2)
                    mids(2, 1)
                act.wait_ge(mid_done, jobs[0])
                act.activation(hidg[:], hid[:], ACT.Gelu_apprx_tanh).then_inc(gelu_ready, 1)
                mids(2, 2)
                act.wait_ge(acc_done, due.total(acc_done))
                act.activation(gate[:], vtok[:, :, GATE_COL:MIXV_W], ACT.Exp, scale=-1.0).then_inc(gexp_ready, 1)
                mids(2, 2)
                act.wait_ge(cs_ready, 1)
                act.activation(ce[:], cs[:], ACT.Exp).then_inc(ce_ready, 1)
                act.wait_ge(cpt_full, 1)
                act.activation(cpT[:], aux[:, 0, :].rearrange("p (a q) -> p a q", a=4),
                               ACT.Copy).then_inc(cpt_done, 1)
                attention(16)
                attention(8, sink=True)
                turned()
                t_chunks(MIX_O)

            def even_mixer():
                squares(h, h_normed)
                turned()
                f_chunks(EV_F)
                t_chunks(2)
                t_chunks(2)
                for t in range(TT):
                    act.wait_ge(acc_done, due.total(acc_done) - 1 + t)
                    for i, (a, n) in enumerate(((0, 2 * P), (2 * P, P))):
                        ins = act.activation(junk[:, t * CQ_W + a:t * CQ_W + a + n], cqs[:, t, a:a + n], ACT.Square,
                                             accum_out=sq[:, 2 * t + i:2 * t + i + 1])
                    ins.then_inc(*sent.one(sq_ready))
                turned(CQ_W // P)
                attention(4, maps=2)
                ahead(1)
                mids(4, 3)
                mids(2, 2)
                t_chunks(1)
                attention(4)
                turned()
                t_chunks(EV_O)

            def cross(n):
                squares(obuf, lambda t: act.wait_ge(mem_full, 16 * n))
                turned()
                f_chunks(4)
                n_h = due.total(acc_done)
                t_chunks(4)
                squares(h, lambda t: act.wait_ge(acc_done, n_h))
                turned()
                f_chunks(4)
                attention(4, full=True)
                turned()
                t_chunks(4)

            def odd_mixer():
                squares(h, h_summed)
                turned()
                f_chunks(8)
                t_chunks(4)

                def own(ins):
                    ins.then_inc(*sent.one(act_own))
                    act.wait_ge(act_own, sent.total(act_own))

                for g in range(4):
                    m = sb_m[:, g % 2, :]
                    act.wait_ge(m_ready, g + 1)
                    own(act.activation(sb_l, m, ACT.Abs))
                    own(act.activation(sb_l, sb_l, ACT.Exp, scale=-1.0))
                    act.activation(sb_l, sb_l, ACT.Ln, bias=1.0).then_inc(ln_ready, 1)
                    act.wait_ge(zs_ready, g + 1)
                    if g:
                        act.wait_ge(so_full, g)
                    act.activation(sb_a, m, ACT.Exp).then_inc(a_ready, 1)
                turned()
                t_chunks(4)

            for c in range(AHEAD):
                split_at(c)
            squares(h, lambda t: act.wait_ge(x_full, 16))
            turned()
            ffn()
            mixer()
            squares(h, h_summed)
            turned()
            ffn()
            squares(h, h_summed)
            even_mixer()
            cross(1)
            squares(h, h_summed)
            turned()
            mlp()
            odd_mixer()
            cross(2)
            squares(h, h_summed)
            turned()
            mlp()
            squares(h, h_summed)

        @block.gpsimd
        def _(pool):
            sent, due = Tally(), Tally()
            norms = [0]
            loaded = [0]
            normed = [0]

            def own(ins):
                ins.then_inc(*sent.one(pool_own))
                pool.wait_ge(pool_own, sent.total(pool_own))

            def load_gain(k):
                if k < N_GAINS:
                    pool.dma_start(gain[:, k % 2, :],
                                   gains[k:k + 1, :].to_broadcast([P, D])).then_inc(gain_full[k % 2], 16)

            def inverse(a, n, width):
                own(pool.tensor_scalar(ms[:, a:a + n], sq[:, a:a + n], 1.0 / width, EPS, ALU.mult, ALU.add))

            def norm(in_place=False):
                for t in range(TT):
                    pool.wait_ge(sq_ready, due(sq_ready))
                    inverse(t, 1, D)
                    pool.tensor_tensor(rstd[:, t:t + 1], ms[:, t:t + 1], nhalf[:, t:t + 1],
                                       ALU.pow).then_inc(*sent.one(rstd_ready))
                k = norms[0]
                norms[0] += 1
                s = h_ready if in_place else xn_ready
                n = due(s, TT)
                if k + 2 < N_GAINS:
                    pool.wait_ge(s, n)
                    load_gain(k + 2)

            def biases(n):
                for _ in range(n):
                    k = loaded[0]
                    loaded[0] += 1
                    if k >= BIAS_SLOTS:
                        pool.wait_ge(mid_done, bias_used_at[k - BIAS_SLOTS])
                    pool.dma_start(bias[:, k % BIAS_SLOTS, :], bias_tiles[k]).then_inc(bias_full[k % BIAS_SLOTS], 16)

            def load_mem(n):
                pool.wait_ge(mid_done, obuf_turned_at[n])
                pool.dma_start(obuf[:], mem.rearrange("(t p) d -> p t d", p=P)).then_inc(mem_full, 16)

            load_gain(0)
            load_gain(1)
            own(pool.memset(nhalf[:], -0.5))
            biases(BIAS_SLOTS)
            norm()
            norm()
            biases(16 - BIAS_SLOTS)
            norm()
            norm(True)
            norm()
            biases(4)
            for t in range(TT):
                pool.wait_ge(sq_ready, due(sq_ready))
                inverse(2 * t, 1, 2 * P)
                inverse(2 * t + 1, 1, P)
                pool.tensor_tensor(rstd[:, 2 * t:2 * t + 2], ms[:, 2 * t:2 * t + 2], nhalf[:, 0:2],
                                   ALU.pow).then_inc(*sent.one(rstd_ready))
            due(xn_ready, TT)
            biases(1)
            pool.wait_ge(dsq_ready, 1)
            inverse(0, 8, P)
            pool.tensor_tensor(rstd[:, 0:8], ms[:, 0:8], nhalf[:, 0:8], ALU.pow).then_inc(*sent.one(rstd_ready))
            load_mem(0)
            norm()
            norm()
            norm()
            norm()
            load_mem(1)
            norm()
            norm()
            norm()
            norm(True)

        @block.sync
        def _(sp):
            sp.dma_start(h[:], x.rearrange("(t p) d -> p t d", p=P)).then_inc(x_full, 16)
            sp.dma_start(ident[:], squares_in[0]).then_inc(ident_full, 16)
            for c in range(RING):
                sp.dma_start(raw[:, c, :], stream[c]).then_inc(raw_full[c], 16)
            consts = [(tri, squares_in[1]), (ones, squares_in[2]),
                      (zeros[:, 0:P], squares_in[3]), (zeros[:, P:T], squares_in[3]), (sbm, sb_mask),
                      (ropet, rope), (cbias, cmp_bias), (cmask, cmp_mask), (cqg, cq_gain.to_broadcast([P, CQ_W])),
                      (subg, sub_gain.to_broadcast([P, P])), (sinkt, sinks.to_broadcast([P, 8])),
                      (posT, cmp_pos), (b1T, cmp_b1), (w2k, cmp_w2k), (w2v, cmp_w2v)]
            consts += [(lamv[:, i, :], lam_vecs[i:i + 1, :].to_broadcast([P, DH])) for i in range(4)]
            assert len(consts) == n_const
            for dst, src in consts:
                sp.dma_start(dst[:], src).then_inc(const_full, 16)
            rounds = N_CHUNKS // RING
            with sp.Fori(1, rounds) as i:
                for s in range(RING):
                    sp.wait_ge(lo_ready, i * RING + (s + 1 - RING))
                    sp.dma_start(raw[:, s, :], stream[i * RING + s]).then_inc(raw_full[s], 16)
            for c in range(rounds * RING, N_CHUNKS):
                sp.wait_ge(lo_ready, c - RING + 1)
                sp.dma_start(raw[:, c % RING, :], stream[c]).then_inc(raw_full[c % RING], 16)
            sp.wait_ge(last_h[0], last_h[1])
            sp.dma_start(out.rearrange("(t p) d -> p t d", p=P), h[:]).then_inc(out_full, 16)
            sp.wait_ge(out_full, 16)



def weight_stream(w):
    chunks = []

    def put(a):
        a = a.reshape(P, -1)
        full = np.zeros((P, CH), np.float32)
        full[:, :a.shape[1]] = a
        chunks.append(full)

    def f_chunk(m, cols):
        put(m[:, cols].reshape(-1, P, len(cols)).transpose(1, 0, 2))

    def f_tiles(m, tiles):
        for i in range(0, len(tiles), 2):
            f_chunk(m, np.concatenate(tiles[i:i + 2]))

    def t_chunks(m, kts):
        for i in range(0, m.shape[0] // P, kts):
            put(m[i * P:(i + kts) * P].reshape(kts, P, m.shape[1]).transpose(1, 0, 2))

    def cols(a, n=P):
        return np.arange(a, a + n)

    def ffn(w_in, w_out):
        def ins(j):
            f_chunk(w_in, np.concatenate([cols(j * P), cols(D_FF + j * P)]))

        def outs(k):
            t_chunks(w_out[2 * k * P:2 * (k + 1) * P], 2)

        for j in range(4):
            ins(j)
        outs(0)
        for k in range(1, FF_TILES // 2 - 1):
            ins(2 * k + 2)
            ins(2 * k + 3)
            outs(k)
        outs(FF_TILES // 2 - 1)

    def mlp(w1, w2):
        f_chunk(w1, cols(0, 2 * P))
        for j in range(1, MLP_STEPS):
            f_chunk(w1, cols(j * 2 * P, 2 * P))
            t_chunks(w2[(j - 1) * 2 * P:j * 2 * P], 2)
        t_chunks(w2[(MLP_STEPS - 1) * 2 * P:], 2)

    def mixer():
        m = w["w_mix_in"][0]
        kv = 512
        qb = 512 + 768 + 24
        kvb = qb + 512
        tiles = [np.tile(cols(kv + b * P + g * DH, DH), 2) for b in (0, 1) for g in (0, 1)]
        tiles += [cols(kv + 2 * P), cols(kv + 4 * P), cols(kvb)]
        for q in (0, qb):
            tiles += [np.concatenate([cols(q + r * DH, DH), cols(q + (4 + r) * DH, DH)]) for r in range(4)]
        tiles.append(tiles[-1])
        f_tiles(m, tiles)
        t_chunks(m[:, np.concatenate([cols(kv + 3 * P), cols(kv + 5 * P), cols(kvb + P), cols(kv + 768, 24)])], 4)
        for name in ("cmp_k_w1", "cmp_v_w1"):
            t_chunks(w[name][0], 8)
        t_chunks(w["w_mix_out"][0], 2)

    def even():
        m = w["ev_w_in_2"][0]
        kr = 512 * 3 + 256 + 128
        swapped = np.concatenate([cols(32, 32), cols(0, 32)])
        tiles = [cols(i * P) for i in range(8)] + [np.tile(cols(kr, DH), 2), np.tile(kr + swapped, 2)]
        f_tiles(m, tiles)
        t_chunks(m[:, 1024:1536], 4)
        t_chunks(m[:, 1536:1536 + CQ_W], 4)
        u = w["mla_w_uq_2"][0]
        nope = [cols(hd * 192) for hd in range(4)]
        rope = [cols(hd * 192 + P, DH) for hd in range(4)]
        rope_swapped = [hd * 192 + P + swapped for hd in range(4)]
        t_chunks(u[:, np.concatenate(nope + rope + rope_swapped)], 2)
        u = w["mla_w_ukv_2"][0]
        t_chunks(u[:, np.concatenate([cols(hd * T) for hd in range(4)] + [cols(hd * T + P) for hd in range(4)])], 1)
        t_chunks(w["ev_w_out_2"][0], 2)

    def cross(l):
        kv = w["xa_wkv_2"][l]
        f_tiles(kv, [cols(i * P) for i in range(8)])
        t_chunks(kv[:, D:], 2)
        f_tiles(w["xa_wq_2"][l], [cols(i * P) for i in range(8)])
        t_chunks(w["xa_wo_2"][l], 2)

    def odd():
        m = w["sb_w_in_2"][0]
        f_tiles(m, [cols(i * P) for i in range(16)])
        t_chunks(m[:, 2 * D:], 2)
        t_chunks(w["sb_w_out_2"][0], 2)

    ffn(w["ffn1_w_in"][0], w["ffn1_w_out"][0])
    mixer()
    ffn(w["ffn2_w_in"][0], w["ffn2_w_out"][0])
    even()
    cross(0)
    mlp(w["mlp_w1_2"][0], w["mlp_w2_2"][0])
    odd()
    cross(1)
    mlp(w["mlp_w1_2"][1], w["mlp_w2_2"][1])
    assert len(chunks) == N_CHUNKS
    return np.stack(chunks)


def shape_constants():
    q, k = np.arange(T)[:, None], np.arange(T)[None, :]
    dist = (q - k).astype(np.float32)

    def tile(values, allowed, scale):
        b = np.where(allowed, values, NEG) / scale
        return np.concatenate([b[:P, :P], b[P:, :]], axis=1).astype(np.float32)

    slopes8 = 2.0 ** (-8.0 * np.arange(1, 9) / 8)
    slopes4 = 2.0 ** (-8.0 * np.arange(1, 5) / 4)
    causal = dist >= 0
    chunked = (k // 64) <= (q // 64)
    tiles = [tile(-s * dist, causal, ATTN_SCALE) for s in slopes8]
    tiles += [tile(-s * dist, causal & (dist < 128), ATTN_SCALE) for s in slopes8]
    tiles += [tile(-s * np.abs(dist), chunked, ATTN_SCALE) for s in slopes4]
    tiles += [tile(0 * dist, chunked, MLA_SCALE)]
    strict = np.where(q.T > k.T, 0.0, NEG).astype(np.float32)
    sb_mask = np.concatenate([strict[:P, :], strict[P:, P:], strict[P:, P:]], axis=1)
    end = np.arange(CBLK) * 16 + 31
    cbias = np.zeros((P, 2, TT, 4, CBLK), np.float32)
    cmask = np.zeros((P, 2, TT, 4, CBLK), np.float32)
    for qt in range(TT):
        d = (qt * P + np.arange(P))[:, None] - end[None, :]
        for g in range(2):
            for r in range(4):
                cbias[:, g, qt, r] = np.where(d >= 0, -slopes8[g * 4 + r] * d, NEG)
                cmask[:, g, qt, r] = d >= 0
    inv = (10000.0 ** (-np.arange(32, dtype=np.float32) / 32)).astype(np.float32)
    ang = inv[:, None] * np.arange(T, dtype=np.float32)[None, :]
    cos, sin = np.cos(ang), np.sin(ang)
    rope = np.stack([np.concatenate([cos] * 4), np.concatenate([-sin, sin] * 2)], axis=1).astype(np.float32)
    eye, tri = np.eye(P), np.tril(np.ones((P, P)))
    squares = np.stack([eye, tri, np.ones((P, P)), np.zeros((P, P))]).astype(np.float32)
    return {
        "bias_tiles": np.stack(tiles), "sb_mask": sb_mask.astype(np.float32),
        "cmp_bias": cbias.reshape(P, 16, CBLK), "cmp_mask": cmask.reshape(P, 16, CBLK),
        "rope": rope, "squares_in": squares,
    }


def kernel(**inputs):
    import concourse.bacc as _bacc
    from concourse.bass_utils import run_bass_kernel_spmd as _run

    w = {n: np.asarray(a) for n, a in inputs.items()}
    arrays = {
        "stream": weight_stream(w),
        "x": w["x"][0],
        "mem": w["mem_2"][0],
        "gains": np.stack([w["ffn1_norm"][0], w["mix_norm"][0], w["ffn2_norm"][0], w["final_norm"],
                           w["ev_norm_2"][0], w["xa_mem_norm_2"][0], w["xa_norm_2"][0], w["mlp_norm_2"][0],
                           w["od_norm_2"][0], w["xa_mem_norm_2"][1], w["xa_norm_2"][1], w["mlp_norm_2"][1],
                           w["final_norm_2"]]),
        "cq_gain": np.concatenate([w["mla_g_cq_2"], w["mla_g_ckv_2"]], axis=1),
        "sub_gain": w["diff_subln_2"],
        "lam_vecs": np.concatenate([w["diff_lq1_2"], w["diff_lk1_2"], w["diff_lq2_2"], w["diff_lk2_2"]]),
        "sinks": w["swa_sinks"],
        "cmp_pos": np.stack([w[n][0].reshape(JJ, P).T for n in ("cmp_k_pos", "cmp_v_pos")], axis=1),
        "cmp_b1": np.stack([w[n][0].reshape(2, P).T for n in ("cmp_k_b1", "cmp_v_b1")], axis=1),
        "cmp_w2k": np.concatenate([w["cmp_k_w2"][0].reshape(2, P, DH)] * 2, axis=2).transpose(1, 0, 2),
        "cmp_w2v": w["cmp_v_w2"][0].reshape(2, P, DH).transpose(1, 0, 2),
        **shape_constants(),
    }
    nc = _bacc.Bacc("TRN2", target_bir_lowering=False, num_devices=1)
    args = {}
    for n in arrays:
        arrays[n] = np.ascontiguousarray(arrays[n])
        args[n] = nc.dram_tensor(f"in_{n}", arrays[n].shape, F32, kind="ExternalInput").ap()
    args["out"] = nc.dram_tensor("out_0", (T, D), F32, kind="ExternalOutput").ap()
    program(nc, **args)
    r = _run(nc, [{f"in_{n}": a for n, a in arrays.items()}], core_ids=[0])
    return r.results[0]["out_0"].reshape(1, T, D)
```

```python
from contextlib import ExitStack

import numpy as np

import concourse.bass as bass
from concourse import mybir

F32 = mybir.dt.float32
F32R = mybir.dt.float32r
ACT = mybir.ActivationFunctionType
ALU = mybir.AluOpType
AX = mybir.AxisListType

P = 128
T = 256
TT = T // P
D = 1024
KT = D // P
CH = 2048
RING = 3
AHEAD = 2
DH = 64
EPS = 1e-6
NEG = -1e30
D_FF = 2816
FF_TILES = D_FF // P
D_MLP = 4096
MLP_STEPS = D_MLP // (2 * P)
CBLK = 15
CCOLS = 2 * CBLK
JJ = 16
KEYCOLS = P + T
SEG = [(0, P), (P, T)]
ATTN_SCALE = DH ** -0.5
MLA_SCALE = 192 ** -0.5
XA_SCALE = 256 ** -0.5
LAMBDA_INIT = 0.2
BIAS_SLOTS = 3

FFN_CHUNKS = FF_TILES + FF_TILES // 2
MIX_F, MIX_V, MIX_C, MIX_O = 8, 2, 4, 4
EV_F, EV_V, EV_M, EV_O = 5, 4, 2, 4
XA_CHUNKS = 16
MLP_CHUNKS = 2 * MLP_STEPS
SB_CHUNKS = 16
N_GAINS = 13
N_CHUNKS = (2 * FFN_CHUNKS + MIX_F + MIX_V + MIX_C + MIX_O + EV_F + EV_V + EV_M + EV_O
            + 2 * XA_CHUNKS + 2 * MLP_CHUNKS + SB_CHUNKS)

KC, VC, KS, KW, KB, QA, QB = 0, 2, 4, 5, 6, 7, 11
VS_COL, VW_COL, VB_COL, GATE_COL, MIXV_W = 0, 128, 256, 384, 408
CQ_W = 384


class Tally:

    def __init__(self):
        self.n = {}

    def __call__(self, sem, k=1):
        self.n[sem.name] = self.n.get(sem.name, 0) + k
        return self.n[sem.name]

    def total(self, sem):
        return self.n.get(sem.name, 0)

    def one(self, sem):
        self(sem)
        return sem, 1


def program(nc, stream, x, mem, gains, cq_gain, sub_gain, lam_vecs, sinks, cmp_pos, cmp_b1, cmp_w2k,
            cmp_w2v, bias_tiles, sb_mask, cmp_bias, cmp_mask, rope, squares_in, out):
    with ExitStack() as ctx:
        def sb(name, shape, dt=F32):
            return ctx.enter_context(nc.sbuf_tensor(name, shape, dt))

        def psum(name, shape):
            return ctx.enter_context(nc.psum_tensor(name, shape, F32))

        def sem(name):
            return ctx.enter_context(nc.semaphore(name))

        raw = sb("raw", [P, RING, CH])
        w_hi = sb("w_hi", [P, RING, CH], F32R)
        w_lo = sb("w_lo", [P, RING, CH], F32R)
        h = sb("h", [P, TT, D])
        xn = sb("xn", [P, TT, D])
        gain = sb("gain", [P, 2, D])
        xT_hi = sb("xT_hi", [P, KT, T], F32R)
        xT_lo = sb("xT_lo", [P, KT, T], F32R)
        g_hi = sb("g_hi", [P, 6, T], F32R)
        g_lo = sb("g_lo", [P, 6, T], F32R)
        proj = sb("proj", [P, 16, T])
        vtok = sb("vtok", [P, TT, D])
        memkT = sb("memkT", [P, KT, T])
        memv = sb("memv", [P, TT, D])
        obuf = sb("obuf", [P, TT, D])
        work = sb("work", [P, 6144])
        bias = sb("bias", [P, BIAS_SLOTS, KEYCOLS])
        ident = sb("ident", [P, P])
        zero = sb("zero", [P, 1])
        sbm = sb("sbm", [P, 2 * T])
        subg = sb("subg", [P, P])
        sinkt = sb("sinkt", [P, 8])
        nsink = sb("nsink", [P, 8])
        tri = sb("tri", [P, P])
        ones = sb("ones", [P, P])
        gate = sb("gate", [P, TT, 24])
        lam = sb("lam", [P, 4])
        sq = sb("sq", [P, 8])
        ms = sb("ms", [P, 8])
        rstd = sb("rstd", [P, 8])
        nhalf = sb("nhalf", [P, 8])
        nmax = sb("nmax", [P, 4, 4])
        rsum = sb("rsum", [P, 4, 4])
        rinv = sb("rinv", [P, 4, 4])
        esink = sb("esink", [P, 4, 2])
        cst = sb("cst", [P, 3, 16])

        def cut(buf, a, *dims):
            n = int(np.prod(dims))
            v = buf.rearrange("p a b -> p (a b)")[:, a:a + n]
            names = "abcd"[:len(dims)]
            if len(dims) == 1:
                return v
            return v.rearrange("p (" + " ".join(names) + ") -> p " + " ".join(names), **dict(zip(names, dims)))

        cbias = cut(memkT, 0, 16, CBLK)
        cmask = cut(memkT, 256, 16, CBLK)
        posT = cut(memkT, 512, 2, JJ)
        b1T = cut(memkT, 544, 2, 2)
        w2k = cut(memkT, 576, 2, P)
        w2v = cut(memkT, 832, 2, DH)
        kcT = cut(memkT, 960, CCOLS)
        vcd = cut(memkT, 1024, 2, 4, DH)
        ropet = cut(memkT, 1536, 2, T)
        cqg = cut(memv, 0, CQ_W)
        lamv = cut(memv, 512, 4, DH)
        knope = [memv[:, i // 2, 512 + i % 2 * T:512 + (i % 2 + 1) * T] for i in range(4)]
        blk_hi = g_hi.rearrange("p a b -> p (a b)")
        blk_lo = g_lo.rearrange("p a b -> p (a b)")

        mix_pad = [work[:, 5120 + i * T:5120 + (i + 1) * T] for i in range(3)]
        diff_pad = [memkT[:, i, :] for i in (0, 1, 2, 4)]
        rope_pad = proj[:, 9, :]

        acc = psum("acc", [P, 4, 512])
        mid = psum("mid", [P, 2, 512])
        aux = psum("aux", [P, 2, 512])

        raw_full = [sem(f"raw_full{i}") for i in range(RING)]
        gain_full = [sem(f"gain_full{i}") for i in range(2)]
        bias_full = [sem(f"bias_full{i}") for i in range(BIAS_SLOTS)]
        x_full = sem("x_full")
        ident_full = sem("ident_full")
        mem_full = sem("mem_full")
        const_full = sem("const_full")
        out_full = sem("out_full")
        hi_ready = sem("hi_ready")
        lo_ready = sem("lo_ready")
        chunk_used = sem("chunk_used")
        sq_ready = sem("sq_ready")
        dsq_ready = sem("dsq_ready")
        rstd_ready = sem("rstd_ready")
        xn_ready = sem("xn_ready")
        h_ready = sem("h_ready")
        mid_full = sem("mid_full")
        mid_done = sem("mid_done")
        thi_ready = sem("thi_ready")
        acc_full = sem("acc_full")
        acc_done = sem("acc_done")
        act_ready = sem("act_ready")
        g_ready = sem("g_ready")
        ghi_ready = sem("ghi_ready")
        glo_ready = sem("glo_ready")
        exp_ready = sem("exp_ready")
        pc_ready = sem("pc_ready")
        turned_full = sem("turned_full")
        turned_done = sem("turned_done")
        o_full = sem("o_full")
        o_done = sem("o_done")
        lam_dots = sem("lam_dots")
        lam_exps = sem("lam_exps")
        blk_ready = sem("blk_ready")
        blkhi_ready = sem("blkhi_ready")
        blklo_ready = sem("blklo_ready")
        gelu_ready = sem("gelu_ready")
        hidd_ready = sem("hidd_ready")
        gexp_ready = sem("gexp_ready")
        cs_ready = sem("cs_ready")
        ce_ready = sem("ce_ready")
        cp_ready = sem("cp_ready")
        cpt_full = sem("cpt_full")
        cpt_done = sem("cpt_done")
        co_full = sem("co_full")
        co_done = sem("co_done")
        rope_ready = sem("rope_ready")
        dnorm_ready = sem("dnorm_ready")
        z_full = sem("z_full")
        m_ready = sem("m_ready")
        act_own = sem("act_own")
        ln_ready = sem("ln_ready")
        sp_ready = sem("sp_ready")
        s_full = sem("s_full")
        zs_ready = sem("zs_ready")
        a_ready = sem("a_ready")
        so_full = sem("so_full")
        side_done = sem("side_done")
        so_done = sem("so_done")
        cmp_full = sem("cmp_full")
        cmp_done = sem("cmp_done")
        dve_own = sem("dve_own")
        pool_own = sem("pool_own")

        n_const = 18
        bias_used_at = []
        obuf_turned_at = []
        last_h = []
        block = ctx.enter_context(nc.Block())

        N_ = work[:, 0:1024].rearrange("p (r c) -> p r c", r=2)
        P_ = work[:, 1024:3072].rearrange("p (r c) -> p r c", r=4)
        PT_ = work[:, 3072:4096].rearrange("p (r c) -> p r c", r=2)
        PC_ = work[:, 4096:5120].rearrange("p (r c) -> p r c", r=2)
        junk = work[:, 5120:6144]
        ff_s = work[:, 0:1536].rearrange("p (r c) -> p r c", r=3)
        ff_g = work[:, 1536:3072].rearrange("p (r c) -> p r c", r=3)
        rot = work[:, 1024:2304].rearrange("p (a c) -> p a c", c=T)
        cqs = work[:, 0:2 * CQ_W].rearrange("p (t c) -> p t c", t=2)
        SBW = 2 * KEYCOLS
        sb_m = work[:, 0:2 * SBW].rearrange("p (r c) -> p r c", r=2)
        sb_l = work[:, 2 * SBW:4 * SBW].rearrange("p (r c) -> p r c", r=2)
        sb_a = work[:, 4 * SBW:6 * SBW].rearrange("p (r c) -> p r c", r=2)
        blk = cut(xn, 0, JJ * CCOLS)
        pre = cut(xn, 512, T)
        hid = cut(xn, 768, 2, 2, CCOLS)
        hidg = cut(xn, 896, 2, 2, CCOLS)
        hidd_flat = cut(xn, 1024, 4 * P)
        hidd = hidd_flat.rearrange("p (m g r c) -> p m g r c", m=2, g=2, r=4)
        cs = cut(xn, 1536, 16, CBLK)
        ce = cut(xn, 1792, 16, CBLK)
        cp_flat = work[:, 4096:4608]
        cp = cp_flat.rearrange("p (a c) -> p a c", a=16)
        cpT = work[:, 4608:5120].rearrange("p (a q) -> p a q", a=4)

        def grp(g):
            return slice(DH * g, DH * (g + 1))

        def mix_keys(g, i):
            return mix_pad[i] if g else proj[:, KS + i, :]

        def sb_heads(p):
            first = 4 * (p // 2) + p % 2
            return first, first + 2

        @block.tensor
        def _(pe):
            sent, due = Tally(), Tally()
            at = [0]
            jobs = [0]
            hidden = [0]
            scored = [0]
            turned_at = [0, 1, 0]

            def mid_bank():
                n = jobs[0]
                jobs[0] += 1
                if n >= 2:
                    pe.wait_ge(mid_done, n - 1)
                return mid[:, n % 2, :]

            def three(out_ap, lhs, rhs, start, stop):
                pe.matmul(out_ap, lhs[0], rhs[0], start=start, stop=False)
                pe.matmul(out_ap, lhs[0], rhs[1], start=False, stop=False)
                return pe.matmul(out_ap, lhs[1], rhs[0], start=False, stop=stop)

            def w_pair(slot, a, n):
                return w_hi[:, slot, a:a + n], w_lo[:, slot, a:a + n]

            def xT_pair(k, t):
                xT_stands(k, t)
                return xT_hi[:, k, t * P:(t + 1) * P], xT_lo[:, k, t * P:(t + 1) * P]

            def xT_stands(k, t):
                n = turned_at[0] + t * turned_at[1] + k // 4 + 1
                if n > turned_at[2]:
                    pe.wait_ge(mid_done, n)
                    turned_at[2] = n

            def f_tile(out_ap, slot, kts, width, col):
                for k in range(kts):
                    xT_stands(k, TT - 1)
                    mm = three(out_ap, w_pair(slot, k * width + col, P), (xT_hi[:, k, :], xT_lo[:, k, :]),
                               k == 0, k == kts - 1)
                return mm

            def f_chunks(n):
                for _ in range(n):
                    c = at[0]
                    bank = mid_bank()
                    pe.wait_ge(lo_ready, c + 1)
                    for m in range(2):
                        mm = f_tile(bank[:, m * T:(m + 1) * T], c % RING, KT, 2 * P, m * P)
                    mm.then_inc(chunk_used, 1)
                    at[0] += 1

            def t_chunk(slot, lhs, kts, width, halves, start, stop):
                for t in range(TT):
                    for k in range(kts):
                        for half in range(halves):
                            w = min(width, 512)
                            mm = three(acc[:, t * halves + half, 0:w], lhs(k, t),
                                       w_pair(slot, k * width + half * 512, w),
                                       start and k == 0, stop and k == kts - 1)
                    if stop and t == 0:
                        mm.then_inc(acc_full, 1)
                mm.then_inc(chunk_used, 1)

            def acc_free():
                if due.total(acc_done):
                    pe.wait_ge(acc_done, due.total(acc_done))
                due(acc_done, TT)

            def t_chunks(width):
                kts, halves = (2, 2) if width == D else (4, 1)
                n = KT // kts
                acc_free()
                for i in range(n):
                    c = at[0]
                    pe.wait_ge(lo_ready, c + 1)
                    t_chunk(c % RING, lambda k, t: xT_pair(i * kts + k, t), kts, width, halves,
                            i == 0, i == n - 1)
                    at[0] += 1

            def turn(src, ready, tiles=KT, per_bank=4):
                turned_at[:] = [jobs[0], -(-tiles // per_bank), 0]
                for t in range(TT):
                    for a in range(0, tiles, per_bank):
                        ready(t, a)
                        bank = mid_bank()
                        for k in range(a, min(a + per_bank, tiles)):
                            mm = pe.transpose(bank[:, (k - a) * P:(k - a + 1) * P],
                                              src[:, t, k * P:(k + 1) * P], ident[:])
                        mm.then_inc(*sent.one(mid_full))

            def normed(t, a):
                pe.wait_ge(xn_ready, due(xn_ready))

            def heads_out(t, a):
                pe.wait_ge(o_done, sent.total(o_full))

            def g_pair(j):
                return lambda k, t: (g_hi[:, j * 2 + k, t * P:(t + 1) * P], g_lo[:, j * 2 + k, t * P:(t + 1) * P])

            def ffn():
                base, g0 = at[0], hidden[0]
                pairs = FF_TILES // 2

                def step_in(c, j, slot, r, wait=True):
                    pe.wait_ge(lo_ready, c + 1)
                    if wait:
                        pe.wait_ge(g_ready, j - 1)
                    for m in range(2):
                        mm = f_tile(mid[:, r, m * T:(m + 1) * T], slot, KT, 2 * P, m * P)
                    mm.then_inc(chunk_used, 1)

                def step_out(c, j, slot, pair, start, stop):
                    pe.wait_ge(lo_ready, c + 1)
                    pe.wait_ge(glo_ready, j)
                    t_chunk(slot, g_pair(pair), 2, D, 2, start, stop)

                acc_free()
                for j in range(4):
                    step_in(base + j, g0 + j, (base + j) % RING, j % 2, j >= 2)
                step_out(base + 4, g0 + 2, (base + 4) % RING, 0, True, False)
                first, loops = base + 5, (pairs - 3) // 2
                with pe.Fori(0, loops) as i:
                    for b in range(2):
                        s = first + 3 * b
                        c, j = i * 6 + s, i * 4 + (g0 + 4 + 2 * b)
                        step_in(c, j, s % RING, 0)
                        step_in(c + 1, j + 1, (s + 1) % RING, 1)
                        step_out(c + 2, j, (s + 2) % RING, (1 + b) % 2, False, False)
                c, j = first + 6 * loops, g0 + 4 + 4 * loops
                step_in(c, j, c % RING, 0)
                step_in(c + 1, j + 1, (c + 1) % RING, 1)
                step_out(c + 2, j, (c + 2) % RING, (pairs - 2) % 2, False, False)
                step_out(c + 3, j + 2, (c + 3) % RING, (pairs - 1) % 2, False, True)
                at[0] = c + 4
                hidden[0] += FF_TILES

            def mlp():
                base, s0 = at[0], hidden[0]
                banks = [mid[:, jobs[0] % 2, :], mid[:, 1 - jobs[0] % 2, :], aux[:, 0, :]]

                def step_in(c, j, slot, r, wait=True):
                    pe.wait_ge(lo_ready, c + 1)
                    if wait:
                        pe.wait_ge(act_ready, j - 2)
                    for m in range(2):
                        mm = f_tile(banks[r][:, m * T:(m + 1) * T], slot, KT, 2 * P, m * P)
                    mm.then_inc(chunk_used, 1)

                def step_out(c, j, slot, r, start, stop):
                    pe.wait_ge(lo_ready, c + 1)
                    pe.wait_ge(glo_ready, j + 1)
                    t_chunk(slot, g_pair(r), 2, D, 2, start, stop)

                acc_free()
                step_in(base, s0, base % RING, 0, False)
                for j in range(1, 4):
                    c = base + 2 * j - 1
                    step_in(c, s0 + j, c % RING, j % 3, j >= 3)
                    step_out(c + 1, s0 + j - 1, (c + 1) % RING, (j - 1) % 3, j == 1, False)
                loops = (MLP_STEPS - 4) // 3
                with pe.Fori(0, loops) as i:
                    for b in range(3):
                        s = base + 7 + 2 * b
                        c = i * 6 + s
                        step_in(c, i * 3 + (s0 + 4 + b), s % RING, (4 + b) % 3)
                        step_out(c + 1, i * 3 + (s0 + 3 + b), (s + 1) % RING, (3 + b) % 3, False, False)
                c = base + MLP_CHUNKS - 1
                step_out(c, s0 + MLP_STEPS - 1, c % RING, (MLP_STEPS - 1) % 3, False, True)
                at[0] = c + 1
                hidden[0] += MLP_STEPS

            def attention(n_units, dv, scores, values, full=False, maps=1, beside=None):
                def score(u):
                    for m in range(maps):
                        scores(u, m, mid_bank()).then_inc(*sent.one(mid_full))

                def turn_probs(u):
                    if maps == 1:
                        pe.wait_ge(exp_ready, scored[0] + 1)
                        src = P_[:, scored[0] % 4, :]
                    else:
                        pe.wait_ge(pc_ready, due(pc_ready))
                        src = PC_[:, u % 2, :]
                    scored[0] += maps
                    n = sent.total(turned_full)
                    if n >= 2:
                        pe.wait_ge(turned_done, n - 1)
                    for b in range(4 if full else 3):
                        mm = pe.transpose(aux[:, n % 2, b * P:(b + 1) * P], src[:, b * P:(b + 1) * P], ident[:])
                    mm.then_inc(*sent.one(turned_full))

                def weigh(u):
                    n = sent.total(o_full)
                    pe.wait_ge(turned_done, n + 1)
                    if n >= 2:
                        pe.wait_ge(o_done, n - 1)
                    bank = acc[:, 2 + n % 2, :]
                    parts = (((0, 0), (1, 1)), ((2, 0), (3, 1))) if full else (((0, 0),), ((1, 0), (2, 1)))
                    for qt in range(TT):
                        for i, (b, kt) in enumerate(parts[qt]):
                            mm = pe.matmul(bank[:, qt * dv:(qt + 1) * dv], PT_[:, n % 2, b * P:(b + 1) * P],
                                           values(u, kt), start=i == 0, stop=i == len(parts[qt]) - 1)
                    mm.then_inc(*sent.one(o_full))

                score(0)
                for u in range(n_units):
                    if u + 1 < n_units:
                        score(u + 1)
                    turn_probs(u)
                    if u >= 1:
                        weigh(u - 1)
                    if beside:
                        beside(u)
                weigh(n_units - 1)

            def head_scores(bank, q, k):
                for qt in range(TT):
                    a, n = SEG[qt]
                    mm = pe.matmul(bank[:, a:a + n], q[:, qt * P:(qt + 1) * P], k[:, 0:n], start=True, stop=True)
                return mm

            def compressed_steps():
                used = [0]

                def bank_():
                    n = used[0]
                    used[0] += 1
                    if n >= 2:
                        pe.wait_ge(cmp_done, n - 1)
                    return acc[:, n % 2, :]

                def first_layer(v):
                    pe.wait_ge(blklo_ready, v + 1)
                    bank = bank_()
                    for half in range(2):
                        c = at[0]
                        pe.wait_ge(lo_ready, c + 1)
                        for j in range(8):
                            jj = half * 8 + j
                            lhs = [b[:, jj * CCOLS:jj * CCOLS + P] for b in (blk_hi, blk_lo)]
                            mm = three(bank[:, 0:T], lhs, w_pair(c % RING, j * T, T), jj == 0, jj == JJ - 1)
                        mm.then_inc(chunk_used, 1)
                        at[0] += 1

                def turn_hidden(v):
                    pe.wait_ge(cmp_done, 2 * v + 1)
                    bank = bank_()
                    for m in range(2):
                        mm = pe.transpose(bank[:, m * CCOLS:(m + 1) * CCOLS], pre[0:CCOLS, m * P:(m + 1) * P],
                                          ident[0:CCOLS, 0:CCOLS])
                    mm.then_inc(cmp_full, 1)

                def second_layer():
                    pe.wait_ge(gelu_ready, 1)
                    bank = bank_()
                    for m in range(2):
                        mm = pe.matmul(bank[:, 0:CCOLS], w2k[:, m, :], hidg[:, 0, m, :], start=m == 0, stop=m == 1)
                    mm.then_inc(cmp_full, 1)
                    pe.wait_ge(hidd_ready, 1)
                    bank = bank_()
                    for g in range(2):
                        for m in range(2):
                            mm = pe.matmul(bank[:, g * DH:(g + 1) * DH],
                                           hidd_flat[:, (2 * m + g) * P:(2 * m + g + 1) * P],
                                           w2v[:, m, :], start=m == 0, stop=m == 1)
                    mm.then_inc(cmp_full, 1)

                def block_scores():
                    pe.wait_ge(cmp_done, 6)
                    for g in range(2):
                        bank = bank_()
                        for qt in range(TT):
                            for r in range(4):
                                a = (qt * 4 + r) * 16
                                mm = pe.matmul(bank[:, a:a + CBLK], proj[grp(g), QA + r, qt * P:(qt + 1) * P],
                                               kcT[grp(g), g * CBLK:(g + 1) * CBLK], start=True, stop=True)
                        mm.then_inc(cmp_full, 1)

                def turn_blocks():
                    pe.wait_ge(cp_ready, 1)
                    bank = bank_()
                    for a in range(4):
                        mm = pe.transpose(bank[:, a * P:(a + 1) * P], cp_flat[:, a * P:(a + 1) * P], ident[:])
                    mm.then_inc(cpt_full, 1)

                def block_outputs():
                    pe.wait_ge(cmp_done, 8)
                    pe.wait_ge(cpt_done, 1)
                    for qt in range(TT):
                        for g in range(2):
                            mm = pe.matmul(acc[:, 1 - qt, g * T:(g + 1) * T], cpT[:, g * 2 + qt, :],
                                           vcd[:, g, :, :], start=True, stop=True)
                        mm.then_inc(co_full, 1)

                return [lambda: first_layer(0), lambda: turn_hidden(0), lambda: first_layer(1),
                        lambda: turn_hidden(1), second_layer, block_scores, turn_blocks, block_outputs]

            def stick_breaking():
                side = [mid[:, 1, :], aux[:, 1, :]]

                def z_scores(p):
                    if p >= 2:
                        pe.wait_ge(m_ready, p - 1)
                    b = 2 * (p % 2)
                    for i, hd in enumerate(sb_heads(p)):
                        q, k = proj[grp(hd % 2), hd // 2, :], proj[grp(hd % 2), 8 + hd // 2, :]
                        pe.matmul(acc[:, b, i * T:(i + 1) * T], k[:, 0:P], q, start=True, stop=True)
                        mm = pe.matmul(acc[:, b + 1, i * P:(i + 1) * P], k[:, P:T], q[:, P:T], start=True, stop=True)
                    mm.then_inc(z_full, 1)

                def later_sums(p):
                    pe.wait_ge(sp_ready, p + 1)
                    if p >= 1:
                        pe.wait_ge(zs_ready, p)
                    sp = sb_l[:, p % 2, :]
                    for i in range(2):
                        s = mid[:, 0, i * T:(i + 1) * T]
                        sp0, sp1 = sp[:, i * T:(i + 1) * T], sp[:, 2 * T + i * P:2 * T + (i + 1) * P]
                        pe.matmul(s[:, 0:P], tri[:], sp0[:, 0:P], start=True, stop=True)
                        pe.matmul(s[:, P:T], tri[:], sp0[:, P:T], start=True, stop=False)
                        pe.matmul(s[:, P:T], ones[:], sp1, start=False, stop=True)
                        mm = pe.matmul(aux[:, 0, i * P:(i + 1) * P], tri[:], sp1, start=True, stop=True)
                    mm.then_inc(s_full, 1)

                def outputs(p):
                    pe.wait_ge(a_ready, p + 1)
                    if p >= 1:
                        pe.wait_ge(so_done, p)
                    a = sb_a[:, p % 2, :]
                    for i, hd in enumerate(sb_heads(p)):
                        v = slice(hd * DH, (hd + 1) * DH)
                        for qt in range(TT):
                            o = aux[:, 0, T + qt * P + i * DH:T + qt * P + (i + 1) * DH]
                            mm = pe.matmul(o, a[:, i * T + qt * P:i * T + (qt + 1) * P], vtok[:, 0, v],
                                           start=True, stop=qt == 0)
                            if qt:
                                mm = pe.matmul(o, a[:, 2 * T + i * P:2 * T + (i + 1) * P], vtok[:, 1, v],
                                               start=False, stop=True)
                    mm.then_inc(so_full, 1)

                def memory(p):
                    c = at[0]
                    pe.wait_ge(lo_ready, c + 1)
                    if p < 4:
                        if p >= 2:
                            pe.wait_ge(side_done, p - 1)
                        for m in range(2):
                            mm = f_tile(side[p % 2][:, m * T:(m + 1) * T], c % RING, KT, 2 * P, m * P)
                    else:
                        if p % 2 == 0:
                            pe.wait_ge(side_done, 4 + (p - 4))
                        for t in range(TT):
                            for k in range(4):
                                mm = three(side[t], xT_pair(p % 2 * 4 + k, t), w_pair(c % RING, k * 512, 512),
                                           p % 2 == 0 and k == 0, p % 2 == 1 and k == 3)
                    mm.then_inc(chunk_used, 1)
                    at[0] += 1

                z_scores(0)
                z_scores(1)
                for p in range(8):
                    memory(p)
                    later_sums(p)
                    if p + 2 < 8:
                        z_scores(p + 2)
                    if p >= 1:
                        outputs(p - 1)
                outputs(7)
                pe.wait_ge(side_done, 8)

            def projected():
                pe.wait_ge(mid_done, jobs[0])
                pe.wait_ge(acc_done, due.total(acc_done))

            def half_values(u):
                if u % 2 == 0:
                    acc_free()
                c = at[0]
                pe.wait_ge(lo_ready, c + 1)
                t_chunk(c % RING, lambda k, t: xT_pair(u % 2 * 4 + k, t), 4, 512, 1, u % 2 == 0, u % 2 == 1)
                at[0] += 1

            def cross():
                turn(xn, normed)
                f_chunks(4)
                projected()

                def scores(u, m, bank):
                    for qt in range(TT):
                        for i in range(2):
                            mm = pe.matmul(bank[:, qt * T:(qt + 1) * T], proj[:, 2 * u + i, qt * P:(qt + 1) * P],
                                           memkT[:, 2 * u + i, :], start=i == 0, stop=i == 1)
                    return mm

                attention(4, T, scores, lambda u, kt: memv[:, kt, u * T:(u + 1) * T], full=True)
                turn(obuf, heads_out)
                t_chunks(D)

            def mixer():
                turn(xn, normed)
                f_chunks(MIX_F)
                t_chunks(MIXV_W)
                projected()
                steps = compressed_steps()
                attention(8, DH, lambda u, m, bank: head_scores(
                    bank, proj[:, QB + u % 4, :], mix_keys(u // 4, 2)),
                    lambda u, kt: vtok[:, kt, VB_COL + DH * (u // 4):][:, 0:DH], beside=lambda u: steps[u]())
                attention(16, DH, lambda u, m, bank: head_scores(
                    bank, proj[:, QA + u // 2 % 4, :], mix_keys(u // 8, u % 2)),
                    lambda u, kt: vtok[:, kt, VS_COL + P * (u % 2) + DH * (u // 8):][:, 0:DH])
                turn(obuf, heads_out)
                pe.wait_ge(co_done, TT)
                t_chunks(D)

            def even_mixer():
                turn(xn, normed)
                f_chunks(EV_F)
                t_chunks(CQ_W)
                t_chunks(512)
                turn(xn, normed, CQ_W // P)
                c = at[0]
                pe.wait_ge(lo_ready, c + 1)
                for pair in range(4):
                    bank = mid_bank()
                    for m in range(2):
                        mm = f_tile(bank[:, m * T:(m + 1) * T], c % RING, 2, D, (2 * pair + m) * P)
                    mm.then_inc(*(sent.one(mid_full) if pair < 3 else (chunk_used, 1)))
                c += 1
                pe.wait_ge(lo_ready, c + 1)
                for pair in range(2):
                    bank = mid_bank()
                    for m in range(2):
                        mm = three(bank[:, m * T:(m + 1) * T], w_pair(c % RING, (2 * pair + m) * P, P),
                                   (xT_hi[:, 2, :], xT_lo[:, 2, :]), True, True)
                    mm.then_inc(*sent.one(mid_full))
                acc_free()
                for t in range(TT):
                    mm = three(acc[:, t, :], xT_pair(2, t), w_pair(c % RING, 512, 512), True, True)
                    mm.then_inc(*((acc_full, 1) if t == 0 else (chunk_used, 1)))
                at[0] = c + 1
                turn(xn, normed)
                projected()
                attention(4, P, lambda u, m, bank: head_scores(
                    bank, proj[:, u, :], diff_pad[u] if m else proj[:, 4 + u, :]),
                    lambda u, kt: vtok[:, kt, u * P:(u + 1) * P], maps=2, beside=lambda u: f_chunks(1))
                pe.wait_ge(rope_ready, 1)

                def scores(u, m, bank):
                    turned_keys = rope_pad if u % 2 else proj[:, 8, :]
                    for qt in range(TT):
                        a, n = SEG[qt]
                        pe.matmul(bank[:, a:a + n], proj[:, 10 + u, qt * P:(qt + 1) * P], knope[u][:, 0:n],
                                  start=True, stop=False)
                        mm = pe.matmul(bank[:, a:a + n], proj[:, 14 + u // 2, qt * P:(qt + 1) * P],
                                       turned_keys[:, 0:n], start=False, stop=True)
                    return mm

                attention(4, P, scores, lambda u, kt: vtok[:, kt, 512 + u * P:512 + (u + 1) * P],
                          beside=lambda u: half_values(u))
                pe.wait_ge(dnorm_ready, 1)
                turn(obuf, heads_out)
                t_chunks(D)

            def odd_mixer():
                turn(xn, normed)
                f_chunks(8)
                t_chunks(D)
                turn(xn, normed)
                projected()
                stick_breaking()
                turn(obuf, lambda t, a: pe.wait_ge(so_done, 8))
                t_chunks(D)

            pe.wait_ge(ident_full, 16)
            turn(xn, normed)
            ffn()
            pe.wait_ge(const_full, 16 * n_const)
            mixer()
            turn(xn, normed)
            ffn()
            even_mixer()
            cross()
            turn(xn, normed)
            mlp()
            odd_mixer()
            cross()
            turn(xn, normed)
            mlp()

        @block.vector
        def _(dve):
            sent, due = Tally(), Tally()
            at = [0]
            jobs = [0]
            hidden = [0]
            norms = [0]
            tiles = [0]
            owed = []
            scored = [0]

            def own(ins):
                ins.then_inc(*sent.one(dve_own))
                dve.wait_ge(dve_own, sent.total(dve_own))

            def split(c, slot):
                dve.wait_ge(hi_ready, c + 1)
                dve.tensor_tensor(w_lo[:, slot, :], raw[:, slot, :], w_hi[:, slot, :],
                                  ALU.subtract).then_inc(lo_ready, 1)

            def ahead(n=1):
                for _ in range(n):
                    c = at[0] + AHEAD
                    if c < N_CHUNKS:
                        split(c, c % RING)
                    at[0] += 1

            def job(signalled=True):
                m = jobs[0]
                jobs[0] += 1
                if signalled:
                    dve.wait_ge(mid_full, due(mid_full))
                else:
                    dve.wait_ge(chunk_used, at[0])
                return mid[:, m % 2, :]

            def gained():
                k = norms[0]
                norms[0] += 1
                dve.wait_ge(gain_full[k % 2], 16 * (k // 2 + 1))
                return gain[:, k % 2, :]

            def norm(src):
                g = gained()
                for t in range(TT):
                    dve.wait_ge(rstd_ready, due(rstd_ready))
                    for c in (slice(0, D // 2), slice(D // 2, D)):
                        dve.scalar_tensor_tensor(xn[:, t, c], src[:, t, c], rstd[:, t:t + 1], g[:, c],
                                                 ALU.mult, ALU.mult).then_inc(*sent.one(xn_ready))

            def final_norm():
                g = gained()
                for t in range(TT):
                    dve.wait_ge(rstd_ready, due(rstd_ready))
                    dve.scalar_tensor_tensor(h[:, t, :], h[:, t, :], rstd[:, t:t + 1], g,
                                             ALU.mult, ALU.mult).then_inc(*sent.one(h_ready))
                last_h[:] = [h_ready, sent.total(h_ready)]

            def turned(tiles_=KT, per_bank=4):
                for t in range(TT):
                    for a in range(0, tiles_, per_bank):
                        n = min(per_bank, tiles_ - a)
                        bank = job()
                        dve.wait_ge(thi_ready, due(thi_ready))
                        dve.tensor_tensor(xT_lo[:, a:a + n, t * P:(t + 1) * P],
                                          bank[:, 0:n * P].rearrange("p (k q) -> p k q", q=P),
                                          xT_hi[:, a:a + n, t * P:(t + 1) * P],
                                          ALU.subtract).then_inc(mid_done, 1)
                while owed:
                    c = owed.pop()
                    split(c, c % RING)

            def f_chunks(n, dst, first=0):
                for i in range(n):
                    a = first + 2 * i
                    ahead()
                    bank = job(False)
                    dve.tensor_copy(dst[:, a:a + 2, :],
                                    bank.rearrange("p (k q) -> p k q", q=T)).then_inc(mid_done, 1)

            def zero_halves(tile, pads):
                for i, pad in enumerate(pads):
                    dve.memset(proj[grp(1), tile + i, :], 0.0)
                    dve.memset(pad[grp(0), :], 0.0)

            def apart(src, tile, pad):
                dve.tensor_copy(proj[grp(0), tile, :], src[grp(0), :])
                return dve.tensor_copy(pad[grp(1), :], src[grp(1), :])

            def acc_tile(t):
                if t == 0:
                    dve.wait_ge(acc_full, due(acc_full))
                else:
                    dve.wait_ge(chunk_used, at[0])

            def t_values(dst, width, chunks):
                ahead(chunks)
                for t in range(TT):
                    acc_tile(t)
                    if width == D:
                        o, src = dst[:, t, :].rearrange("p (a b) -> p a b", a=2), acc[:, 2 * t:2 * t + 2, :]
                    else:
                        o, src = dst[:, t, 0:width], acc[:, t, 0:width]
                    dve.tensor_copy(o, src).then_inc(*sent.one(acc_done))

            def residual(scale, chunks):
                ahead(chunks - 1)
                if at[0] + AHEAD < N_CHUNKS:
                    owed.append(at[0] + AHEAD)
                at[0] += 1
                for t in range(TT):
                    acc_tile(t)
                    ht = h[:, t, :].rearrange("p (a b) -> p a b", a=2)
                    dve.scalar_tensor_tensor(ht, acc[:, 2 * t:2 * t + 2, :], scale, ht, ALU.mult,
                                             ALU.add).then_inc(*sent.one(acc_done))

            def ffn():
                base, g0 = at[0], hidden[0]

                def step_in(c, j, slot, r, g):
                    split(c + AHEAD, slot)
                    dve.wait_ge(act_ready, j + 1)
                    dve.tensor_tensor(ff_g[:, r, 0:T], ff_s[:, r, 0:T], mid[:, r, T:2 * T],
                                      ALU.mult).then_inc(g_ready, 1)
                    dve.wait_ge(ghi_ready, j + 1)
                    dve.tensor_tensor(g_lo[:, g, :], ff_g[:, r, 0:T], g_hi[:, g, :],
                                      ALU.subtract).then_inc(glo_ready, 1)

                for j in range(4):
                    step_in(base + j, g0 + j, (base + j + AHEAD) % RING, j % 2, j % 4)
                split(base + 4 + AHEAD, (base + 4 + AHEAD) % RING)
                first, loops = base + 5, (FF_TILES // 2 - 3) // 2
                with dve.Fori(0, loops) as i:
                    for b in range(2):
                        s = first + 3 * b
                        for n in range(2):
                            step_in(i * 6 + (s + n), i * 4 + (g0 + 4 + 2 * b + n), (s + n + AHEAD) % RING, n,
                                    2 * b + n)
                        split(i * 6 + (s + 2 + AHEAD), (s + 2 + AHEAD) % RING)
                c, j = first + 6 * loops, 4 + 4 * loops
                for n in range(2):
                    step_in(c + n, g0 + j + n, (c + n + AHEAD) % RING, n, (j + n) % 4)
                hidden[0] += FF_TILES
                at[0] = c + 2
                residual(0.5, 2)

            def mlp():
                base, s0 = at[0], hidden[0]

                def step_in(c, j, slot, r):
                    if slot is not None:
                        split(c + AHEAD, slot)
                    dve.wait_ge(act_ready, j + 1)
                    dve.tensor_tensor(ff_g[:, r, :], ff_s[:, r, :], ff_s[:, r, :], ALU.mult).then_inc(g_ready, 1)
                    dve.wait_ge(ghi_ready, j + 1)
                    dve.wait_ge(g_ready, j + 1)
                    dve.tensor_tensor(g_lo[:, 2 * r:2 * r + 2, :], ff_g[:, r, :].rearrange(
                        "p (k q) -> p k q", k=2), g_hi[:, 2 * r:2 * r + 2, :], ALU.subtract).then_inc(glo_ready, 1)

                def steps(j):
                    c = base + 2 * j - 1
                    step_in(c, s0 + j, (c + AHEAD) % RING if c + AHEAD < N_CHUNKS else None, j % 3)
                    if c + 1 + AHEAD < N_CHUNKS:
                        split(c + 1 + AHEAD, (c + 1 + AHEAD) % RING)

                step_in(base, s0, (base + AHEAD) % RING, 0)
                for j in range(1, 4):
                    steps(j)
                loops = (MLP_STEPS - 4) // 3
                if base + MLP_CHUNKS == N_CHUNKS:
                    loops -= 1
                with dve.Fori(0, loops) as i:
                    for b in range(3):
                        s = base + 7 + 2 * b
                        step_in(i * 6 + s, i * 3 + (s0 + 4 + b), (s + AHEAD) % RING, (4 + b) % 3)
                        split(i * 6 + (s + 1 + AHEAD), (s + 1 + AHEAD) % RING)
                for j in range(4 + 3 * loops, MLP_STEPS):
                    steps(j)
                hidden[0] += MLP_STEPS
                at[0] = base + MLP_CHUNKS - 1
                residual(1.0, 1)

            def attention(n_units, scale, finish, combine=None, tile_of=None, full=False, maps=1, sink=False,
                          beside=None):
                segs = [(0, T), (T, T)] if full else SEG
                base, e0 = tiles[0], scored[0]
                seen = [-1]

                def unit(u):
                    k = None
                    if tile_of is not None:
                        k = base + tile_of(u)
                        if k != seen[0]:
                            dve.wait_ge(bias_full[k % BIAS_SLOTS], 16 * (k // BIAS_SLOTS + 1))
                            seen[0] = k
                    for _ in range(maps):
                        e = scored[0]
                        scored[0] += 1
                        bank = job()
                        if e >= 2:
                            dve.wait_ge(exp_ready, e - 1)
                        for qt in range(TT):
                            a, n = segs[qt]
                            b = zero[:].to_broadcast([P, n]) if k is None else bias[:, k % BIAS_SLOTS, a:a + n]
                            ins = dve.tensor_tensor_reduce(N_[:, e % 2, a:a + n], bank[:, a:a + n], b, -scale,
                                                           -NEG, ALU.add, ALU.min, nmax[:, e % 4, qt:qt + 1])
                        if sink:
                            own(ins)
                            ins = dve.tensor_scalar(nmax[:, e % 4, 0:2], nmax[:, e % 4, 0:2],
                                                    nsink[:, u:u + 1], None, ALU.min)
                        ins.then_inc(mid_done, 1)
                    if k is not None:
                        while len(bias_used_at) <= k:
                            bias_used_at.append(0)
                        bias_used_at[k] = jobs[0]

                def output(u):
                    s = (e0 + u * maps) % 4
                    if maps == 1:
                        dve.wait_ge(exp_ready, e0 + u + 1)
                        if sink:
                            own(dve.tensor_tensor(rsum[:, s, 0:2], rsum[:, s, 0:2], esink[:, s, :], ALU.add))
                        own(dve.reciprocal(rinv[:, s, 0:2], rsum[:, s, 0:2]))
                    n = sent.total(o_done)
                    dve.wait_ge(o_full, n + 1)
                    finish(u, acc[:, 2 + n % 2, :], rinv[:, s, :]).then_inc(*sent.one(o_done))

                unit(0)
                for u in range(n_units):
                    if u + 1 < n_units:
                        unit(u + 1)
                    if combine is not None:
                        combine(u, e0)
                    if u >= 1:
                        output(u - 1)
                    if beside:
                        beside(u)
                output(n_units - 1)
                if tile_of is not None:
                    tiles[0] = base + tile_of(n_units - 1) + 1

            def plain_out(base, w):
                def finish(u, bank, inv):
                    for qt in range(TT):
                        ins = dve.tensor_scalar(obuf[:, qt, base + u * w:base + (u + 1) * w],
                                                bank[:, qt * w:(qt + 1) * w], inv[:, qt:qt + 1], None, ALU.mult)
                    return ins
                return finish

            def nsa_out(u, bank, inv):
                hd, branch = u // 2, u % 2
                own(dve.tensor_tensor(inv[:, 0:2], inv[:, 0:2], gate[:, :, hd * 3 + 1 + branch], ALU.mult))
                if branch:
                    dve.wait_ge(o_done, sent.total(o_done))
                for qt in range(TT):
                    o = obuf[:, qt, hd * DH:(hd + 1) * DH]
                    ins = dve.scalar_tensor_tensor(o, bank[:, qt * DH:(qt + 1) * DH], inv[:, qt:qt + 1], o,
                                                   ALU.mult, ALU.add)
                return ins

            def diff_combine(u, e0):
                e = e0 + 2 * u
                dve.wait_ge(exp_ready, e + 2)
                a, b = e % 4, (e + 1) % 4
                dve.reciprocal(rinv[:, a, 0:2], rsum[:, a, 0:2])
                own(dve.reciprocal(rinv[:, b, 0:2], rsum[:, b, 0:2]))
                own(dve.tensor_scalar(rinv[:, b, 0:2], rinv[:, b, 0:2], lam[:, 3:4], None, ALU.mult))
                for qt in range(TT):
                    c, n = SEG[qt]
                    ins = dve.tensor_scalar(P_[:, b, c:c + n], P_[:, b, c:c + n], rinv[:, b, qt:qt + 1], None,
                                            ALU.mult)
                own(ins)
                if u >= 2:
                    dve.wait_ge(turned_full, sent.total(o_done) + 1)
                for qt in range(TT):
                    c, n = SEG[qt]
                    ins = dve.scalar_tensor_tensor(PC_[:, u % 2, c:c + n], P_[:, a, c:c + n],
                                                   rinv[:, a, qt:qt + 1], P_[:, b, c:c + n], ALU.mult, ALU.add)
                ins.then_inc(pc_ready, 1)

            def diff_out(u, bank, inv):
                for qt in range(TT):
                    ins = dve.tensor_copy(obuf[:, qt, u * P:(u + 1) * P], bank[:, qt * P:(qt + 1) * P])
                return ins

            def blocks(v):
                if v:
                    dve.wait_ge(blkhi_ready, v)
                for g in range(2):
                    for par in range(2):
                        rows = grp(par)
                        src = proj[rows, KC + 2 * v + g, :].rearrange("p (c b) -> p b c", b=16)
                        bl = blk[rows, :].rearrange("p (j c) -> p j c", j=JJ)
                        for nx in range(2):
                            ins = dve.tensor_tensor(
                                bl[:, nx * 8:nx * 8 + 8, g * CBLK:(g + 1) * CBLK],
                                src[:, par:16:2, nx:nx + CBLK],
                                posT[rows, v, nx * 8:nx * 8 + 8].unsqueeze(2).to_broadcast([DH, 8, CBLK]),
                                ALU.add)
                ins.then_inc(blk_ready, 1)

            def blocks_lo(v):
                dve.wait_ge(blkhi_ready, v + 1)
                dve.tensor_tensor(blk_lo[:, 0:JJ * CCOLS], blk, blk_hi[:, 0:JJ * CCOLS],
                                  ALU.subtract).then_inc(blklo_ready, 1)

            def compressed_steps():
                used = [0]

                def bank_():
                    used[0] += 1
                    return acc[:, (used[0] - 1) % 2, :]

                def first_layer(v):
                    ahead(2)
                    dve.wait_ge(chunk_used, at[0])
                    dve.tensor_copy(pre[0:CCOLS, :], bank_()[0:CCOLS, 0:T]).then_inc(cmp_done, 1)
                    if v == 0:
                        blocks(1)

                def add_bias(v):
                    if v == 0:
                        blocks_lo(1)
                    dve.wait_ge(cmp_full, v + 1)
                    bank = bank_()
                    for k in range(2):
                        ins = dve.tensor_scalar(hid[:, v, k, :], bank[:, k * CCOLS:(k + 1) * CCOLS],
                                                b1T[:, v, k:k + 1], None, ALU.add)
                    ins.then_inc(cmp_done, 1)

                def second_layer():
                    dve.wait_ge(gelu_ready, 1)
                    for k in range(2):
                        for g in range(2):
                            ins = dve.tensor_copy(hidd[:, k, g, :, 0:CBLK], hidg[:, 1, k, g * CBLK:(g + 1) * CBLK]
                                                  .unsqueeze(1).to_broadcast([P, 4, CBLK]))
                    ins.then_inc(hidd_ready, 1)
                    dve.wait_ge(cmp_full, 3)
                    dve.tensor_copy(kcT, bank_()[:, 0:CCOLS]).then_inc(cmp_done, 1)
                    dve.wait_ge(cmp_full, 4)
                    bank = bank_()
                    for g in range(2):
                        for r in range(4):
                            rows = slice(32 * r, 32 * r + 32)
                            ins = dve.tensor_copy(vcd[rows, g, r, :], bank[rows, g * DH:(g + 1) * DH])
                    ins.then_inc(cmp_done, 1)

                def less_maximum():
                    for g in range(2):
                        dve.wait_ge(cmp_full, 5 + g)
                        sc = bank_()[:, 0:128].rearrange("p (a c) -> p a c", a=8)[:, :, 0:CBLK]
                        dve.scalar_tensor_tensor(cs[:, 8 * g:8 * g + 8, :], sc, ATTN_SCALE,
                                                 cbias[:, 8 * g:8 * g + 8, :], ALU.mult, ALU.add).then_inc(cmp_done, 1)
                    dve.wait_ge(cmp_done, 8)
                    own(dve.tensor_reduce(cst[:, 0, :], cs, AX.X, ALU.max))
                    dve.tensor_tensor(cs, cs, cst[:, 0, :].unsqueeze(2).to_broadcast([P, 16, CBLK]),
                                      ALU.subtract).then_inc(cs_ready, 1)

                def probabilities():
                    dve.wait_ge(ce_ready, 1)
                    own(dve.tensor_reduce(cst[:, 1, :], ce, AX.X, ALU.add))
                    own(dve.reciprocal(cst[:, 2, :], cst[:, 1, :]))
                    for g in range(2):
                        for qt in range(TT):
                            a = (g * 2 + qt) * 4
                            dve.tensor_tensor(cst[:, 2, a:a + 4], cst[:, 2, a:a + 4],
                                              gate[:, qt, 12 * g:12 * g + 12:3], ALU.mult)
                    own(dve.tensor_tensor(ce, ce, cmask, ALU.mult))
                    dve.tensor_tensor(cp[:, :, 0:CBLK], ce, cst[:, 2, :].unsqueeze(2).to_broadcast([P, 16, CBLK]),
                                      ALU.mult).then_inc(cp_ready, 1)

                def block_outputs():
                    for qt in range(TT):
                        dve.wait_ge(co_full, qt + 1)
                        dve.tensor_copy(obuf[:, qt, 0:512], acc[:, 1 - qt, :]).then_inc(*sent.one(co_done))
                    dve.wait_ge(co_done, TT)

                return [lambda: first_layer(0), lambda: add_bias(0), lambda: first_layer(1),
                        lambda: add_bias(1), second_layer, less_maximum, probabilities, block_outputs]

            def mixer():
                dve.wait_ge(const_full, 16 * n_const)
                dve.tensor_scalar(nsink[:], sinkt[:], -1.0, None, ALU.mult)
                dve.tensor_scalar(subg[:], subg[:], 1.0 - LAMBDA_INIT, None, ALU.mult)
                for i in range(2):
                    ins = dve.tensor_tensor_reduce(lamv[:, 2 * i, :], lamv[:, 2 * i, :], lamv[:, 2 * i + 1, :], 1.0,
                                                   0.0, ALU.mult, ALU.add, lam[:, i:i + 1])
                ins.then_inc(lam_dots, 1)
                norm(h)
                turned()
                f_chunks(2, proj)
                ahead()
                bank = job(False)
                zero_halves(KS, mix_pad)
                apart(bank[:, 0:T], KS, mix_pad[0])
                apart(bank[:, T:2 * T], KW, mix_pad[1]).then_inc(mid_done, 1)
                ahead()
                bank = job(False)
                apart(bank[:, 0:T], KB, mix_pad[2])
                dve.tensor_copy(proj[:, QA, :], bank[:, T:2 * T]).then_inc(mid_done, 1)
                f_chunks(MIX_F - 4, proj, 8)
                dve.wait_ge(mid_done, jobs[0])
                blocks(0)
                dve.memset(blk_hi[:, JJ * CCOLS:JJ * CCOLS + P].bitcast(F32), 0.0)
                dve.memset(blk_lo[:, JJ * CCOLS:JJ * CCOLS + P].bitcast(F32), 0.0)
                blocks_lo(0)
                dve.memset(vcd, 0.0)
                dve.memset(hidd_flat, 0.0)
                dve.memset(cp_flat, 0.0)
                t_values(vtok, MIXV_W, MIX_V)
                dve.wait_ge(lam_exps, 1)
                own(dve.tensor_tensor(lam[:, 2:3], lam[:, 0:1], lam[:, 1:2], ALU.subtract))
                own(dve.tensor_scalar(lam[:, 3:4], lam[:, 2:3], LAMBDA_INIT, -1.0, ALU.add, ALU.mult))
                dve.wait_ge(gexp_ready, 1)
                own(dve.tensor_scalar(gate[:], gate[:], 1.0, None, ALU.add))
                own(dve.reciprocal(gate[:], gate[:]))
                steps = compressed_steps()
                attention(8, ATTN_SCALE, plain_out(512, DH), tile_of=lambda u: u, sink=True,
                          beside=lambda u: steps[u]())
                attention(16, ATTN_SCALE, nsa_out, tile_of=lambda u: u // 2)
                turned()
                obuf_turned_at.append(jobs[0])
                residual(1.0, MIX_O)

            def even_mixer():
                norm(h)
                turned()
                f_chunks(2, proj)
                zero_halves(4, diff_pad)
                for i in range(2):
                    ahead()
                    bank = job(False)
                    for m in range(2):
                        ins = apart(bank[:, m * T:(m + 1) * T], 4 + 2 * i + m, diff_pad[2 * i + m])
                    ins.then_inc(mid_done, 1)
                f_chunks(1, proj, 8)
                t_values(cqs, CQ_W, 2)
                for t in range(TT):
                    dve.wait_ge(rstd_ready, due(rstd_ready))
                    for i, (a, n) in enumerate(((0, 2 * P), (2 * P, P))):
                        ins = dve.scalar_tensor_tensor(xn[:, t, a:a + n], cqs[:, t, a:a + n],
                                                       rstd[:, 2 * t + i:2 * t + i + 1], cqg[:, a:a + n],
                                                       ALU.mult, ALU.mult)
                    ins.then_inc(*sent.one(xn_ready))
                t_values(vtok, 512, 2)
                turned(CQ_W // P)
                for pair in range(4):
                    if pair == 3:
                        ahead()
                    bank = job(pair < 3)
                    dst = proj[:, 10 + 2 * pair:12 + 2 * pair, :] if pair < 2 else rot[:, 2 * pair - 4:2 * pair - 2, :]
                    dve.tensor_copy(dst, bank.rearrange("p (k q) -> p k q", q=T)).then_inc(mid_done, 1)
                for pair in range(2):
                    bank = job()
                    dve.tensor_copy(memv[:, pair, 512:1024], bank).then_inc(mid_done, 1)
                t_values(vtok[:, :, 512:1024], 512, 1)
                norm(obuf)
                dve.wait_ge(mid_done, jobs[0])
                cos, sin = ropet[:, 0, :], ropet[:, 1, :]
                for a in (rot[:, 0, :], rot[:, 1, :], proj[:, 8, :]):
                    dve.tensor_tensor(a, a, cos, ALU.mult)
                for b in (rot[:, 2, :], rot[:, 3, :], proj[:, 9, :]):
                    ins = dve.tensor_tensor(b, b, sin, ALU.mult)
                own(ins)
                dve.tensor_tensor(proj[:, 14, :], rot[:, 0, :], rot[:, 2, :], ALU.add)
                dve.tensor_tensor(proj[:, 15, :], rot[:, 1, :], rot[:, 3, :], ALU.add)
                dve.tensor_tensor(rope_pad[grp(1), :], proj[grp(1), 8, :], proj[grp(1), 9, :], ALU.add)
                own(dve.tensor_tensor(proj[grp(0), 8, :], proj[grp(0), 8, :], proj[grp(0), 9, :], ALU.add))
                dve.memset(rope_pad[grp(0), :], 0.0)
                dve.memset(proj[grp(1), 8, :], 0.0).then_inc(rope_ready, 1)
                turned()
                dve.wait_ge(rope_ready, 1)
                attention(4, ATTN_SCALE, diff_out, combine=diff_combine, tile_of=lambda u: u, maps=2,
                          beside=lambda u: f_chunks(1, memkT[:, 2 * u:2 * u + 2, :]))
                dve.wait_ge(o_done, sent.total(o_done))
                for qt in range(TT):
                    for u in range(4):
                        k = qt * 4 + u
                        o = obuf[:, qt, u * P:(u + 1) * P]
                        ins = dve.tensor_tensor_reduce(junk[:, k * P:(k + 1) * P], o, o, 1.0, 0.0,
                                                       ALU.mult, ALU.add, sq[:, k:k + 1])
                ins.then_inc(dsq_ready, 1)

                def half_values(u):
                    if u % 2:
                        t_values(memv[:, :, (u // 2) * 512:(u // 2 + 1) * 512], 512, 1)
                    else:
                        ahead()

                attention(4, MLA_SCALE, plain_out(512, P), tile_of=lambda u: 0, beside=half_values)
                dve.wait_ge(rstd_ready, due(rstd_ready))
                for qt in range(TT):
                    for u in range(4):
                        o = obuf[:, qt, u * P:(u + 1) * P]
                        k = qt * 4 + u
                        ins = dve.scalar_tensor_tensor(o, o, rstd[:, k:k + 1], subg[:], ALU.mult, ALU.mult)
                ins.then_inc(dnorm_ready, 1)
                turned()
                residual(1.0, EV_O)

            def cross():
                norm(h)
                turned()
                f_chunks(4, proj)
                attention(4, XA_SCALE, plain_out(0, T), full=True)
                turned()
                obuf_turned_at.append(jobs[0])
                residual(1.0, 4)

            def odd_mixer():
                norm(h)
                turned()
                f_chunks(8, proj)
                t_values(vtok, D, 4)
                norm(obuf)
                turned()
                mask0 = sbm[:, 0:T].unsqueeze(1).to_broadcast([P, 2, T])

                def masked(p):
                    b = 2 * (p % 2)
                    dve.wait_ge(z_full, p + 1)
                    dve.scalar_tensor_tensor(sb_m[:, p % 2, 0:2 * T].rearrange("p (a b) -> p a b", a=2),
                                             acc[:, b, :].rearrange("p (a b) -> p a b", a=2), ATTN_SCALE, mask0,
                                             ALU.mult, ALU.add)
                    dve.scalar_tensor_tensor(sb_m[:, p % 2, 2 * T:SBW], acc[:, b + 1, 0:T], ATTN_SCALE,
                                             sbm[:, T:2 * T], ALU.mult, ALU.add).then_inc(m_ready, 1)

                def output(p):
                    dve.wait_ge(so_full, p + 1)
                    for qt in range(TT):
                        for i, hh in enumerate(sb_heads(p)):
                            ins = dve.tensor_copy(obuf[:, qt, hh * DH:(hh + 1) * DH],
                                                  aux[:, 0, T + qt * P + i * DH:T + qt * P + (i + 1) * DH])
                    ins.then_inc(so_done, 1)

                def memory(p):
                    ahead()
                    if p < 4:
                        dve.wait_ge(chunk_used, at[0])
                        dve.tensor_copy(memkT[:, 2 * p:2 * p + 2, :], (mid, aux)[p % 2][:, 1, :].rearrange(
                            "p (k q) -> p k q", q=T)).then_inc(side_done, 1)
                    elif p % 2:
                        dve.wait_ge(chunk_used, at[0])
                        for t in range(TT):
                            dve.tensor_copy(memv[:, t, (p // 2 - 2) * 512:(p // 2 - 1) * 512],
                                            (mid, aux)[t][:, 1, :]).then_inc(side_done, 1)

                masked(0)
                for p in range(8):
                    if p + 1 < 8:
                        if p >= 1:
                            dve.wait_ge(a_ready, p)
                        masked(p + 1)
                    dve.wait_ge(ln_ready, p + 1)
                    dve.scalar_tensor_tensor(sb_l[:, p % 2, :], sb_m[:, p % 2, :], 0.0, sb_l[:, p % 2, :], ALU.max,
                                             ALU.add).then_inc(sp_ready, 1)
                    memory(p)
                    if p >= 1:
                        output(p - 1)
                    dve.wait_ge(s_full, p + 1)
                    m0, m1 = sb_m[:, p % 2, 0:2 * T], sb_m[:, p % 2, 2 * T:SBW]
                    dve.tensor_tensor(m0, m0, mid[:, 0, :], ALU.subtract)
                    dve.tensor_tensor(m1, m1, aux[:, 0, 0:T], ALU.subtract).then_inc(zs_ready, 1)
                output(7)
                turned()
                residual(1.0, 4)

            for c in range(AHEAD):
                split(c, c % RING)
            norm(h)
            turned()
            ffn()
            mixer()
            norm(h)
            turned()
            ffn()
            final_norm()
            even_mixer()
            cross()
            norm(h)
            turned()
            mlp()
            odd_mixer()
            cross()
            norm(h)
            turned()
            mlp()
            final_norm()

        @block.scalar
        def _(act):
            sent, due = Tally(), Tally()
            at = [0]
            jobs = [0]
            hidden = [0]
            scored = [0]
            units = [0]

            def split(c, slot, chunk_waits):
                used, arrived = chunk_waits
                if used is not None:
                    act.wait_ge(chunk_used, used)
                act.wait_ge(raw_full[slot], arrived)
                act.activation(w_hi[:, slot, :], raw[:, slot, :], ACT.Copy).then_inc(hi_ready, 1)

            def split_at(c):
                if c < N_CHUNKS:
                    split(c, c % RING, (c - RING + 1 if c >= RING else None, 16 * (c // RING + 1)))

            def split_in_loop(c, i, per):
                split(c, c % RING, (i * per + (c - RING + 1), i * (16 * per // RING) + 16 * (c // RING + 1)))

            def ahead(n=1):
                for _ in range(n):
                    split_at(at[0] + AHEAD)
                    at[0] += 1

            def squares(src, ready):
                for t in range(TT):
                    ready(t)
                    if sent.total(sq_ready):
                        act.wait_ge(sq_ready, sent.total(sq_ready))
                    act.activation(junk, src[:, t, :], ACT.Square,
                                   accum_out=sq[:, t:t + 1]).then_inc(*sent.one(sq_ready))

            def h_summed(t):
                act.wait_ge(acc_done, due.total(acc_done) - 1 + t)

            def h_normed(t):
                act.wait_ge(h_ready, due(h_ready))

            def turned(tiles_=KT, per_bank=4):
                for t in range(TT):
                    for a in range(0, tiles_, per_bank):
                        n = min(per_bank, tiles_ - a)
                        m = jobs[0]
                        jobs[0] += 1
                        act.wait_ge(mid_full, due(mid_full))
                        act.activation(xT_hi[:, a:a + n, t * P:(t + 1) * P],
                                       mid[:, m % 2, 0:n * P].rearrange("p (k q) -> p k q", q=P),
                                       ACT.Copy).then_inc(thi_ready, 1)

            def mids(n, signalled):
                jobs[0] += n
                due(mid_full, signalled)

            def f_chunks(n):
                ahead(n)
                mids(n, 0)

            def t_chunks(n):
                ahead(n)
                due(acc_done, TT)

            def ffn():
                base, g0 = at[0], hidden[0]

                def step(c, j, r, g):
                    act.wait_ge(chunk_used, c + 1)
                    act.activation(ff_s[:, r, 0:T], mid[:, r, 0:T], ACT.Silu).then_inc(act_ready, 1)
                    act.wait_ge(g_ready, j + 1)
                    act.activation(g_hi[:, g, :], ff_g[:, r, 0:T], ACT.Copy).then_inc(ghi_ready, 1)

                for j in range(4):
                    split_at(base + j + AHEAD)
                    step(base + j, g0 + j, j % 2, j % 4)
                split_at(base + 4 + AHEAD)
                first, loops = base + 5, (FF_TILES // 2 - 3) // 2
                with act.Fori(0, loops) as i:
                    for b in range(2):
                        s = first + 3 * b
                        for n in range(2):
                            split_in_loop(s + n + AHEAD, i, 6)
                            step(i * 6 + (s + n), i * 4 + (g0 + 4 + 2 * b + n), n, 2 * b + n)
                        split_in_loop(s + 2 + AHEAD, i, 6)
                c, j = first + 6 * loops, 4 + 4 * loops
                for n in range(2):
                    split_at(c + n + AHEAD)
                    step(c + n, g0 + j + n, n, (j + n) % 4)
                hidden[0] += FF_TILES
                at[0] = c + 2
                t_chunks(2)

            def mlp():
                base, s0 = at[0], hidden[0]
                banks = [mid[:, jobs[0] % 2, :], mid[:, 1 - jobs[0] % 2, :], aux[:, 0, :]]

                def step(c, j, r, wait=True):
                    act.wait_ge(chunk_used, c + 1)
                    if wait:
                        act.wait_ge(glo_ready, j - 2)
                    act.activation(ff_s[:, r, :], banks[r], ACT.Relu).then_inc(act_ready, 1)
                    act.wait_ge(act_ready, j + 1)
                    act.activation(g_hi[:, 2 * r:2 * r + 2, :], ff_s[:, r, :].rearrange("p (k q) -> p k q", k=2),
                                   ACT.Square).then_inc(ghi_ready, 1)

                def steps(j):
                    c = base + 2 * j - 1
                    split_at(c + AHEAD)
                    step(c, s0 + j, j % 3, j >= 3)
                    split_at(c + 1 + AHEAD)

                split_at(base + AHEAD)
                step(base, s0, 0, False)
                for j in range(1, 4):
                    steps(j)
                loops = (MLP_STEPS - 4) // 3
                if base + MLP_CHUNKS == N_CHUNKS:
                    loops -= 1
                with act.Fori(0, loops) as i:
                    for b in range(3):
                        s = base + 7 + 2 * b
                        split_in_loop(s + AHEAD, i, 6)
                        step(i * 6 + s, i * 3 + (s0 + 4 + b), (4 + b) % 3)
                        split_in_loop(s + 1 + AHEAD, i, 6)
                for j in range(4 + 3 * loops, MLP_STEPS):
                    steps(j)
                hidden[0] += MLP_STEPS
                at[0] = base + MLP_CHUNKS - 1
                t_chunks(1)

            def attention(n_units, full=False, maps=1, sink=False, beside=None):
                segs = [(0, T), (T, T)] if full else SEG
                width = 2 * T if full else KEYCOLS

                def unit(u):
                    for _ in range(maps):
                        m, e = jobs[0], scored[0]
                        jobs[0] += 1
                        scored[0] += 1
                        due(mid_full)
                        act.wait_ge(mid_done, m + 1)
                        if u >= 2:
                            act.wait_ge(turned_full, u0 + u - 1) if maps == 1 else act.wait_ge(pc_ready, u - 1)
                        for qt in range(TT):
                            a, n = segs[qt]
                            if sink:
                                act.activation(esink[:, e % 4, qt:qt + 1], sinkt[:, u:u + 1], ACT.Exp,
                                               bias=nmax[:, e % 4, qt:qt + 1])
                            ins = act.activation(P_[:, e % 4, a:a + n], N_[:, e % 2, a:a + n], ACT.Exp,
                                                 bias=nmax[:, e % 4, qt:qt + 1], scale=-1.0,
                                                 accum_out=rsum[:, e % 4, qt:qt + 1])
                        ins.then_inc(exp_ready, 1)

                def copied(u):
                    n = u0 + u
                    act.wait_ge(turned_full, n + 1)
                    if n >= 2:
                        act.wait_ge(o_full, n - 1)
                    act.activation(PT_[:, n % 2, 0:width], aux[:, n % 2, 0:width],
                                   ACT.Copy).then_inc(turned_done, 1)

                u0 = units[0]
                unit(0)
                for u in range(n_units):
                    if u + 1 < n_units:
                        unit(u + 1)
                    copied(u)
                    if beside:
                        beside(u)
                units[0] += n_units

            def mixer():
                squares(h, h_summed)
                turned()
                f_chunks(MIX_F)
                act.wait_ge(lam_dots, 1)
                act.activation(lam[:, 0:2], lam[:, 0:2], ACT.Exp).then_inc(lam_exps, 1)
                act.wait_ge(blk_ready, 1)
                act.activation(blk_hi[:, 0:JJ * CCOLS], blk, ACT.Copy).then_inc(blkhi_ready, 1)
                t_chunks(MIX_V)
                act.wait_ge(acc_done, due.total(acc_done))
                act.activation(gate[:], vtok[:, :, GATE_COL:MIXV_W], ACT.Exp, scale=-1.0).then_inc(gexp_ready, 1)

                def second_blocks():
                    act.wait_ge(blk_ready, 2)
                    act.wait_ge(chunk_used, at[0])
                    act.activation(blk_hi[:, 0:JJ * CCOLS], blk, ACT.Copy).then_inc(blkhi_ready, 1)

                def gelu():
                    act.wait_ge(cmp_done, 4)
                    act.activation(hidg, hid, ACT.Gelu_apprx_tanh).then_inc(gelu_ready, 1)

                def exponentials():
                    act.wait_ge(cs_ready, 1)
                    act.activation(ce, cs, ACT.Exp).then_inc(ce_ready, 1)

                def copy_turned():
                    act.wait_ge(cpt_full, 1)
                    act.activation(cpT, acc[:, 0, :].rearrange("p (a q) -> p a q", a=4),
                                   ACT.Copy).then_inc(cpt_done, 1)

                steps = [lambda: ahead(2), second_blocks, lambda: ahead(2), gelu, None, exponentials, None,
                         copy_turned]
                attention(8, sink=True, beside=lambda u: steps[u] and steps[u]())
                attention(16)
                turned()
                t_chunks(MIX_O)

            def even_mixer():
                squares(h, h_normed)
                turned()
                f_chunks(EV_F)
                t_chunks(2)
                for t in range(TT):
                    act.wait_ge(acc_done, due.total(acc_done) - 1 + t)
                    for i, (a, n) in enumerate(((0, 2 * P), (2 * P, P))):
                        ins = act.activation(junk[:, t * CQ_W + a:t * CQ_W + a + n], cqs[:, t, a:a + n], ACT.Square,
                                             accum_out=sq[:, 2 * t + i:2 * t + i + 1])
                    ins.then_inc(*sent.one(sq_ready))
                t_chunks(2)
                turned(CQ_W // P)
                ahead(1)
                mids(4, 3)
                mids(2, 2)
                squares(obuf, lambda t: act.wait_ge(mem_full, 16))
                t_chunks(1)
                turned()
                attention(4, maps=2, beside=lambda u: f_chunks(1))
                attention(4, beside=lambda u: t_chunks(1) if u % 2 else ahead())
                turned()
                t_chunks(EV_O)

            def cross():
                squares(h, h_summed)
                turned()
                f_chunks(4)
                attention(4, full=True)
                turned()
                t_chunks(4)

            def odd_mixer():
                squares(h, h_summed)
                turned()
                f_chunks(8)
                squares(obuf, lambda t: act.wait_ge(mem_full, 32))
                t_chunks(4)
                turned()

                def own(ins):
                    ins.then_inc(*sent.one(act_own))
                    act.wait_ge(act_own, sent.total(act_own))

                def weights(p):
                    act.wait_ge(zs_ready, p + 1)
                    act.activation(sb_a[:, p % 2, :], sb_m[:, p % 2, :], ACT.Exp).then_inc(a_ready, 1)

                for p in range(8):
                    act.wait_ge(m_ready, p + 1)
                    l = sb_l[:, p % 2, :]
                    own(act.activation(l, sb_m[:, p % 2, :], ACT.Abs))
                    own(act.activation(l, l, ACT.Exp, scale=-1.0))
                    if p >= 1:
                        weights(p - 1)
                    act.activation(l, l, ACT.Ln, bias=1.0).then_inc(ln_ready, 1)
                    ahead()
                weights(7)
                turned()
                t_chunks(4)

            for c in range(AHEAD):
                split_at(c)
            squares(h, lambda t: act.wait_ge(x_full, 16))
            turned()
            ffn()
            mixer()
            squares(h, h_summed)
            turned()
            ffn()
            squares(h, h_summed)
            even_mixer()
            cross()
            squares(h, h_summed)
            turned()
            mlp()
            odd_mixer()
            cross()
            squares(h, h_summed)
            turned()
            mlp()
            squares(h, h_summed)

        @block.gpsimd
        def _(pool):
            sent, due = Tally(), Tally()
            norms = [0]
            loaded = [0]
            normed = [0]

            def own(ins):
                ins.then_inc(*sent.one(pool_own))
                pool.wait_ge(pool_own, sent.total(pool_own))

            def load_gain(k):
                if k < N_GAINS:
                    pool.dma_start(gain[:, k % 2, :],
                                   gains[k:k + 1, :].to_broadcast([P, D])).then_inc(gain_full[k % 2], 16)

            def inverse(a, n, width):
                own(pool.tensor_scalar(ms[:, a:a + n], sq[:, a:a + n], 1.0 / width, EPS, ALU.mult, ALU.add))

            def norm(in_place=False):
                for t in range(TT):
                    pool.wait_ge(sq_ready, due(sq_ready))
                    inverse(t, 1, D)
                    pool.tensor_tensor(rstd[:, t:t + 1], ms[:, t:t + 1], nhalf[:, t:t + 1],
                                       ALU.pow).then_inc(*sent.one(rstd_ready))
                k = norms[0]
                norms[0] += 1
                s = h_ready if in_place else xn_ready
                n = due(s, TT if in_place else 2 * TT)
                if k + 2 < N_GAINS:
                    pool.wait_ge(s, n)
                    load_gain(k + 2)

            def biases(n):
                for _ in range(n):
                    k = loaded[0]
                    loaded[0] += 1
                    if k >= BIAS_SLOTS:
                        pool.wait_ge(mid_done, bias_used_at[k - BIAS_SLOTS])
                    pool.dma_start(bias[:, k % BIAS_SLOTS, :], bias_tiles[k]).then_inc(bias_full[k % BIAS_SLOTS], 16)

            def load_mem(n):
                pool.wait_ge(mid_done, obuf_turned_at[n])
                pool.dma_start(obuf[:], mem.rearrange("(t p) d -> p t d", p=P)).then_inc(mem_full, 16)

            load_gain(0)
            load_gain(1)
            own(pool.memset(nhalf[:], -0.5))
            biases(BIAS_SLOTS)
            norm()
            norm()
            biases(16 - BIAS_SLOTS)
            load_mem(0)
            norm()
            norm(True)
            norm()
            biases(3)
            for t in range(TT):
                pool.wait_ge(sq_ready, due(sq_ready))
                inverse(2 * t, 1, 2 * P)
                inverse(2 * t + 1, 1, P)
                pool.tensor_tensor(rstd[:, 2 * t:2 * t + 2], ms[:, 2 * t:2 * t + 2], nhalf[:, 0:2],
                                   ALU.pow).then_inc(*sent.one(rstd_ready))
            due(xn_ready, TT)
            norm()
            biases(2)
            pool.wait_ge(dsq_ready, 1)
            inverse(0, 8, P)
            pool.tensor_tensor(rstd[:, 0:8], ms[:, 0:8], nhalf[:, 0:8], ALU.pow).then_inc(*sent.one(rstd_ready))
            norm()
            load_mem(1)
            norm()
            norm()
            norm()
            norm()
            norm()
            norm(True)

        @block.sync
        def _(sp):
            sp.dma_start(h[:], x.rearrange("(t p) d -> p t d", p=P)).then_inc(x_full, 16)
            sp.dma_start(ident[:], squares_in[0]).then_inc(ident_full, 16)
            for c in range(RING):
                sp.dma_start(raw[:, c, :], stream[c]).then_inc(raw_full[c], 16)
            consts = [(tri, squares_in[1]), (ones, squares_in[2]), (zero, squares_in[3, 0:1, 0:1].to_broadcast([P, 1])), (sbm, sb_mask),
                      (ropet, rope), (cbias, cmp_bias), (cmask, cmp_mask), (cqg, cq_gain.to_broadcast([P, CQ_W])),
                      (subg, sub_gain.to_broadcast([P, P])), (sinkt, sinks.to_broadcast([P, 8])),
                      (posT, cmp_pos), (b1T, cmp_b1), (w2k, cmp_w2k), (w2v, cmp_w2v)]
            consts += [(lamv[:, i, :], lam_vecs[i:i + 1, :].to_broadcast([P, DH])) for i in range(4)]
            assert len(consts) == n_const
            for dst, src in consts:
                sp.dma_start(dst[:], src).then_inc(const_full, 16)
            rounds = N_CHUNKS // RING
            with sp.Fori(1, rounds) as i:
                for s in range(RING):
                    sp.wait_ge(lo_ready, i * RING + (s + 1 - RING))
                    sp.dma_start(raw[:, s, :], stream[i * RING + s]).then_inc(raw_full[s], 16)
            for c in range(rounds * RING, N_CHUNKS):
                sp.wait_ge(lo_ready, c - RING + 1)
                sp.dma_start(raw[:, c % RING, :], stream[c]).then_inc(raw_full[c % RING], 16)
            sp.wait_ge(last_h[0], last_h[1])
            sp.dma_start(out.rearrange("(t p) d -> p t d", p=P), h[:]).then_inc(out_full, 16)
            sp.wait_ge(out_full, 16)



def weight_stream(w):
    chunks = []

    def put(a):
        a = a.reshape(P, -1)
        full = np.zeros((P, CH), np.float32)
        full[:, :a.shape[1]] = a
        chunks.append(full)

    def f_chunk(m, cols):
        put(m[:, cols].reshape(-1, P, len(cols)).transpose(1, 0, 2))

    def f_tiles(m, tiles):
        for i in range(0, len(tiles), 2):
            f_chunk(m, np.concatenate(tiles[i:i + 2]))

    def t_chunks(m, kts):
        for i in range(0, m.shape[0] // P, kts):
            put(m[i * P:(i + kts) * P].reshape(kts, P, m.shape[1]).transpose(1, 0, 2))

    def cols(a, n=P):
        return np.arange(a, a + n)

    def ffn(w_in, w_out):
        def ins(j):
            f_chunk(w_in, np.concatenate([cols(j * P), cols(D_FF + j * P)]))

        def outs(k):
            t_chunks(w_out[2 * k * P:2 * (k + 1) * P], 2)

        for j in range(4):
            ins(j)
        outs(0)
        for k in range(1, FF_TILES // 2 - 1):
            ins(2 * k + 2)
            ins(2 * k + 3)
            outs(k)
        outs(FF_TILES // 2 - 1)

    def mlp(w1, w2):
        f_chunk(w1, cols(0, 2 * P))
        for j in range(1, MLP_STEPS):
            f_chunk(w1, cols(j * 2 * P, 2 * P))
            t_chunks(w2[(j - 1) * 2 * P:j * 2 * P], 2)
        t_chunks(w2[(MLP_STEPS - 1) * 2 * P:], 2)

    def mixer():
        m = w["w_mix_in"][0]
        kv = 512
        qb = 512 + 768 + 24
        kvb = qb + 512
        tiles = [np.tile(cols(kv + b * P + g * DH, DH), 2) for b in (0, 1) for g in (0, 1)]
        tiles += [cols(kv + 2 * P), cols(kv + 4 * P), cols(kvb)]
        for q in (0, qb):
            tiles += [np.concatenate([cols(q + r * DH, DH), cols(q + (4 + r) * DH, DH)]) for r in range(4)]
        tiles.append(tiles[-1])
        f_tiles(m, tiles)
        t_chunks(m[:, np.concatenate([cols(kv + 3 * P), cols(kv + 5 * P), cols(kvb + P), cols(kv + 768, 24)])], 4)
        for name in ("cmp_k_w1", "cmp_v_w1"):
            t_chunks(w[name][0], 8)
        t_chunks(w["w_mix_out"][0], 2)

    def even():
        m = w["ev_w_in_2"][0]
        kr = 512 * 3 + 256 + 128
        swapped = np.concatenate([cols(32, 32), cols(0, 32)])
        tiles = [cols(i * P) for i in range(8)] + [np.tile(cols(kr, DH), 2), np.tile(kr + swapped, 2)]
        f_tiles(m, tiles)
        t_chunks(m[:, 1536:1536 + CQ_W], 4)
        t_chunks(m[:, 1024:1536], 4)
        u = w["mla_w_uq_2"][0]
        nope = [cols(hd * 192) for hd in range(4)]
        rope = [cols(hd * 192 + P, DH) for hd in range(4)]
        rope_swapped = [hd * 192 + P + swapped for hd in range(4)]
        t_chunks(u[:, np.concatenate(nope + rope + rope_swapped)], 2)
        u = w["mla_w_ukv_2"][0]
        t_chunks(u[:, np.concatenate([cols(hd * T) for hd in range(4)] + [cols(hd * T + P) for hd in range(4)])], 1)
        memory(0)
        t_chunks(w["ev_w_out_2"][0], 2)

    def memory(l):
        kv = w["xa_wkv_2"][l]
        f_tiles(kv, [cols(i * P) for i in range(8)])
        t_chunks(kv[:, D:D + 512], 4)
        t_chunks(kv[:, D + 512:], 4)

    def cross(l):
        f_tiles(w["xa_wq_2"][l], [cols(i * P) for i in range(8)])
        t_chunks(w["xa_wo_2"][l], 2)

    def odd():
        m = w["sb_w_in_2"][0]
        f_tiles(m, [cols(i * P) for i in range(16)])
        t_chunks(m[:, 2 * D:], 2)
        memory(1)
        t_chunks(w["sb_w_out_2"][0], 2)

    ffn(w["ffn1_w_in"][0], w["ffn1_w_out"][0])
    mixer()
    ffn(w["ffn2_w_in"][0], w["ffn2_w_out"][0])
    even()
    cross(0)
    mlp(w["mlp_w1_2"][0], w["mlp_w2_2"][0])
    odd()
    cross(1)
    mlp(w["mlp_w1_2"][1], w["mlp_w2_2"][1])
    assert len(chunks) == N_CHUNKS
    return np.stack(chunks)


def shape_constants():
    q, k = np.arange(T)[:, None], np.arange(T)[None, :]
    dist = (q - k).astype(np.float32)

    def tile(values, allowed, scale):
        b = np.where(allowed, values, NEG) / scale
        return np.concatenate([b[:P, :P], b[P:, :]], axis=1).astype(np.float32)

    slopes8 = 2.0 ** (-8.0 * np.arange(1, 9) / 8)
    slopes4 = 2.0 ** (-8.0 * np.arange(1, 5) / 4)
    causal = dist >= 0
    chunked = (k // 64) <= (q // 64)
    tiles = [tile(-s * dist, causal & (dist < 128), ATTN_SCALE) for s in slopes8]
    tiles += [tile(-s * dist, causal, ATTN_SCALE) for s in slopes8]
    tiles += [tile(-s * np.abs(dist), chunked, ATTN_SCALE) for s in slopes4]
    tiles += [tile(0 * dist, chunked, MLA_SCALE)]
    strict = np.where(q.T > k.T, 0.0, NEG).astype(np.float32)
    sb_mask = np.concatenate([strict[:P, :], strict[P:, P:], strict[P:, P:]], axis=1)
    end = np.arange(CBLK) * 16 + 31
    cbias = np.zeros((P, 2, TT, 4, CBLK), np.float32)
    cmask = np.zeros((P, 2, TT, 4, CBLK), np.float32)
    for qt in range(TT):
        d = (qt * P + np.arange(P))[:, None] - end[None, :]
        for g in range(2):
            for r in range(4):
                cbias[:, g, qt, r] = np.where(d >= 0, -slopes8[g * 4 + r] * d, NEG)
                cmask[:, g, qt, r] = d >= 0
    inv = (10000.0 ** (-np.arange(32, dtype=np.float32) / 32)).astype(np.float32)
    ang = inv[:, None] * np.arange(T, dtype=np.float32)[None, :]
    cos, sin = np.cos(ang), np.sin(ang)
    rope = np.stack([np.concatenate([cos] * 4), np.concatenate([-sin, sin] * 2)], axis=1).astype(np.float32)
    eye, tri = np.eye(P), np.tril(np.ones((P, P)))
    squares = np.stack([eye, tri, np.ones((P, P)), np.zeros((P, P))]).astype(np.float32)
    return {
        "bias_tiles": np.stack(tiles), "sb_mask": sb_mask.astype(np.float32),
        "cmp_bias": cbias.reshape(P, 16, CBLK), "cmp_mask": cmask.reshape(P, 16, CBLK),
        "rope": rope, "squares_in": squares,
    }


def kernel(**inputs):
    import concourse.bacc as _bacc
    from concourse.bass_utils import run_bass_kernel_spmd as _run

    w = {n: np.asarray(a) for n, a in inputs.items()}
    arrays = {
        "stream": weight_stream(w),
        "x": w["x"][0],
        "mem": w["mem_2"][0],
        "gains": np.stack([w["ffn1_norm"][0], w["mix_norm"][0], w["ffn2_norm"][0], w["final_norm"],
                           w["ev_norm_2"][0], w["xa_mem_norm_2"][0], w["xa_norm_2"][0], w["mlp_norm_2"][0],
                           w["od_norm_2"][0], w["xa_mem_norm_2"][1], w["xa_norm_2"][1], w["mlp_norm_2"][1],
                           w["final_norm_2"]]),
        "cq_gain": np.concatenate([w["mla_g_cq_2"], w["mla_g_ckv_2"]], axis=1),
        "sub_gain": w["diff_subln_2"],
        "lam_vecs": np.concatenate([w["diff_lq1_2"], w["diff_lk1_2"], w["diff_lq2_2"], w["diff_lk2_2"]]),
        "sinks": w["swa_sinks"],
        "cmp_pos": np.stack([w[n][0].reshape(JJ, P).T for n in ("cmp_k_pos", "cmp_v_pos")], axis=1),
        "cmp_b1": np.stack([w[n][0].reshape(2, P).T for n in ("cmp_k_b1", "cmp_v_b1")], axis=1),
        "cmp_w2k": np.concatenate([w["cmp_k_w2"][0].reshape(2, P, DH)] * 2, axis=2).transpose(1, 0, 2),
        "cmp_w2v": w["cmp_v_w2"][0].reshape(2, P, DH).transpose(1, 0, 2),
        **shape_constants(),
    }
    nc = _bacc.Bacc("TRN2", target_bir_lowering=False, num_devices=1)
    args = {}
    for n in arrays:
        arrays[n] = np.ascontiguousarray(arrays[n])
        args[n] = nc.dram_tensor(f"in_{n}", arrays[n].shape, F32, kind="ExternalInput").ap()
    args["out"] = nc.dram_tensor("out_0", (T, D), F32, kind="ExternalOutput").ap()
    program(nc, **args)
    r = _run(nc, [{f"in_{n}": a for n, a in arrays.items()}], core_ids=[0])
    return r.results[0]["out_0"].reshape(1, T, D)
```

```python
from contextlib import ExitStack

import numpy as np

import concourse.bass as bass
from concourse import mybir

F32 = mybir.dt.float32
F32R = mybir.dt.float32r
ACT = mybir.ActivationFunctionType
ALU = mybir.AluOpType
AX = mybir.AxisListType

P = 128
T = 256
TT = T // P
D = 1024
KT = D // P
CH = 2048
RING = 3
AHEAD = 2
DH = 64
EPS = 1e-6
NEG = -1e30
D_FF = 2816
FF_TILES = D_FF // P
D_MLP = 4096
MLP_STEPS = D_MLP // (2 * P)
CBLK = 15
CCOLS = 2 * CBLK
JJ = 16
KEYCOLS = P + T
SEG = [(0, P), (P, T)]
ATTN_SCALE = DH ** -0.5
MLA_SCALE = 192 ** -0.5
XA_SCALE = 256 ** -0.5
LAMBDA_INIT = 0.2
BIAS_SLOTS = 3
N_GAINS = 13

FFN_CHUNKS = FF_TILES + FF_TILES // 2
MIX_F, MIX_V, MIX_C, MIX_O = 8, 2, 4, 4
EV_F, EV_V, EV_M, EV_O = 5, 4, 2, 4
XA_CHUNKS = 16
MLP_CHUNKS = 2 * MLP_STEPS
SB_CHUNKS = 16
N_CHUNKS = (2 * FFN_CHUNKS + MIX_F + MIX_V + MIX_C + MIX_O + EV_F + EV_V + EV_M + EV_O
            + 2 * XA_CHUNKS + 2 * MLP_CHUNKS + SB_CHUNKS)

MIXV_W = 408
CQ_W = 384
MIX_V0 = FFN_CHUNKS + MIX_F
EV_V0 = 2 * FFN_CHUNKS + MIX_F + MIX_V + MIX_C + MIX_O + EV_F
FILLED = {MIX_V0 - 1: KT * P, MIX_V0: 4 * MIXV_W, MIX_V0 + 1: 4 * MIXV_W, EV_V0: 4 * CQ_W, EV_V0 + 1: 4 * CQ_W,
          EV_V0 + EV_V + 1: D}

KC, VC, KS, KW, KB, QA, QB = 0, 2, 4, 5, 6, 7, 11
VS_COL, VW_COL, VB_COL, GATE_COL = 0, 128, 256, 384


def filled(c):
    return FILLED.get(c, CH) if isinstance(c, int) else CH


class Tally:

    def __init__(self):
        self.n = {}

    def __call__(self, sem, k=1):
        self.n[sem.name] = self.n.get(sem.name, 0) + k
        return self.n[sem.name]

    def total(self, sem):
        return self.n.get(sem.name, 0)

    def one(self, sem):
        self(sem)
        return sem, 1


def program(nc, stream, x, mem, gains, cq_gain, sub_gain, lam_vecs, sinks, cmp_pos, cmp_b1, cmp_w2k,
            cmp_w2v, bias_tiles, sb_mask, cmp_bias, cmp_mask, rope, squares_in, out):
    with ExitStack() as ctx:
        def sb(name, shape, dt=F32):
            return ctx.enter_context(nc.sbuf_tensor(name, shape, dt))

        def psum(name, shape):
            return ctx.enter_context(nc.psum_tensor(name, shape, F32))

        def sem(name):
            return ctx.enter_context(nc.semaphore(name))

        raw = sb("raw", [P, RING, CH])
        w_hi = sb("w_hi", [P, RING, CH], F32R)
        w_lo = sb("w_lo", [P, RING, CH], F32R)
        h = sb("h", [P, TT, D])
        xn = sb("xn", [P, TT, D])
        gain = sb("gain", [P, 2, D])
        xT_hi = sb("xT_hi", [P, KT, T], F32R)
        xT_lo = sb("xT_lo", [P, KT, T], F32R)
        g_hi = sb("g_hi", [P, 6, T], F32R)
        g_lo = sb("g_lo", [P, 6, T], F32R)
        proj = sb("proj", [P, 16, T])
        vtok = sb("vtok", [P, TT, D])
        memkT = sb("memkT", [P, KT, T])
        memv = sb("memv", [P, TT, D])
        obuf = sb("obuf", [P, TT, D])
        work = sb("work", [P, 6144])
        bias = sb("bias", [P, BIAS_SLOTS, KEYCOLS])
        ident = sb("ident", [P, P])
        zero = sb("zero", [P, 1])
        sbm = sb("sbm", [P, 2 * T])
        subg = sb("subg", [P, P])
        sinkt = sb("sinkt", [P, 8])
        nsink = sb("nsink", [P, 8])
        tri = sb("tri", [P, P])
        ones = sb("ones", [P, P])
        gate = sb("gate", [P, TT, 24])
        lam = sb("lam", [P, 4])
        sq = sb("sq", [P, 8])
        ms = sb("ms", [P, 8])
        rstd = sb("rstd", [P, 8])
        nhalf = sb("nhalf", [P, 8])
        nmax = sb("nmax", [P, 4, 4])
        rsum = sb("rsum", [P, 4, 4])
        rinv = sb("rinv", [P, 4, 4])
        esink = sb("esink", [P, 4, 2])
        cst = sb("cst", [P, 3, 16])

        def cut(buf, a, *dims):
            n = int(np.prod(dims))
            v = buf.rearrange("p a b -> p (a b)")[:, a:a + n]
            names = "abcd"[:len(dims)]
            if len(dims) == 1:
                return v
            return v.rearrange("p (" + " ".join(names) + ") -> p " + " ".join(names), **dict(zip(names, dims)))

        cbias = cut(memkT, 0, 16, CBLK)
        cmask = cut(memkT, 256, 16, CBLK)
        posT = cut(memkT, 512, 2, JJ)
        b1T = cut(memkT, 544, 2, 2)
        w2k = cut(memkT, 576, 2, P)
        w2v = cut(memkT, 832, 2, DH)
        kcT = cut(memkT, 960, CCOLS)
        vcd = cut(memkT, 1024, 2, 4, DH)
        ropet = cut(memkT, 1536, 2, T)
        cqg = cut(memv, 0, CQ_W)
        lamv = cut(memv, 512, 4, DH)
        knope = [memv[:, i // 2, 512 + i % 2 * T:512 + (i % 2 + 1) * T] for i in range(4)]
        blk_hi = g_hi.rearrange("p a b -> p (a b)")
        blk_lo = g_lo.rearrange("p a b -> p (a b)")

        mix_pad = [work[:, 5120 + i * T:5120 + (i + 1) * T] for i in range(3)]
        diff_pad = [memkT[:, i, :] for i in (0, 1, 2, 4)]
        rope_pad = proj[:, 9, :]

        acc = psum("acc", [P, 4, 512])
        mid = psum("mid", [P, 2, 512])
        aux = psum("aux", [P, 2, 512])

        raw_full = [sem(f"raw_full{i}") for i in range(RING)]
        gain_full = [sem(f"gain_full{i}") for i in range(2)]
        bias_full = [sem(f"bias_full{i}") for i in range(BIAS_SLOTS)]
        x_full = sem("x_full")
        ident_full = sem("ident_full")
        mem_full = sem("mem_full")
        const_full = sem("const_full")
        out_full = sem("out_full")
        hi_ready = sem("hi_ready")
        lo_ready = sem("lo_ready")
        chunk_used = sem("chunk_used")
        sq_ready = sem("sq_ready")
        dsq_ready = sem("dsq_ready")
        rstd_ready = sem("rstd_ready")
        xn_ready = sem("xn_ready")
        h_ready = sem("h_ready")
        mid_full = sem("mid_full")
        mid_done = sem("mid_done")
        thi_ready = sem("thi_ready")
        acc_full = sem("acc_full")
        acc_done = sem("acc_done")
        act_ready = sem("act_ready")
        g_ready = sem("g_ready")
        ghi_ready = sem("ghi_ready")
        glo_ready = sem("glo_ready")
        exp_ready = sem("exp_ready")
        pc_ready = sem("pc_ready")
        turned_full = sem("turned_full")
        turned_done = sem("turned_done")
        o_full = sem("o_full")
        o_done = sem("o_done")
        lam_dots = sem("lam_dots")
        lam_exps = sem("lam_exps")
        blk_ready = sem("blk_ready")
        blkhi_ready = sem("blkhi_ready")
        blklo_ready = sem("blklo_ready")
        gelu_ready = sem("gelu_ready")
        hidd_ready = sem("hidd_ready")
        gexp_ready = sem("gexp_ready")
        cs_ready = sem("cs_ready")
        ce_ready = sem("ce_ready")
        cp_ready = sem("cp_ready")
        cpt_full = sem("cpt_full")
        cpt_done = sem("cpt_done")
        co_full = sem("co_full")
        co_done = sem("co_done")
        rope_ready = sem("rope_ready")
        dnorm_ready = sem("dnorm_ready")
        z_full = sem("z_full")
        m_ready = sem("m_ready")
        act_own = sem("act_own")
        ln_ready = sem("ln_ready")
        sp_ready = sem("sp_ready")
        s_full = sem("s_full")
        zs_ready = sem("zs_ready")
        a_ready = sem("a_ready")
        so_full = sem("so_full")
        side_done = sem("side_done")
        so_done = sem("so_done")
        cmp_full = sem("cmp_full")
        cmp_done = sem("cmp_done")
        dve_own = sem("dve_own")
        pool_own = sem("pool_own")

        n_const = 18
        bias_used_at = []
        obuf_turned_at = []
        rope_from = []
        last_h = []
        block = ctx.enter_context(nc.Block())

        N_ = work[:, 0:1024].rearrange("p (r c) -> p r c", r=2)
        P_ = work[:, 1024:3072].rearrange("p (r c) -> p r c", r=4)
        PT_ = work[:, 3072:4096].rearrange("p (r c) -> p r c", r=2)
        PC_ = work[:, 4096:5120].rearrange("p (r c) -> p r c", r=2)
        junk = work[:, 5120:6144]
        ff_s = work[:, 0:1536].rearrange("p (r c) -> p r c", r=3)
        ff_g = work[:, 1536:3072].rearrange("p (r c) -> p r c", r=3)
        rot = [memv[:, i // 2, i % 2 * T:(i % 2 + 1) * T] for i in range(4)]
        cqs = work[:, 0:2 * CQ_W].rearrange("p (t c) -> p t c", t=2)
        SBW = 2 * KEYCOLS
        sb_m = work[:, 0:2 * SBW].rearrange("p (r c) -> p r c", r=2)
        sb_l = work[:, 2 * SBW:4 * SBW].rearrange("p (r c) -> p r c", r=2)
        sb_a = work[:, 4 * SBW:6 * SBW].rearrange("p (r c) -> p r c", r=2)
        blk = cut(xn, 0, JJ * CCOLS)
        pre = cut(xn, 512, T)
        hid = cut(xn, 768, 2, 2, CCOLS)
        hidg = cut(xn, 896, 2, 2, CCOLS)
        hidd_flat = cut(xn, 1024, 4 * P)
        hidd = hidd_flat.rearrange("p (m g r c) -> p m g r c", m=2, g=2, r=4)
        cs = cut(xn, 1536, 16, CBLK)
        ce = cut(xn, 1792, 16, CBLK)
        cp_flat = work[:, 4096:4608]
        cp = cp_flat.rearrange("p (a c) -> p a c", a=16)
        cpT = work[:, 4608:5120].rearrange("p (a q) -> p a q", a=4)

        def grp(g):
            return slice(DH * g, DH * (g + 1))

        def mix_keys(g, i):
            return mix_pad[i] if g else proj[:, KS + i, :]

        def step(steps, u):
            if u < len(steps) and steps[u]:
                steps[u]()

        def turn_parts(tiles, fine):
            if tiles < KT:
                return [(t, 0, tiles) for t in range(TT)]
            if fine:
                return [(0, 0, 4), (0, 4, 4), (1, 0, 2), (1, 2, 2), (1, 4, 4)]
            return [(t, a, 4) for t in range(TT) for a in (0, 4)]

        def read_order(parts):
            return sorted(range(len(parts)), key=lambda i: (parts[i][1] // 4, parts[i]))

        def turn_banks(first, n):
            a = (first + n) % 2
            return [mid[:, a, :], mid[:, 1 - a, :], aux[:, 0, :], aux[:, 1, :], acc[:, 0, :]][:n]

        def sb_heads(p):
            first = 4 * (p // 2) + p % 2
            return first, first + 2

        @block.tensor
        def _(pe):
            sent, due = Tally(), Tally()
            at = [0]
            jobs = [0]
            hidden = [0]
            scored = [0]
            xT_at = {}
            waited = [0]
            read_at = [0, 0]

            def mid_bank():
                n = jobs[0]
                jobs[0] += 1
                if read_at[n % 2]:
                    pe.wait_ge(mid_done, read_at[n % 2])
                read_at[n % 2] = n + 1
                return mid[:, n % 2, :]

            def three(out_ap, lhs, rhs, start, stop):
                pe.matmul(out_ap, lhs[0], rhs[0], start=start, stop=False)
                pe.matmul(out_ap, lhs[0], rhs[1], start=False, stop=False)
                return pe.matmul(out_ap, lhs[1], rhs[0], start=False, stop=stop)

            def w_pair(slot, a, n):
                return w_hi[:, slot, a:a + n], w_lo[:, slot, a:a + n]

            def xT_pair(k, t):
                xT_stands(k, t)
                return xT_hi[:, k, t * P:(t + 1) * P], xT_lo[:, k, t * P:(t + 1) * P]

            def xT_stands(k, t):
                n = xT_at[t, k]
                if n > waited[0]:
                    pe.wait_ge(mid_done, n)
                    waited[0] = n

            def f_tile(out_ap, slot, kts, width, col):
                for k in range(kts):
                    xT_stands(k, TT - 1)
                    mm = three(out_ap, w_pair(slot, k * width + col, P), (xT_hi[:, k, :], xT_lo[:, k, :]),
                               k == 0, k == kts - 1)
                return mm

            def f_chunks(n, tiles=2):
                for _ in range(n):
                    c = at[0]
                    bank = mid_bank()
                    pe.wait_ge(lo_ready, c + 1)
                    for m in range(tiles):
                        mm = f_tile(bank[:, m * T:(m + 1) * T], c % RING, KT, tiles * P, m * P)
                    mm.then_inc(chunk_used, 1)
                    at[0] += 1

            def t_chunk(slot, lhs, kts, width, halves, start, stop):
                for t in range(TT):
                    steps = [(k, half) for k in range(kts) for half in range(halves)]
                    if stop:
                        steps.sort(key=lambda step: step[1])
                    for k, half in steps:
                        w = min(width, 512)
                        mm = three(acc[:, t * halves + half, 0:w], lhs(k, t),
                                   w_pair(slot, k * width + half * 512, w),
                                   start and k == 0, stop and k == kts - 1)
                        if stop and k == kts - 1 and (t, half) != (TT - 1, halves - 1):
                            mm.then_inc(acc_full, 1)
                mm.then_inc(chunk_used, 1)

            def acc_free(halves=2):
                if due.total(acc_done):
                    pe.wait_ge(acc_done, due.total(acc_done))
                due(acc_done, TT * halves)

            def t_chunks(width):
                kts, halves = (2, 2) if width == D else (4, 1)
                n = KT // kts
                acc_free(halves)
                for i in range(n):
                    c = at[0]
                    pe.wait_ge(lo_ready, c + 1)
                    t_chunk(c % RING, lambda k, t: xT_pair(i * kts + k, t), kts, width, halves,
                            i == 0, i == n - 1)
                    at[0] += 1

            def turn(src, ready, tiles=KT, fine=False):
                parts = turn_parts(tiles, fine)
                first = jobs[0]
                for i, bank in enumerate(turn_banks(first, len(parts))):
                    t, a, n = parts[i]
                    ready(t, a)
                    if i < 2:
                        which = (first + len(parts) + i) % 2
                        if read_at[which]:
                            pe.wait_ge(mid_done, read_at[which])
                    elif i == 4 and due.total(acc_done):
                        pe.wait_ge(acc_done, due.total(acc_done))
                    for k in range(a, a + n):
                        mm = pe.transpose(bank[:, (k - a) * P:(k - a + 1) * P],
                                          src[:, t, k * P:(k + 1) * P], ident[:])
                    mm.then_inc(*sent.one(mid_full))
                jobs[0] += len(parts)
                for done, i in enumerate(read_order(parts)):
                    t, a, n = parts[i]
                    for k in range(a, a + n):
                        xT_at[t, k] = first + done + 1
                    if i < 2:
                        read_at[(first + len(parts) + i) % 2] = first + done + 1

            def normed(t, a):
                pe.wait_ge(xn_ready, due(xn_ready))

            def heads_out(t, a):
                pe.wait_ge(o_done, sent.total(o_full))

            def g_pair(j):
                return lambda k, t: (g_hi[:, j * 2 + k, t * P:(t + 1) * P], g_lo[:, j * 2 + k, t * P:(t + 1) * P])

            def ffn():
                base, g0 = at[0], hidden[0]
                pairs = FF_TILES // 2
                banks = [mid[:, (jobs[0] + r) % 2, :] for r in range(2)]

                def step_in(c, j, slot, r, wait=True):
                    pe.wait_ge(lo_ready, c + 1)
                    if wait:
                        pe.wait_ge(g_ready, j - 1)
                    for m in range(2):
                        mm = f_tile(banks[r][:, m * T:(m + 1) * T], slot, KT, 2 * P, m * P)
                    mm.then_inc(chunk_used, 1)

                def step_out(c, j, slot, pair, start, stop):
                    pe.wait_ge(lo_ready, c + 1)
                    pe.wait_ge(glo_ready, j)
                    t_chunk(slot, g_pair(pair), 2, D, 2, start, stop)

                acc_free()
                for j in range(4):
                    step_in(base + j, g0 + j, (base + j) % RING, j % 2, j >= 2)
                step_out(base + 4, g0 + 2, (base + 4) % RING, 0, True, False)
                first, loops = base + 5, (pairs - 3) // 2
                with pe.Fori(0, loops) as i:
                    for b in range(2):
                        s = first + 3 * b
                        c, j = i * 6 + s, i * 4 + (g0 + 4 + 2 * b)
                        step_in(c, j, s % RING, 0)
                        step_in(c + 1, j + 1, (s + 1) % RING, 1)
                        step_out(c + 2, j, (s + 2) % RING, (1 + b) % 2, False, False)
                c, j = first + 6 * loops, g0 + 4 + 4 * loops
                step_in(c, j, c % RING, 0)
                step_in(c + 1, j + 1, (c + 1) % RING, 1)
                step_out(c + 2, j, (c + 2) % RING, (pairs - 2) % 2, False, False)
                step_out(c + 3, j + 2, (c + 3) % RING, (pairs - 1) % 2, False, True)
                at[0] = c + 4
                hidden[0] += FF_TILES

            def mlp():
                base, s0 = at[0], hidden[0]
                banks = [mid[:, jobs[0] % 2, :], mid[:, 1 - jobs[0] % 2, :], aux[:, 0, :]]

                def step_in(c, j, slot, r, wait=True):
                    pe.wait_ge(lo_ready, c + 1)
                    if wait:
                        pe.wait_ge(act_ready, j - 2)
                    for m in range(2):
                        mm = f_tile(banks[r][:, m * T:(m + 1) * T], slot, KT, 2 * P, m * P)
                    mm.then_inc(chunk_used, 1)

                def step_out(c, j, slot, r, start, stop):
                    pe.wait_ge(lo_ready, c + 1)
                    pe.wait_ge(glo_ready, j + 1)
                    t_chunk(slot, g_pair(r), 2, D, 2, start, stop)

                acc_free()
                step_in(base, s0, base % RING, 0, False)
                for j in range(1, 4):
                    c = base + 2 * j - 1
                    step_in(c, s0 + j, c % RING, j % 3, j >= 3)
                    step_out(c + 1, s0 + j - 1, (c + 1) % RING, (j - 1) % 3, j == 1, False)
                loops = (MLP_STEPS - 4) // 3
                with pe.Fori(0, loops) as i:
                    for b in range(3):
                        s = base + 7 + 2 * b
                        c = i * 6 + s
                        step_in(c, i * 3 + (s0 + 4 + b), s % RING, (4 + b) % 3)
                        step_out(c + 1, i * 3 + (s0 + 3 + b), (s + 1) % RING, (3 + b) % 3, False, False)
                c = base + MLP_CHUNKS - 1
                step_out(c, s0 + MLP_STEPS - 1, c % RING, (MLP_STEPS - 1) % 3, False, True)
                at[0] = c + 1
                hidden[0] += MLP_STEPS

            def attention(n_units, dv, scores, values, full=False, maps=1, beside=None):
                def score(u):
                    for m in range(maps):
                        scores(u, m, mid_bank()).then_inc(*sent.one(mid_full))

                def turn_probs(u):
                    if maps == 1:
                        pe.wait_ge(exp_ready, scored[0] + 1)
                        src = P_[:, scored[0] % 4, :]
                    else:
                        pe.wait_ge(pc_ready, due(pc_ready))
                        src = PC_[:, u % 2, :]
                    scored[0] += maps
                    n = sent.total(turned_full)
                    if n >= 2:
                        pe.wait_ge(turned_done, n - 1)
                    for b in range(4 if full else 3):
                        mm = pe.transpose(aux[:, n % 2, b * P:(b + 1) * P], src[:, b * P:(b + 1) * P], ident[:])
                    mm.then_inc(*sent.one(turned_full))

                def weigh(u):
                    n = sent.total(o_full)
                    pe.wait_ge(turned_done, n + 1)
                    if n >= 2:
                        pe.wait_ge(o_done, n - 1)
                    bank = acc[:, 2 + n % 2, :]
                    parts = (((0, 0), (1, 1)), ((2, 0), (3, 1))) if full else (((0, 0),), ((1, 0), (2, 1)))
                    for qt in range(TT):
                        for i, (b, kt) in enumerate(parts[qt]):
                            mm = pe.matmul(bank[:, qt * dv:(qt + 1) * dv], PT_[:, n % 2, b * P:(b + 1) * P],
                                           values(u, kt), start=i == 0, stop=i == len(parts[qt]) - 1)
                    mm.then_inc(*sent.one(o_full))

                score(0)
                for u in range(n_units):
                    if u + 1 < n_units:
                        score(u + 1)
                    if beside:
                        beside(u)
                    turn_probs(u)
                    if u >= 1:
                        weigh(u - 1)
                weigh(n_units - 1)

            def head_scores(bank, q, k):
                for qt in range(TT):
                    a, n = SEG[qt]
                    mm = pe.matmul(bank[:, a:a + n], q[:, qt * P:(qt + 1) * P], k[:, 0:n], start=True, stop=True)
                return mm

            def compressed_steps():
                used = [0]

                def bank_():
                    n = used[0]
                    used[0] += 1
                    if n >= 2:
                        pe.wait_ge(cmp_done, n - 1)
                    return acc[:, n % 2, :]

                def first_layer(v):
                    pe.wait_ge(blklo_ready, v + 1)
                    bank = bank_()
                    for half in range(2):
                        c = at[0]
                        pe.wait_ge(lo_ready, c + 1)
                        for j in range(8):
                            jj = half * 8 + j
                            lhs = [b[:, jj * CCOLS:jj * CCOLS + P] for b in (blk_hi, blk_lo)]
                            mm = three(bank[:, 0:T], lhs, w_pair(c % RING, j * T, T), jj == 0, jj == JJ - 1)
                        mm.then_inc(chunk_used, 1)
                        at[0] += 1

                def turn_hidden(v):
                    pe.wait_ge(cmp_done, 2 * v + 1)
                    bank = bank_()
                    for m in range(2):
                        mm = pe.transpose(bank[:, m * CCOLS:(m + 1) * CCOLS], pre[0:CCOLS, m * P:(m + 1) * P],
                                          ident[0:CCOLS, 0:CCOLS])
                    mm.then_inc(cmp_full, 1)

                def second_layer():
                    pe.wait_ge(gelu_ready, 1)
                    bank = bank_()
                    for m in range(2):
                        mm = pe.matmul(bank[:, 0:CCOLS], w2k[:, m, :], hidg[:, 0, m, :], start=m == 0, stop=m == 1)
                    mm.then_inc(cmp_full, 1)
                    pe.wait_ge(hidd_ready, 1)
                    bank = bank_()
                    for g in range(2):
                        for m in range(2):
                            mm = pe.matmul(bank[:, g * DH:(g + 1) * DH],
                                           hidd_flat[:, (2 * m + g) * P:(2 * m + g + 1) * P],
                                           w2v[:, m, :], start=m == 0, stop=m == 1)
                    mm.then_inc(cmp_full, 1)

                def block_scores():
                    pe.wait_ge(cmp_done, 6)
                    bank = bank_()
                    for qt in range(TT):
                        for r in range(4):
                            a = (qt * 4 + r) * 32
                            mm = pe.matmul(bank[:, a:a + CCOLS], proj[:, QA + r, qt * P:(qt + 1) * P], kcT,
                                           start=True, stop=True)
                    mm.then_inc(cmp_full, 1)

                def turn_blocks():
                    pe.wait_ge(cp_ready, 1)
                    bank = bank_()
                    for a in range(4):
                        mm = pe.transpose(bank[:, a * P:(a + 1) * P], cp_flat[:, a * P:(a + 1) * P], ident[:])
                    mm.then_inc(cpt_full, 1)

                def block_outputs():
                    pe.wait_ge(cmp_done, 7)
                    pe.wait_ge(cpt_done, 1)
                    for qt in range(TT):
                        for g in range(2):
                            mm = pe.matmul(acc[:, qt, g * T:(g + 1) * T], cpT[:, g * 2 + qt, :],
                                           vcd[:, g, :, :], start=True, stop=True)
                        mm.then_inc(co_full, 1)

                return [lambda: first_layer(0), lambda: turn_hidden(0), lambda: first_layer(1),
                        lambda: turn_hidden(1), second_layer, block_scores, None, None, turn_blocks,
                        block_outputs]

            def stick_breaking():
                side = [mid[:, 1, :], aux[:, 1, :]]

                def z_scores(p):
                    if p >= 2:
                        pe.wait_ge(m_ready, p - 1)
                    b = 2 * (p % 2)
                    for i, hd in enumerate(sb_heads(p)):
                        q, k = proj[grp(hd % 2), hd // 2, :], proj[grp(hd % 2), 8 + hd // 2, :]
                        pe.matmul(acc[:, b, i * T:(i + 1) * T], k[:, 0:P], q, start=True, stop=True)
                        mm = pe.matmul(acc[:, b + 1, i * P:(i + 1) * P], k[:, P:T], q[:, P:T], start=True, stop=True)
                    mm.then_inc(z_full, 1)

                def later_sums(p):
                    pe.wait_ge(sp_ready, p + 1)
                    if p >= 1:
                        pe.wait_ge(zs_ready, p)
                    sp = sb_l[:, p % 2, :]
                    for i in range(2):
                        s = mid[:, 0, i * T:(i + 1) * T]
                        sp0, sp1 = sp[:, i * T:(i + 1) * T], sp[:, 2 * T + i * P:2 * T + (i + 1) * P]
                        pe.matmul(s[:, 0:P], tri[:], sp0[:, 0:P], start=True, stop=True)
                        pe.matmul(s[:, P:T], tri[:], sp0[:, P:T], start=True, stop=False)
                        pe.matmul(s[:, P:T], ones[:], sp1, start=False, stop=True)
                        mm = pe.matmul(aux[:, 0, i * P:(i + 1) * P], tri[:], sp1, start=True, stop=True)
                    mm.then_inc(s_full, 1)

                def outputs(p):
                    pe.wait_ge(a_ready, p + 1)
                    if p >= 1:
                        pe.wait_ge(so_done, p)
                    a = sb_a[:, p % 2, :]
                    for i, hd in enumerate(sb_heads(p)):
                        v = slice(hd * DH, (hd + 1) * DH)
                        for qt in range(TT):
                            o = aux[:, 0, T + qt * P + i * DH:T + qt * P + (i + 1) * DH]
                            mm = pe.matmul(o, a[:, i * T + qt * P:i * T + (qt + 1) * P], vtok[:, 0, v],
                                           start=True, stop=qt == 0)
                            if qt:
                                mm = pe.matmul(o, a[:, 2 * T + i * P:2 * T + (i + 1) * P], vtok[:, 1, v],
                                               start=False, stop=True)
                    mm.then_inc(so_full, 1)

                def memory(p):
                    c = at[0]
                    pe.wait_ge(lo_ready, c + 1)
                    if p < 4:
                        if p >= 2:
                            pe.wait_ge(side_done, p - 1)
                        for m in range(2):
                            mm = f_tile(side[p % 2][:, m * T:(m + 1) * T], c % RING, KT, 2 * P, m * P)
                    else:
                        if p % 2 == 0:
                            pe.wait_ge(side_done, 4 + (p - 4))
                        for t in range(TT):
                            for k in range(4):
                                mm = three(side[t], xT_pair(p % 2 * 4 + k, t), w_pair(c % RING, k * 512, 512),
                                           p % 2 == 0 and k == 0, p % 2 == 1 and k == 3)
                    mm.then_inc(chunk_used, 1)
                    at[0] += 1

                z_scores(0)
                z_scores(1)
                for p in range(8):
                    memory(p)
                    later_sums(p)
                    if p + 2 < 8:
                        z_scores(p + 2)
                    if p >= 1:
                        outputs(p - 1)
                outputs(7)
                pe.wait_ge(side_done, 8)

            def projected():
                pe.wait_ge(mid_done, jobs[0])
                pe.wait_ge(acc_done, due.total(acc_done))

            def half_values(u):
                if u % 2 == 0:
                    acc_free(1)
                c = at[0]
                pe.wait_ge(lo_ready, c + 1)
                t_chunk(c % RING, lambda k, t: xT_pair(u % 2 * 4 + k, t), 4, 512, 1, u % 2 == 0, u % 2 == 1)
                at[0] += 1

            def cross():
                turn(xn, normed, fine=True)
                f_chunks(4)
                projected()

                def scores(u, m, bank):
                    for qt in range(TT):
                        for i in range(2):
                            mm = pe.matmul(bank[:, qt * T:(qt + 1) * T], proj[:, 2 * u + i, qt * P:(qt + 1) * P],
                                           memkT[:, 2 * u + i, :], start=i == 0, stop=i == 1)
                    return mm

                attention(4, T, scores, lambda u, kt: memv[:, kt, u * T:(u + 1) * T], full=True)
                turn(obuf, heads_out)
                t_chunks(D)

            def mixer():
                turn(xn, normed, fine=True)
                f_chunks(MIX_F - 1)
                f_chunks(1, 1)
                t_chunks(MIXV_W)
                projected()
                steps = compressed_steps()
                attention(8, DH, lambda u, m, bank: head_scores(
                    bank, proj[:, QB + u % 4, :], mix_keys(u // 4, 2)),
                    lambda u, kt: vtok[:, kt, VB_COL + DH * (u // 4):][:, 0:DH],
                    beside=lambda u: step(steps, u))
                attention(16, DH, lambda u, m, bank: head_scores(
                    bank, proj[:, QA + u // 2 % 4, :], mix_keys(u // 8, u % 2)),
                    lambda u, kt: vtok[:, kt, VS_COL + P * (u % 2) + DH * (u // 8):][:, 0:DH],
                    beside=lambda u: step(steps, u + 8))
                pe.wait_ge(co_done, TT)
                turn(obuf, heads_out)
                t_chunks(D)

            def even_mixer():
                turn(xn, normed, fine=True)
                f_chunks(EV_F)
                t_chunks(CQ_W)
                t_chunks(512)
                turn(xn, normed, CQ_W // P)
                c = at[0]
                pe.wait_ge(lo_ready, c + 1)
                for pair in range(4):
                    bank = mid_bank()
                    for m in range(2):
                        mm = f_tile(bank[:, m * T:(m + 1) * T], c % RING, 2, D, (2 * pair + m) * P)
                    mm.then_inc(*(sent.one(mid_full) if pair < 3 else (chunk_used, 1)))
                c += 1
                pe.wait_ge(lo_ready, c + 1)
                for pair in range(2):
                    bank = mid_bank()
                    for m in range(2):
                        mm = three(bank[:, m * T:(m + 1) * T], w_pair(c % RING, (2 * pair + m) * P, P),
                                   (xT_hi[:, 2, :], xT_lo[:, 2, :]), True, True)
                    mm.then_inc(*sent.one(mid_full))
                acc_free(1)
                for t in range(TT):
                    mm = three(acc[:, t, :], xT_pair(2, t), w_pair(c % RING, 512, 512), True, True)
                    mm.then_inc(*((acc_full, 1) if t == 0 else (chunk_used, 1)))
                at[0] = c + 1
                turn(xn, normed)
                projected()
                attention(4, P, lambda u, m, bank: head_scores(
                    bank, proj[:, u, :], diff_pad[u] if m else proj[:, 4 + u, :]),
                    lambda u, kt: vtok[:, kt, u * P:(u + 1) * P], maps=2, beside=lambda u: f_chunks(1))
                pe.wait_ge(rope_ready, 1)

                def scores(u, m, bank):
                    turned_keys = rope_pad if u % 2 else proj[:, 8, :]
                    for qt in range(TT):
                        a, n = SEG[qt]
                        pe.matmul(bank[:, a:a + n], proj[:, 10 + u, qt * P:(qt + 1) * P], knope[u][:, 0:n],
                                  start=True, stop=False)
                        mm = pe.matmul(bank[:, a:a + n], proj[:, 14 + u // 2, qt * P:(qt + 1) * P],
                                       turned_keys[:, 0:n], start=False, stop=True)
                    return mm

                attention(4, P, scores, lambda u, kt: vtok[:, kt, 512 + u * P:512 + (u + 1) * P],
                          beside=lambda u: half_values(u))
                pe.wait_ge(dnorm_ready, 1)
                turn(obuf, heads_out)
                t_chunks(D)

            def odd_mixer():
                turn(xn, normed, fine=True)
                f_chunks(8)
                t_chunks(D)
                turn(xn, normed)
                projected()
                stick_breaking()
                turn(obuf, lambda t, a: pe.wait_ge(so_done, 8))
                t_chunks(D)

            pe.wait_ge(ident_full, 16)
            turn(xn, normed, fine=True)
            ffn()
            pe.wait_ge(const_full, 16 * n_const)
            mixer()
            turn(xn, normed, fine=True)
            ffn()
            even_mixer()
            cross()
            turn(xn, normed, fine=True)
            mlp()
            odd_mixer()
            cross()
            turn(xn, normed, fine=True)
            mlp()

        @block.vector
        def _(dve):
            sent, due = Tally(), Tally()
            at = [0]
            jobs = [0]
            hidden = [0]
            norms = [0]
            tiles = [0]
            owed = []
            scored = [0]

            def own(ins):
                ins.then_inc(*sent.one(dve_own))
                dve.wait_ge(dve_own, sent.total(dve_own))

            def split(c, slot):
                dve.wait_ge(hi_ready, c + 1)
                n = filled(c)
                dve.tensor_tensor(w_lo[:, slot, 0:n], raw[:, slot, 0:n], w_hi[:, slot, 0:n],
                                  ALU.subtract).then_inc(lo_ready, 1)

            def ahead(n=1):
                for _ in range(n):
                    c = at[0] + AHEAD
                    if c < N_CHUNKS:
                        split(c, c % RING)
                    at[0] += 1

            def job(signalled=True):
                m = jobs[0]
                jobs[0] += 1
                if signalled:
                    dve.wait_ge(mid_full, due(mid_full))
                else:
                    dve.wait_ge(chunk_used, at[0])
                return mid[:, m % 2, :]

            def gained():
                k = norms[0]
                norms[0] += 1
                dve.wait_ge(gain_full[k % 2], 16 * (k // 2 + 1))
                return gain[:, k % 2, :]

            def norm(src, fine=False):
                g = gained()
                for t in range(TT):
                    dve.wait_ge(rstd_ready, due(rstd_ready))
                    for c in [slice(a * P, (a + n) * P) for tt, a, n in turn_parts(KT, fine) if tt == t]:
                        dve.scalar_tensor_tensor(xn[:, t, c], src[:, t, c], rstd[:, t:t + 1], g[:, c],
                                                 ALU.mult, ALU.mult).then_inc(*sent.one(xn_ready))

            def final_norm():
                g = gained()
                for t in range(TT):
                    dve.wait_ge(rstd_ready, due(rstd_ready))
                    for c in (slice(0, D // 2), slice(D // 2, D)):
                        dve.scalar_tensor_tensor(h[:, t, c], h[:, t, c], rstd[:, t:t + 1], g[:, c],
                                                 ALU.mult, ALU.mult).then_inc(*sent.one(h_ready))
                last_h[:] = [h_ready, sent.total(h_ready)]

            def turned(tiles_=KT, fine=False):
                parts = turn_parts(tiles_, fine)
                banks = turn_banks(jobs[0], len(parts))
                full, high = due.total(mid_full), due.total(thi_ready)
                for i in read_order(parts):
                    t, a, n = parts[i]
                    dve.wait_ge(mid_full, full + i + 1)
                    dve.wait_ge(thi_ready, high + i + 1)
                    dve.tensor_tensor(xT_lo[:, a:a + n, t * P:(t + 1) * P],
                                      banks[i][:, 0:n * P].rearrange("p (k q) -> p k q", q=P),
                                      xT_hi[:, a:a + n, t * P:(t + 1) * P],
                                      ALU.subtract).then_inc(mid_done, 1)
                jobs[0] += len(parts)
                due(mid_full, len(parts))
                due(thi_ready, len(parts))
                pay()

            def f_chunks(n, dst, first=0, tiles=2):
                for i in range(n):
                    a = first + 2 * i
                    ahead()
                    bank = job(False)
                    dve.tensor_copy(dst[:, a:a + tiles, :],
                                    bank[:, 0:tiles * T].rearrange("p (k q) -> p k q", q=T)).then_inc(mid_done, 1)

            def zero_halves(tile, pads):
                for i, pad in enumerate(pads):
                    dve.memset(proj[grp(1), tile + i, :], 0.0)
                    dve.memset(pad[grp(0), :], 0.0)

            def apart(src, tile, pad):
                dve.tensor_copy(proj[grp(0), tile, :], src[grp(0), :])
                return dve.tensor_copy(pad[grp(1), :], src[grp(1), :])

            def acc_banks(halves=2):
                for t in range(TT):
                    for half in range(halves):
                        if (t, half) == (TT - 1, halves - 1):
                            dve.wait_ge(chunk_used, at[0])
                        else:
                            dve.wait_ge(acc_full, due(acc_full))
                        yield t, half, acc[:, t * halves + half, :]

            def owe_split():
                if at[0] + AHEAD < N_CHUNKS:
                    owed.append(at[0] + AHEAD)
                at[0] += 1

            def pay():
                while owed:
                    c = owed.pop()
                    split(c, c % RING)

            def t_values(dst, width, chunks, owe=False):
                ahead(chunks - 1)
                owe_split() if owe else ahead()
                for t, half, bank in acc_banks(2 if width == D else 1):
                    w = min(width, 512)
                    dve.tensor_copy(dst[:, t, half * 512:half * 512 + w],
                                    bank[:, 0:w]).then_inc(*sent.one(acc_done))

            def residual(scale, chunks):
                ahead(chunks - 1)
                owe_split()
                for t, half, bank in acc_banks():
                    ht = h[:, t, half * 512:(half + 1) * 512]
                    dve.scalar_tensor_tensor(ht, bank, scale, ht, ALU.mult, ALU.add).then_inc(*sent.one(acc_done))

            def ffn():
                base, g0, bank0 = at[0], hidden[0], jobs[0]

                def step_in(c, j, slot, r, g):
                    split(c + AHEAD, slot)
                    dve.wait_ge(act_ready, j + 1)
                    dve.tensor_tensor(ff_g[:, r, 0:T], ff_s[:, r, 0:T], mid[:, (bank0 + r) % 2, T:2 * T],
                                      ALU.mult).then_inc(g_ready, 1)
                    dve.wait_ge(ghi_ready, j + 1)
                    dve.tensor_tensor(g_lo[:, g, :], ff_g[:, r, 0:T], g_hi[:, g, :],
                                      ALU.subtract).then_inc(glo_ready, 1)

                for j in range(4):
                    step_in(base + j, g0 + j, (base + j + AHEAD) % RING, j % 2, j % 4)
                split(base + 4 + AHEAD, (base + 4 + AHEAD) % RING)
                first, loops = base + 5, (FF_TILES // 2 - 3) // 2
                with dve.Fori(0, loops) as i:
                    for b in range(2):
                        s = first + 3 * b
                        for n in range(2):
                            step_in(i * 6 + (s + n), i * 4 + (g0 + 4 + 2 * b + n), (s + n + AHEAD) % RING, n,
                                    2 * b + n)
                        split(i * 6 + (s + 2 + AHEAD), (s + 2 + AHEAD) % RING)
                c, j = first + 6 * loops, 4 + 4 * loops
                for n in range(2):
                    step_in(c + n, g0 + j + n, (c + n + AHEAD) % RING, n, (j + n) % 4)
                hidden[0] += FF_TILES
                at[0] = c + 2
                residual(0.5, 2)

            def mlp():
                base, s0 = at[0], hidden[0]

                def step_in(c, j, slot, r):
                    if slot is not None:
                        split(c + AHEAD, slot)
                    dve.wait_ge(act_ready, j + 1)
                    dve.tensor_tensor(ff_g[:, r, :], ff_s[:, r, :], ff_s[:, r, :], ALU.mult).then_inc(g_ready, 1)
                    dve.wait_ge(ghi_ready, j + 1)
                    dve.wait_ge(g_ready, j + 1)
                    dve.tensor_tensor(g_lo[:, 2 * r:2 * r + 2, :], ff_g[:, r, :].rearrange(
                        "p (k q) -> p k q", k=2), g_hi[:, 2 * r:2 * r + 2, :], ALU.subtract).then_inc(glo_ready, 1)

                def steps(j):
                    c = base + 2 * j - 1
                    step_in(c, s0 + j, (c + AHEAD) % RING if c + AHEAD < N_CHUNKS else None, j % 3)
                    if c + 1 + AHEAD < N_CHUNKS:
                        split(c + 1 + AHEAD, (c + 1 + AHEAD) % RING)

                step_in(base, s0, (base + AHEAD) % RING, 0)
                for j in range(1, 4):
                    steps(j)
                loops = (MLP_STEPS - 4) // 3
                if base + MLP_CHUNKS == N_CHUNKS:
                    loops -= 1
                with dve.Fori(0, loops) as i:
                    for b in range(3):
                        s = base + 7 + 2 * b
                        step_in(i * 6 + s, i * 3 + (s0 + 4 + b), (s + AHEAD) % RING, (4 + b) % 3)
                        split(i * 6 + (s + 1 + AHEAD), (s + 1 + AHEAD) % RING)
                for j in range(4 + 3 * loops, MLP_STEPS):
                    steps(j)
                hidden[0] += MLP_STEPS
                at[0] = base + MLP_CHUNKS - 1
                residual(1.0, 1)

            def attention(n_units, scale, finish, combine=None, tile_of=None, full=False, maps=1, sink=False,
                          beside=None):
                segs = [(0, T), (T, T)] if full else SEG
                base, e0 = tiles[0], scored[0]
                seen = [-1]

                def unit(u):
                    k = None
                    if tile_of is not None:
                        k = base + tile_of(u)
                        if k != seen[0]:
                            dve.wait_ge(bias_full[k % BIAS_SLOTS], 16 * (k // BIAS_SLOTS + 1))
                            seen[0] = k
                    for _ in range(maps):
                        e = scored[0]
                        scored[0] += 1
                        bank = job()
                        if e >= 2:
                            dve.wait_ge(exp_ready, e - 1)
                        for qt in range(TT):
                            a, n = segs[qt]
                            b = zero[:].to_broadcast([P, n]) if k is None else bias[:, k % BIAS_SLOTS, a:a + n]
                            ins = dve.tensor_tensor_reduce(N_[:, e % 2, a:a + n], bank[:, a:a + n], b, -scale,
                                                           -NEG, ALU.add, ALU.min, nmax[:, e % 4, qt:qt + 1])
                        if sink:
                            own(ins)
                            ins = dve.tensor_scalar(nmax[:, e % 4, 0:2], nmax[:, e % 4, 0:2],
                                                    nsink[:, u:u + 1], None, ALU.min)
                        ins.then_inc(mid_done, 1)
                    if k is not None:
                        while len(bias_used_at) <= k:
                            bias_used_at.append(0)
                        bias_used_at[k] = jobs[0]

                def output(u):
                    s = (e0 + u * maps) % 4
                    if maps == 1:
                        dve.wait_ge(exp_ready, e0 + u + 1)
                        if sink:
                            own(dve.tensor_tensor(rsum[:, s, 0:2], rsum[:, s, 0:2], esink[:, s, :], ALU.add))
                        own(dve.reciprocal(rinv[:, s, 0:2], rsum[:, s, 0:2]))
                    n = sent.total(o_done)
                    dve.wait_ge(o_full, n + 1)
                    finish(u, acc[:, 2 + n % 2, :], rinv[:, s, :]).then_inc(*sent.one(o_done))

                unit(0)
                for u in range(n_units):
                    if u + 1 < n_units:
                        unit(u + 1)
                    if combine is not None:
                        combine(u, e0)
                    if beside:
                        beside(u)
                    if u >= 1:
                        output(u - 1)
                output(n_units - 1)
                if tile_of is not None:
                    tiles[0] = base + tile_of(n_units - 1) + 1

            def plain_out(base, w):
                def finish(u, bank, inv):
                    for qt in range(TT):
                        ins = dve.tensor_scalar(obuf[:, qt, base + u * w:base + (u + 1) * w],
                                                bank[:, qt * w:(qt + 1) * w], inv[:, qt:qt + 1], None, ALU.mult)
                    return ins
                return finish

            def nsa_out(u, bank, inv):
                hd, branch = u // 2, u % 2
                own(dve.tensor_tensor(inv[:, 0:2], inv[:, 0:2], gate[:, :, hd * 3 + 1 + branch], ALU.mult))
                if branch:
                    dve.wait_ge(o_done, sent.total(o_done))
                for qt in range(TT):
                    o = obuf[:, qt, hd * DH:(hd + 1) * DH]
                    ins = dve.scalar_tensor_tensor(o, bank[:, qt * DH:(qt + 1) * DH], inv[:, qt:qt + 1], o,
                                                   ALU.mult, ALU.add)
                return ins

            def diff_combine(u, e0):
                e = e0 + 2 * u
                dve.wait_ge(exp_ready, e + 2)
                a, b = e % 4, (e + 1) % 4
                dve.reciprocal(rinv[:, a, 0:2], rsum[:, a, 0:2])
                own(dve.reciprocal(rinv[:, b, 0:2], rsum[:, b, 0:2]))
                own(dve.tensor_scalar(rinv[:, b, 0:2], rinv[:, b, 0:2], lam[:, 3:4], None, ALU.mult))
                for qt in range(TT):
                    c, n = SEG[qt]
                    ins = dve.tensor_scalar(P_[:, b, c:c + n], P_[:, b, c:c + n], rinv[:, b, qt:qt + 1], None,
                                            ALU.mult)
                own(ins)
                if u >= 2:
                    dve.wait_ge(turned_full, sent.total(o_done) + 1)
                for qt in range(TT):
                    c, n = SEG[qt]
                    ins = dve.scalar_tensor_tensor(PC_[:, u % 2, c:c + n], P_[:, a, c:c + n],
                                                   rinv[:, a, qt:qt + 1], P_[:, b, c:c + n], ALU.mult, ALU.add)
                ins.then_inc(pc_ready, 1)

            def diff_out(u, bank, inv):
                for qt in range(TT):
                    ins = dve.tensor_copy(obuf[:, qt, u * P:(u + 1) * P], bank[:, qt * P:(qt + 1) * P])
                return ins

            def blocks(v):
                if v:
                    dve.wait_ge(blkhi_ready, v)
                for g in range(2):
                    for par in range(2):
                        rows = grp(par)
                        src = proj[rows, KC + 2 * v + g, :].rearrange("p (c b) -> p b c", b=16)
                        bl = blk[rows, :].rearrange("p (j c) -> p j c", j=JJ)
                        for nx in range(2):
                            ins = dve.tensor_tensor(
                                bl[:, nx * 8:nx * 8 + 8, g * CBLK:(g + 1) * CBLK],
                                src[:, par:16:2, nx:nx + CBLK],
                                posT[rows, v, nx * 8:nx * 8 + 8].unsqueeze(2).to_broadcast([DH, 8, CBLK]),
                                ALU.add)
                ins.then_inc(blk_ready, 1)

            def blocks_lo(v):
                dve.wait_ge(blkhi_ready, v + 1)
                dve.tensor_tensor(blk_lo[:, 0:JJ * CCOLS], blk, blk_hi[:, 0:JJ * CCOLS],
                                  ALU.subtract).then_inc(blklo_ready, 1)

            def compressed_steps():
                used = [0]

                def bank_():
                    used[0] += 1
                    return acc[:, (used[0] - 1) % 2, :]

                def first_layer(v):
                    if v == 0:
                        pay()
                        blocks(1)
                    ahead()
                    owe_split()
                    dve.wait_ge(chunk_used, at[0])
                    dve.tensor_copy(pre[0:CCOLS, :], bank_()[0:CCOLS, 0:T]).then_inc(cmp_done, 1)

                def add_bias(v):
                    pay()
                    if v == 0:
                        blocks_lo(1)
                        dve.memset(vcd, 0.0)
                        dve.memset(kcT, 0.0)
                        dve.memset(hidd_flat, 0.0)
                        dve.memset(cp_flat, 0.0)
                    dve.wait_ge(cmp_full, v + 1)
                    bank = bank_()
                    for k in range(2):
                        ins = dve.tensor_scalar(hid[:, v, k, :], bank[:, k * CCOLS:(k + 1) * CCOLS],
                                                b1T[:, v, k:k + 1], None, ALU.add)
                    ins.then_inc(cmp_done, 1)

                def scalars():
                    dve.wait_ge(lam_exps, 1)
                    own(dve.tensor_tensor(lam[:, 2:3], lam[:, 0:1], lam[:, 1:2], ALU.subtract))
                    dve.tensor_scalar(lam[:, 3:4], lam[:, 2:3], LAMBDA_INIT, -1.0, ALU.add, ALU.mult)
                    dve.wait_ge(gexp_ready, 1)
                    own(dve.tensor_scalar(gate[:], gate[:], 1.0, None, ALU.add))
                    own(dve.reciprocal(gate[:], gate[:]))

                def second_layer():
                    scalars()
                    dve.wait_ge(gelu_ready, 1)
                    for k in range(2):
                        for g in range(2):
                            ins = dve.tensor_copy(hidd[:, k, g, :, 0:CBLK], hidg[:, 1, k, g * CBLK:(g + 1) * CBLK]
                                                  .unsqueeze(1).to_broadcast([P, 4, CBLK]))
                    ins.then_inc(hidd_ready, 1)
                    dve.wait_ge(cmp_full, 3)
                    bank = bank_()
                    for g in range(2):
                        c = slice(g * CBLK, (g + 1) * CBLK)
                        ins = dve.tensor_copy(kcT[grp(g), c], bank[grp(g), c])
                    ins.then_inc(cmp_done, 1)
                    dve.wait_ge(cmp_full, 4)
                    bank = bank_()
                    for g in range(2):
                        for r in range(4):
                            rows = slice(32 * r, 32 * r + 32)
                            ins = dve.tensor_copy(vcd[rows, g, r, :], bank[rows, g * DH:(g + 1) * DH])
                    ins.then_inc(cmp_done, 1)

                def less_maximum():
                    dve.wait_ge(cmp_full, 5)
                    scores = bank_()[:, 0:256].rearrange("p (a c) -> p a c", a=8)
                    for g in range(2):
                        ins = dve.scalar_tensor_tensor(cs[:, 8 * g:8 * g + 8, :],
                                                       scores[:, :, g * CBLK:(g + 1) * CBLK], ATTN_SCALE,
                                                       cbias[:, 8 * g:8 * g + 8, :], ALU.mult, ALU.add)
                    ins.then_inc(cmp_done, 1)
                    dve.wait_ge(cmp_done, 7)
                    own(dve.tensor_reduce(cst[:, 0, :], cs, AX.X, ALU.max))
                    dve.tensor_tensor(cs, cs, cst[:, 0, :].unsqueeze(2).to_broadcast([P, 16, CBLK]),
                                      ALU.subtract).then_inc(cs_ready, 1)

                def probabilities():
                    dve.wait_ge(ce_ready, 1)
                    own(dve.tensor_reduce(cst[:, 1, :], ce, AX.X, ALU.add))
                    own(dve.reciprocal(cst[:, 2, :], cst[:, 1, :]))
                    for g in range(2):
                        for qt in range(TT):
                            a = (g * 2 + qt) * 4
                            dve.tensor_tensor(cst[:, 2, a:a + 4], cst[:, 2, a:a + 4],
                                              gate[:, qt, 12 * g:12 * g + 12:3], ALU.mult)
                    own(dve.tensor_tensor(ce, ce, cmask, ALU.mult))
                    dve.tensor_tensor(cp[:, :, 0:CBLK], ce, cst[:, 2, :].unsqueeze(2).to_broadcast([P, 16, CBLK]),
                                      ALU.mult).then_inc(cp_ready, 1)

                def block_outputs():
                    for qt in range(TT):
                        dve.wait_ge(co_full, qt + 1)
                        dve.tensor_copy(obuf[:, qt, 0:512], acc[:, qt, :]).then_inc(*sent.one(co_done))
                    dve.wait_ge(co_done, TT)

                return [lambda: first_layer(0), lambda: add_bias(0), lambda: first_layer(1),
                        lambda: add_bias(1), second_layer, less_maximum, None, probabilities, None,
                        block_outputs]

            def mixer():
                dve.wait_ge(const_full, 16 * n_const)
                dve.tensor_scalar(nsink[:], sinkt[:], -1.0, None, ALU.mult)
                dve.tensor_scalar(subg[:], subg[:], 1.0 - LAMBDA_INIT, None, ALU.mult)
                for i in range(2):
                    ins = dve.tensor_tensor_reduce(lamv[:, 2 * i, :], lamv[:, 2 * i, :], lamv[:, 2 * i + 1, :], 1.0,
                                                   0.0, ALU.mult, ALU.add, lam[:, i:i + 1])
                ins.then_inc(lam_dots, 1)
                norm(h, fine=True)
                turned(fine=True)
                f_chunks(2, proj)
                ahead()
                bank = job(False)
                zero_halves(KS, mix_pad)
                apart(bank[:, 0:T], KS, mix_pad[0])
                apart(bank[:, T:2 * T], KW, mix_pad[1]).then_inc(mid_done, 1)
                ahead()
                bank = job(False)
                apart(bank[:, 0:T], KB, mix_pad[2])
                dve.tensor_copy(proj[:, QA, :], bank[:, T:2 * T]).then_inc(mid_done, 1)
                f_chunks(MIX_F - 5, proj, 8)
                f_chunks(1, proj, 14, 1)
                dve.wait_ge(mid_done, jobs[0])
                blocks(0)
                dve.memset(blk_hi[:, JJ * CCOLS:JJ * CCOLS + P].bitcast(F32), 0.0)
                dve.memset(blk_lo[:, JJ * CCOLS:JJ * CCOLS + P].bitcast(F32), 0.0)
                blocks_lo(0)
                t_values(vtok, MIXV_W, MIX_V, owe=True)
                steps = compressed_steps()
                attention(8, ATTN_SCALE, plain_out(512, DH), tile_of=lambda u: u, sink=True,
                          beside=lambda u: step(steps, u))
                attention(16, ATTN_SCALE, nsa_out, tile_of=lambda u: u // 2, beside=lambda u: step(steps, u + 8))
                turned()
                obuf_turned_at.append(jobs[0])
                residual(1.0, MIX_O)

            def even_mixer():
                norm(h, fine=True)
                turned(fine=True)
                f_chunks(2, proj)
                zero_halves(4, diff_pad)
                for i in range(2):
                    ahead()
                    bank = job(False)
                    for m in range(2):
                        ins = apart(bank[:, m * T:(m + 1) * T], 4 + 2 * i + m, diff_pad[2 * i + m])
                    ins.then_inc(mid_done, 1)
                f_chunks(1, proj, 8)
                t_values(cqs, CQ_W, 2)
                for t in range(TT):
                    dve.wait_ge(rstd_ready, due(rstd_ready))
                    for i, (a, n) in enumerate(((0, 2 * P), (2 * P, P))):
                        ins = dve.scalar_tensor_tensor(xn[:, t, a:a + n], cqs[:, t, a:a + n],
                                                       rstd[:, 2 * t + i:2 * t + i + 1], cqg[:, a:a + n],
                                                       ALU.mult, ALU.mult)
                    ins.then_inc(*sent.one(xn_ready))
                t_values(vtok, 512, 2)
                turned(CQ_W // P)
                for pair in range(4):
                    if pair == 3:
                        ahead()
                    bank = job(pair < 3)
                    if pair < 2:
                        dst = proj[:, 10 + 2 * pair:12 + 2 * pair, :].rearrange("p k q -> p (k q)")
                    else:
                        dst = memv[:, pair - 2, 0:2 * T]
                    dve.tensor_copy(dst, bank).then_inc(mid_done, 1)
                rope_from.append(jobs[0])
                norm(obuf)
                for pair in range(2):
                    bank = job()
                    dve.tensor_copy(memv[:, pair, 512:1024], bank).then_inc(mid_done, 1)
                t_values(vtok[:, :, 512:1024], 512, 1, owe=True)
                turned()
                attention(4, ATTN_SCALE, diff_out, combine=diff_combine, tile_of=lambda u: u, maps=2,
                          beside=lambda u: f_chunks(1, memkT[:, 2 * u:2 * u + 2, :]))
                dve.wait_ge(o_done, sent.total(o_done))
                for qt in range(TT):
                    for u in range(4):
                        k = qt * 4 + u
                        o = obuf[:, qt, u * P:(u + 1) * P]
                        ins = dve.tensor_tensor_reduce(junk[:, k * P:(k + 1) * P], o, o, 1.0, 0.0,
                                                       ALU.mult, ALU.add, sq[:, k:k + 1])
                ins.then_inc(dsq_ready, 1)

                def diff_norm():
                    dve.wait_ge(rstd_ready, due(rstd_ready))
                    for qt in range(TT):
                        for u in range(4):
                            o = obuf[:, qt, u * P:(u + 1) * P]
                            k = qt * 4 + u
                            ins = dve.scalar_tensor_tensor(o, o, rstd[:, k:k + 1], subg[:], ALU.mult, ALU.mult)
                    ins.then_inc(dnorm_ready, 1)

                def half_values(u):
                    if u == 2:
                        diff_norm()
                    if u % 2:
                        t_values(memv[:, :, (u // 2) * 512:(u // 2 + 1) * 512], 512, 1)
                    else:
                        ahead()

                attention(4, MLA_SCALE, plain_out(512, P), tile_of=lambda u: 0, beside=half_values)
                turned()
                residual(1.0, EV_O)

            def cross():
                norm(h, fine=True)
                turned(fine=True)
                f_chunks(4, proj)
                attention(4, XA_SCALE, plain_out(0, T), full=True)
                turned()
                obuf_turned_at.append(jobs[0])
                residual(1.0, 4)

            def odd_mixer():
                norm(h, fine=True)
                turned(fine=True)
                f_chunks(8, proj)
                norm(obuf)
                t_values(vtok, D, 4, owe=True)
                turned()
                mask0 = sbm[:, 0:T].unsqueeze(1).to_broadcast([P, 2, T])

                def masked(p):
                    b = 2 * (p % 2)
                    dve.wait_ge(z_full, p + 1)
                    dve.scalar_tensor_tensor(sb_m[:, p % 2, 0:2 * T].rearrange("p (a b) -> p a b", a=2),
                                             acc[:, b, :].rearrange("p (a b) -> p a b", a=2), ATTN_SCALE, mask0,
                                             ALU.mult, ALU.add)
                    dve.scalar_tensor_tensor(sb_m[:, p % 2, 2 * T:SBW], acc[:, b + 1, 0:T], ATTN_SCALE,
                                             sbm[:, T:2 * T], ALU.mult, ALU.add).then_inc(m_ready, 1)

                def output(p):
                    dve.wait_ge(so_full, p + 1)
                    for qt in range(TT):
                        for i, hh in enumerate(sb_heads(p)):
                            ins = dve.tensor_copy(obuf[:, qt, hh * DH:(hh + 1) * DH],
                                                  aux[:, 0, T + qt * P + i * DH:T + qt * P + (i + 1) * DH])
                    ins.then_inc(so_done, 1)

                def memory(p):
                    if p < 4:
                        dve.wait_ge(chunk_used, at[0])
                        dve.tensor_copy(memkT[:, 2 * p:2 * p + 2, :], (mid, aux)[p % 2][:, 1, :].rearrange(
                            "p (k q) -> p k q", q=T)).then_inc(side_done, 1)
                    elif p % 2:
                        dve.wait_ge(chunk_used, at[0])
                        for t in range(TT):
                            dve.tensor_copy(memv[:, t, (p // 2 - 2) * 512:(p // 2 - 1) * 512],
                                            (mid, aux)[t][:, 1, :]).then_inc(side_done, 1)

                masked(0)
                for p in range(8):
                    if p + 1 < 8:
                        if p >= 1:
                            dve.wait_ge(a_ready, p)
                        masked(p + 1)
                    dve.wait_ge(ln_ready, p + 1)
                    dve.scalar_tensor_tensor(sb_l[:, p % 2, :], sb_m[:, p % 2, :], 0.0, sb_l[:, p % 2, :], ALU.max,
                                             ALU.add).then_inc(sp_ready, 1)
                    if p < 7:
                        ahead()
                        memory(p)
                    else:
                        owe_split()
                    if p >= 1:
                        output(p - 1)
                    dve.wait_ge(s_full, p + 1)
                    m0, m1 = sb_m[:, p % 2, 0:2 * T], sb_m[:, p % 2, 2 * T:SBW]
                    dve.tensor_tensor(m0, m0, mid[:, 0, :], ALU.subtract)
                    dve.tensor_tensor(m1, m1, aux[:, 0, 0:T], ALU.subtract).then_inc(zs_ready, 1)
                memory(7)
                output(7)
                turned()
                residual(1.0, 4)

            norm(h, fine=True)
            split(0, 0)
            owed.append(1)
            turned(fine=True)
            ffn()
            mixer()
            norm(h, fine=True)
            turned(fine=True)
            ffn()
            final_norm()
            even_mixer()
            cross()
            norm(h, fine=True)
            turned(fine=True)
            mlp()
            odd_mixer()
            cross()
            norm(h, fine=True)
            turned(fine=True)
            mlp()
            final_norm()

        @block.scalar
        def _(act):
            sent, due = Tally(), Tally()
            at = [0]
            jobs = [0]
            hidden = [0]
            scored = [0]
            units = [0]

            def split(c, slot, chunk_waits):
                n = filled(c)
                used, arrived = chunk_waits
                if used is not None:
                    act.wait_ge(chunk_used, used)
                act.wait_ge(raw_full[slot], arrived)
                act.activation(w_hi[:, slot, 0:n], raw[:, slot, 0:n], ACT.Copy).then_inc(hi_ready, 1)

            def split_at(c):
                if c < N_CHUNKS:
                    split(c, c % RING, (c - RING + 1 if c >= RING else None, 16 * (c // RING + 1)))

            def split_in_loop(c, i, per):
                assert c not in FILLED
                split(c, c % RING, (i * per + (c - RING + 1), i * (16 * per // RING) + 16 * (c // RING + 1)))

            def ahead(n=1):
                for _ in range(n):
                    split_at(at[0] + AHEAD)
                    at[0] += 1

            def squares(src, ready):
                for t in range(TT):
                    for half in range(2):
                        ready(t, half)
                        if sent.total(sq_ready) > 1:
                            act.wait_ge(sq_ready, sent.total(sq_ready) - 1)
                        c = slice(half * 512, (half + 1) * 512)
                        act.activation(junk[:, c], src[:, t, c], ACT.Square, scale=D ** -0.5,
                                       accum_out=sq[:, 2 * t + half:2 * t + half + 1]).then_inc(*sent.one(sq_ready))

            def h_summed(t, half):
                act.wait_ge(acc_done, due.total(acc_done) - 3 + 2 * t + half)

            def h_normed(t, half):
                act.wait_ge(h_ready, due(h_ready))

            def loaded(sem_, value):
                return lambda t, half: act.wait_ge(sem_, value)

            def turned(tiles_=KT, fine=False):
                parts = turn_parts(tiles_, fine)
                for (t, a, n), bank in zip(parts, turn_banks(jobs[0], len(parts))):
                    act.wait_ge(mid_full, due(mid_full))
                    act.activation(xT_hi[:, a:a + n, t * P:(t + 1) * P],
                                   bank[:, 0:n * P].rearrange("p (k q) -> p k q", q=P),
                                   ACT.Copy).then_inc(thi_ready, 1)
                jobs[0] += len(parts)

            def mids(n, signalled):
                jobs[0] += n
                due(mid_full, signalled)

            def f_chunks(n):
                ahead(n)
                mids(n, 0)

            def t_chunks(n, halves=2):
                ahead(n)
                due(acc_done, TT * halves)

            def ffn():
                base, g0, bank0 = at[0], hidden[0], jobs[0]

                def step(c, j, r, g):
                    act.wait_ge(chunk_used, c + 1)
                    act.activation(ff_s[:, r, 0:T], mid[:, (bank0 + r) % 2, 0:T], ACT.Silu).then_inc(act_ready, 1)
                    act.wait_ge(g_ready, j + 1)
                    act.activation(g_hi[:, g, :], ff_g[:, r, 0:T], ACT.Copy).then_inc(ghi_ready, 1)

                for j in range(4):
                    split_at(base + j + AHEAD)
                    step(base + j, g0 + j, j % 2, j % 4)
                split_at(base + 4 + AHEAD)
                first, loops = base + 5, (FF_TILES // 2 - 3) // 2
                with act.Fori(0, loops) as i:
                    for b in range(2):
                        s = first + 3 * b
                        for n in range(2):
                            split_in_loop(s + n + AHEAD, i, 6)
                            step(i * 6 + (s + n), i * 4 + (g0 + 4 + 2 * b + n), n, 2 * b + n)
                        split_in_loop(s + 2 + AHEAD, i, 6)
                c, j = first + 6 * loops, 4 + 4 * loops
                for n in range(2):
                    split_at(c + n + AHEAD)
                    step(c + n, g0 + j + n, n, (j + n) % 4)
                hidden[0] += FF_TILES
                at[0] = c + 2
                t_chunks(2)

            def mlp():
                base, s0 = at[0], hidden[0]
                banks = [mid[:, jobs[0] % 2, :], mid[:, 1 - jobs[0] % 2, :], aux[:, 0, :]]

                def step(c, j, r, wait=True):
                    act.wait_ge(chunk_used, c + 1)
                    if wait:
                        act.wait_ge(glo_ready, j - 2)
                    act.activation(ff_s[:, r, :], banks[r], ACT.Relu).then_inc(act_ready, 1)
                    act.wait_ge(act_ready, j + 1)
                    act.activation(g_hi[:, 2 * r:2 * r + 2, :], ff_s[:, r, :].rearrange("p (k q) -> p k q", k=2),
                                   ACT.Square).then_inc(ghi_ready, 1)

                def steps(j):
                    c = base + 2 * j - 1
                    split_at(c + AHEAD)
                    step(c, s0 + j, j % 3, j >= 3)
                    split_at(c + 1 + AHEAD)

                split_at(base + AHEAD)
                step(base, s0, 0, False)
                for j in range(1, 4):
                    steps(j)
                loops = (MLP_STEPS - 4) // 3
                if base + MLP_CHUNKS == N_CHUNKS:
                    loops -= 1
                with act.Fori(0, loops) as i:
                    for b in range(3):
                        s = base + 7 + 2 * b
                        split_in_loop(s + AHEAD, i, 6)
                        step(i * 6 + s, i * 3 + (s0 + 4 + b), (4 + b) % 3)
                        split_in_loop(s + 1 + AHEAD, i, 6)
                for j in range(4 + 3 * loops, MLP_STEPS):
                    steps(j)
                hidden[0] += MLP_STEPS
                at[0] = base + MLP_CHUNKS - 1
                t_chunks(1)

            def attention(n_units, full=False, maps=1, sink=False, beside=None):
                segs = [(0, T), (T, T)] if full else SEG
                width = 2 * T if full else KEYCOLS

                def unit(u):
                    for _ in range(maps):
                        m, e = jobs[0], scored[0]
                        jobs[0] += 1
                        scored[0] += 1
                        due(mid_full)
                        act.wait_ge(mid_done, m + 1)
                        if u >= 2:
                            act.wait_ge(turned_full, u0 + u - 1) if maps == 1 else act.wait_ge(pc_ready, u - 1)
                        for qt in range(TT):
                            a, n = segs[qt]
                            if sink:
                                act.activation(esink[:, e % 4, qt:qt + 1], sinkt[:, u:u + 1], ACT.Exp,
                                               bias=nmax[:, e % 4, qt:qt + 1])
                            ins = act.activation(P_[:, e % 4, a:a + n], N_[:, e % 2, a:a + n], ACT.Exp,
                                                 bias=nmax[:, e % 4, qt:qt + 1], scale=-1.0,
                                                 accum_out=rsum[:, e % 4, qt:qt + 1])
                        ins.then_inc(exp_ready, 1)

                def copied(u):
                    n = u0 + u
                    act.wait_ge(turned_full, n + 1)
                    if n >= 2:
                        act.wait_ge(o_full, n - 1)
                    act.activation(PT_[:, n % 2, 0:width], aux[:, n % 2, 0:width],
                                   ACT.Copy).then_inc(turned_done, 1)

                u0 = units[0]
                unit(0)
                for u in range(n_units):
                    if u + 1 < n_units:
                        unit(u + 1)
                    if beside:
                        beside(u)
                    copied(u)
                units[0] += n_units

            def mixer():
                squares(h, h_summed)
                turned(fine=True)
                f_chunks(MIX_F)
                act.wait_ge(lam_dots, 1)
                act.activation(lam[:, 0:2], lam[:, 0:2], ACT.Exp).then_inc(lam_exps, 1)
                act.wait_ge(blk_ready, 1)
                act.activation(blk_hi[:, 0:JJ * CCOLS], blk, ACT.Copy).then_inc(blkhi_ready, 1)
                t_chunks(MIX_V, 1)
                act.wait_ge(acc_done, due.total(acc_done))
                act.activation(gate[:], vtok[:, :, GATE_COL:MIXV_W], ACT.Exp, scale=-1.0).then_inc(gexp_ready, 1)

                def second_blocks():
                    act.wait_ge(blk_ready, 2)
                    act.wait_ge(chunk_used, at[0])
                    act.activation(blk_hi[:, 0:JJ * CCOLS], blk, ACT.Copy).then_inc(blkhi_ready, 1)

                def gelu():
                    act.wait_ge(cmp_done, 4)
                    act.activation(hidg, hid, ACT.Gelu_apprx_tanh).then_inc(gelu_ready, 1)

                def exponentials():
                    act.wait_ge(cs_ready, 1)
                    act.activation(ce, cs, ACT.Exp).then_inc(ce_ready, 1)

                def copy_turned():
                    act.wait_ge(cpt_full, 1)
                    act.activation(cpT, acc[:, 1, :].rearrange("p (a q) -> p a q", a=4),
                                   ACT.Copy).then_inc(cpt_done, 1)

                steps = [lambda: ahead(2), second_blocks, lambda: ahead(2), gelu, None, None, exponentials, None,
                         copy_turned]
                attention(8, sink=True, beside=lambda u: step(steps, u))
                attention(16, beside=lambda u: step(steps, u + 8))
                turned()
                t_chunks(MIX_O)

            def even_mixer():
                squares(h, h_normed)
                turned(fine=True)
                f_chunks(EV_F)
                t_chunks(2, 1)
                for t in range(TT):
                    act.wait_ge(acc_done, due.total(acc_done) - 1 + t)
                    for i, (a, n) in enumerate(((0, 2 * P), (2 * P, P))):
                        ins = act.activation(junk[:, t * CQ_W + a:t * CQ_W + a + n], cqs[:, t, a:a + n], ACT.Square,
                                             accum_out=sq[:, 2 * t + i:2 * t + i + 1])
                    ins.then_inc(*sent.one(sq_ready))
                t_chunks(2, 1)
                turned(CQ_W // P)
                squares(obuf, loaded(mem_full, 16))
                ahead(1)
                mids(4, 3)
                mids(2, 2)
                t_chunks(1, 1)
                turned()
                attention(4, maps=2, beside=lambda u: f_chunks(1))
                attention(4, beside=lambda u: t_chunks(1, 1) if u % 2 else ahead())
                turned()
                t_chunks(EV_O)

            def cross():
                squares(h, h_summed)
                turned(fine=True)
                f_chunks(4)
                attention(4, full=True)
                turned()
                t_chunks(4)

            def odd_mixer():
                squares(h, h_summed)
                turned(fine=True)
                f_chunks(8)
                squares(obuf, loaded(mem_full, 32))
                t_chunks(4)
                turned()

                def own(ins):
                    ins.then_inc(*sent.one(act_own))
                    act.wait_ge(act_own, sent.total(act_own))

                def weights(p):
                    act.wait_ge(zs_ready, p + 1)
                    act.activation(sb_a[:, p % 2, :], sb_m[:, p % 2, :], ACT.Exp).then_inc(a_ready, 1)

                for p in range(8):
                    act.wait_ge(m_ready, p + 1)
                    l = sb_l[:, p % 2, :]
                    own(act.activation(l, sb_m[:, p % 2, :], ACT.Abs))
                    own(act.activation(l, l, ACT.Exp, scale=-1.0))
                    if p >= 1:
                        weights(p - 1)
                    act.activation(l, l, ACT.Ln, bias=1.0).then_inc(ln_ready, 1)
                    ahead()
                weights(7)
                turned()
                t_chunks(4)

            squares(h, loaded(x_full, 16))
            split_at(0)
            turned(fine=True)
            split_at(1)
            ffn()
            mixer()
            squares(h, h_summed)
            turned(fine=True)
            ffn()
            squares(h, h_summed)
            even_mixer()
            cross()
            squares(h, h_summed)
            turned(fine=True)
            mlp()
            odd_mixer()
            cross()
            squares(h, h_summed)
            turned(fine=True)
            mlp()
            squares(h, h_summed)

        @block.gpsimd
        def _(pool):
            sent, due = Tally(), Tally()
            norms = [0]
            loaded = [0]

            def own(ins):
                ins.then_inc(*sent.one(pool_own))
                pool.wait_ge(pool_own, sent.total(pool_own))

            def load_gain(k):
                if k < N_GAINS:
                    pool.dma_start(gain[:, k % 2, :],
                                   gains[k:k + 1, :].to_broadcast([P, D])).then_inc(gain_full[k % 2], 16)

            def inverse(a, n, width):
                own(pool.tensor_scalar(ms[:, a:a + n], sq[:, a:a + n], 1.0 / width, EPS, ALU.mult, ALU.add))

            def norm(in_place=False, fine=True):
                for t in range(TT):
                    pool.wait_ge(sq_ready, due(sq_ready, 2))
                    own(pool.tensor_scalar(ms[:, t:t + 1], sq[:, 2 * t:2 * t + 1], sq[:, 2 * t + 1:2 * t + 2], EPS,
                                           ALU.add, ALU.add))
                    pool.tensor_tensor(rstd[:, t:t + 1], ms[:, t:t + 1], nhalf[:, t:t + 1],
                                       ALU.pow).then_inc(*sent.one(rstd_ready))
                k = norms[0]
                norms[0] += 1
                s = h_ready if in_place else xn_ready
                n = due(s, 2 * TT if in_place else len(turn_parts(KT, fine)))
                if k + 2 < N_GAINS:
                    pool.wait_ge(s, n)
                    load_gain(k + 2)

            def biases(n):
                for _ in range(n):
                    k = loaded[0]
                    loaded[0] += 1
                    if k >= BIAS_SLOTS:
                        pool.wait_ge(mid_done, bias_used_at[k - BIAS_SLOTS])
                    pool.dma_start(bias[:, k % BIAS_SLOTS, :], bias_tiles[k]).then_inc(bias_full[k % BIAS_SLOTS], 16)

            def load_mem(n):
                pool.wait_ge(mid_done, obuf_turned_at[n])
                pool.dma_start(obuf[:], mem.rearrange("(t p) d -> p t d", p=P)).then_inc(mem_full, 16)

            def rope():
                pool.wait_ge(const_full, 16 * n_const)
                pool.wait_ge(mid_done, rope_from[0])
                cos, sin = ropet[:, 0, :], ropet[:, 1, :]
                for a in (rot[0], rot[1], proj[:, 8, :]):
                    pool.tensor_tensor(a, a, cos, ALU.mult)
                for b in (rot[2], rot[3], proj[:, 9, :]):
                    ins = pool.tensor_tensor(b, b, sin, ALU.mult)
                own(ins)
                pool.tensor_tensor(proj[:, 14, :], rot[0], rot[2], ALU.add)
                own(pool.tensor_tensor(proj[:, 15, :], rot[1], rot[3], ALU.add))
                own(pool.tensor_tensor(rope_pad[grp(1), :], proj[grp(1), 8, :], proj[grp(1), 9, :], ALU.add))
                own(pool.tensor_tensor(proj[grp(0), 8, :], proj[grp(0), 8, :], proj[grp(0), 9, :], ALU.add))
                own(pool.memset(rope_pad[grp(0), :], 0.0))
                pool.memset(proj[grp(1), 8, :], 0.0).then_inc(rope_ready, 1)
                pool.wait_ge(rope_ready, 1)

            load_gain(0)
            load_gain(1)
            own(pool.memset(nhalf[:], -0.5))
            biases(BIAS_SLOTS)
            norm()
            norm()
            biases(16 - BIAS_SLOTS)
            load_mem(0)
            norm()
            norm(True)
            norm()
            biases(3)
            for t in range(TT):
                pool.wait_ge(sq_ready, due(sq_ready))
                inverse(2 * t, 1, 2 * P)
                inverse(2 * t + 1, 1, P)
                pool.tensor_tensor(rstd[:, 2 * t:2 * t + 2], ms[:, 2 * t:2 * t + 2], nhalf[:, 0:2],
                                   ALU.pow).then_inc(*sent.one(rstd_ready))
            due(xn_ready, TT)
            norm(fine=False)
            rope()
            biases(2)
            pool.wait_ge(dsq_ready, 1)
            inverse(0, 8, P)
            pool.tensor_tensor(rstd[:, 0:8], ms[:, 0:8], nhalf[:, 0:8], ALU.pow).then_inc(*sent.one(rstd_ready))
            norm()
            load_mem(1)
            norm()
            norm()
            norm(fine=False)
            norm()
            norm()
            norm(True)

        @block.sync
        def _(sp):
            sp.dma_start(h[:], x.rearrange("(t p) d -> p t d", p=P)).then_inc(x_full, 16)
            sp.dma_start(ident[:], squares_in[0]).then_inc(ident_full, 16)
            for c in range(RING):
                sp.dma_start(raw[:, c, :], stream[c]).then_inc(raw_full[c], 16)
            consts = [(tri, squares_in[1]), (ones, squares_in[2]),
                      (zero, squares_in[3, 0:1, 0:1].to_broadcast([P, 1])), (sbm, sb_mask), (ropet, rope),
                      (cbias, cmp_bias), (cmask, cmp_mask), (cqg, cq_gain.to_broadcast([P, CQ_W])),
                      (subg, sub_gain.to_broadcast([P, P])), (sinkt, sinks.to_broadcast([P, 8])),
                      (posT, cmp_pos), (b1T, cmp_b1), (w2k, cmp_w2k), (w2v, cmp_w2v)]
            consts += [(lamv[:, i, :], lam_vecs[i:i + 1, :].to_broadcast([P, DH])) for i in range(4)]
            assert len(consts) == n_const
            for dst, src in consts:
                sp.dma_start(dst[:], src).then_inc(const_full, 16)
            rounds = N_CHUNKS // RING
            with sp.Fori(1, rounds) as i:
                for s in range(RING):
                    sp.wait_ge(lo_ready, i * RING + (s + 1 - RING))
                    sp.dma_start(raw[:, s, :], stream[i * RING + s]).then_inc(raw_full[s], 16)
            for c in range(rounds * RING, N_CHUNKS):
                sp.wait_ge(lo_ready, c - RING + 1)
                sp.dma_start(raw[:, c % RING, :], stream[c]).then_inc(raw_full[c % RING], 16)
            for t in range(TT):
                sp.wait_ge(last_h[0], last_h[1] - 2 * (TT - 1 - t))
                sp.dma_start(out[t * P:(t + 1) * P, :], h[:, t, :]).then_inc(out_full, 16)
            sp.wait_ge(out_full, 16 * TT)



def weight_stream(w):
    chunks = []

    def put(a):
        a = a.reshape(P, -1)
        full = np.zeros((P, CH), np.float32)
        full[:, :a.shape[1]] = a
        chunks.append(full)

    def f_chunk(m, cols):
        put(m[:, cols].reshape(-1, P, len(cols)).transpose(1, 0, 2))

    def f_tiles(m, tiles):
        for i in range(0, len(tiles), 2):
            f_chunk(m, np.concatenate(tiles[i:i + 2]))

    def t_chunks(m, kts):
        for i in range(0, m.shape[0] // P, kts):
            put(m[i * P:(i + kts) * P].reshape(kts, P, m.shape[1]).transpose(1, 0, 2))

    def cols(a, n=P):
        return np.arange(a, a + n)

    def ffn(w_in, w_out):
        def ins(j):
            f_chunk(w_in, np.concatenate([cols(j * P), cols(D_FF + j * P)]))

        def outs(k):
            t_chunks(w_out[2 * k * P:2 * (k + 1) * P], 2)

        for j in range(4):
            ins(j)
        outs(0)
        for k in range(1, FF_TILES // 2 - 1):
            ins(2 * k + 2)
            ins(2 * k + 3)
            outs(k)
        outs(FF_TILES // 2 - 1)

    def mlp(w1, w2):
        f_chunk(w1, cols(0, 2 * P))
        for j in range(1, MLP_STEPS):
            f_chunk(w1, cols(j * 2 * P, 2 * P))
            t_chunks(w2[(j - 1) * 2 * P:j * 2 * P], 2)
        t_chunks(w2[(MLP_STEPS - 1) * 2 * P:], 2)

    def mixer():
        m = w["w_mix_in"][0]
        kv = 512
        qb = 512 + 768 + 24
        kvb = qb + 512
        tiles = [np.tile(cols(kv + b * P + g * DH, DH), 2) for b in (0, 1) for g in (0, 1)]
        tiles += [cols(kv + 2 * P), cols(kv + 4 * P), cols(kvb)]
        for q in (0, qb):
            tiles += [np.concatenate([cols(q + r * DH, DH), cols(q + (4 + r) * DH, DH)]) for r in range(4)]
        f_tiles(m, tiles)
        t_chunks(m[:, np.concatenate([cols(kv + 3 * P), cols(kv + 5 * P), cols(kvb + P), cols(kv + 768, 24)])], 4)
        for name in ("cmp_k_w1", "cmp_v_w1"):
            t_chunks(w[name][0], 8)
        t_chunks(w["w_mix_out"][0], 2)

    def even():
        m = w["ev_w_in_2"][0]
        kr = 512 * 3 + 256 + 128
        swapped = np.concatenate([cols(32, 32), cols(0, 32)])
        tiles = [cols(i * P) for i in range(8)] + [np.tile(cols(kr, DH), 2), np.tile(kr + swapped, 2)]
        f_tiles(m, tiles)
        t_chunks(m[:, 1536:1536 + CQ_W], 4)
        t_chunks(m[:, 1024:1536], 4)
        u = w["mla_w_uq_2"][0]
        nope = [cols(hd * 192) for hd in range(4)]
        rope = [cols(hd * 192 + P, DH) for hd in range(4)]
        rope_swapped = [hd * 192 + P + swapped for hd in range(4)]
        t_chunks(u[:, np.concatenate(nope + rope + rope_swapped)], 2)
        u = w["mla_w_ukv_2"][0]
        t_chunks(u[:, np.concatenate([cols(hd * T) for hd in range(4)] + [cols(hd * T + P) for hd in range(4)])], 1)
        memory(0)
        t_chunks(w["ev_w_out_2"][0], 2)

    def memory(l):
        kv = w["xa_wkv_2"][l]
        f_tiles(kv, [cols(i * P) for i in range(8)])
        t_chunks(kv[:, D:D + 512], 4)
        t_chunks(kv[:, D + 512:], 4)

    def cross(l):
        f_tiles(w["xa_wq_2"][l], [cols(i * P) for i in range(8)])
        t_chunks(w["xa_wo_2"][l], 2)

    def odd():
        m = w["sb_w_in_2"][0]
        f_tiles(m, [cols(i * P) for i in range(16)])
        t_chunks(m[:, 2 * D:], 2)
        memory(1)
        t_chunks(w["sb_w_out_2"][0], 2)

    ffn(w["ffn1_w_in"][0], w["ffn1_w_out"][0])
    mixer()
    ffn(w["ffn2_w_in"][0], w["ffn2_w_out"][0])
    even()
    cross(0)
    mlp(w["mlp_w1_2"][0], w["mlp_w2_2"][0])
    odd()
    cross(1)
    mlp(w["mlp_w1_2"][1], w["mlp_w2_2"][1])
    assert len(chunks) == N_CHUNKS
    return np.stack(chunks)


def shape_constants():
    q, k = np.arange(T)[:, None], np.arange(T)[None, :]
    dist = (q - k).astype(np.float32)

    def tile(values, allowed, scale):
        b = np.where(allowed, values, NEG) / scale
        return np.concatenate([b[:P, :P], b[P:, :]], axis=1).astype(np.float32)

    slopes8 = 2.0 ** (-8.0 * np.arange(1, 9) / 8)
    slopes4 = 2.0 ** (-8.0 * np.arange(1, 5) / 4)
    causal = dist >= 0
    chunked = (k // 64) <= (q // 64)
    tiles = [tile(-s * dist, causal & (dist < 128), ATTN_SCALE) for s in slopes8]
    tiles += [tile(-s * dist, causal, ATTN_SCALE) for s in slopes8]
    tiles += [tile(-s * np.abs(dist), chunked, ATTN_SCALE) for s in slopes4]
    tiles += [tile(0 * dist, chunked, MLA_SCALE)]
    strict = np.where(q.T > k.T, 0.0, NEG).astype(np.float32)
    sb_mask = np.concatenate([strict[:P, :], strict[P:, P:], strict[P:, P:]], axis=1)
    end = np.arange(CBLK) * 16 + 31
    cbias = np.zeros((P, 2, TT, 4, CBLK), np.float32)
    cmask = np.zeros((P, 2, TT, 4, CBLK), np.float32)
    for qt in range(TT):
        d = (qt * P + np.arange(P))[:, None] - end[None, :]
        for g in range(2):
            for r in range(4):
                cbias[:, g, qt, r] = np.where(d >= 0, -slopes8[g * 4 + r] * d, NEG)
                cmask[:, g, qt, r] = d >= 0
    inv = (10000.0 ** (-np.arange(32, dtype=np.float32) / 32)).astype(np.float32)
    ang = inv[:, None] * np.arange(T, dtype=np.float32)[None, :]
    cos, sin = np.cos(ang), np.sin(ang)
    rope = np.stack([np.concatenate([cos] * 4), np.concatenate([-sin, sin] * 2)], axis=1).astype(np.float32)
    eye, tri = np.eye(P), np.tril(np.ones((P, P)))
    squares = np.stack([eye, tri, np.ones((P, P)), np.zeros((P, P))]).astype(np.float32)
    return {
        "bias_tiles": np.stack(tiles), "sb_mask": sb_mask.astype(np.float32),
        "cmp_bias": cbias.reshape(P, 16, CBLK), "cmp_mask": cmask.reshape(P, 16, CBLK),
        "rope": rope, "squares_in": squares,
    }


def kernel(**inputs):
    import concourse.bacc as _bacc
    from concourse.bass_utils import run_bass_kernel_spmd as _run

    w = {n: np.asarray(a) for n, a in inputs.items()}
    arrays = {
        "stream": weight_stream(w),
        "x": w["x"][0],
        "mem": w["mem_2"][0],
        "gains": np.stack([w["ffn1_norm"][0], w["mix_norm"][0], w["ffn2_norm"][0], w["final_norm"],
                           w["ev_norm_2"][0], w["xa_mem_norm_2"][0], w["xa_norm_2"][0], w["mlp_norm_2"][0],
                           w["od_norm_2"][0], w["xa_mem_norm_2"][1], w["xa_norm_2"][1], w["mlp_norm_2"][1],
                           w["final_norm_2"]]),
        "cq_gain": np.concatenate([w["mla_g_cq_2"], w["mla_g_ckv_2"]], axis=1),
        "sub_gain": w["diff_subln_2"],
        "lam_vecs": np.concatenate([w["diff_lq1_2"], w["diff_lk1_2"], w["diff_lq2_2"], w["diff_lk2_2"]]),
        "sinks": w["swa_sinks"],
        "cmp_pos": np.stack([w[n][0].reshape(JJ, P).T for n in ("cmp_k_pos", "cmp_v_pos")], axis=1),
        "cmp_b1": np.stack([w[n][0].reshape(2, P).T for n in ("cmp_k_b1", "cmp_v_b1")], axis=1),
        "cmp_w2k": np.concatenate([w["cmp_k_w2"][0].reshape(2, P, DH)] * 2, axis=2).transpose(1, 0, 2),
        "cmp_w2v": w["cmp_v_w2"][0].reshape(2, P, DH).transpose(1, 0, 2),
        **shape_constants(),
    }
    nc = _bacc.Bacc("TRN2", target_bir_lowering=False, num_devices=1)
    args = {}
    for n in arrays:
        arrays[n] = np.ascontiguousarray(arrays[n])
        args[n] = nc.dram_tensor(f"in_{n}", arrays[n].shape, F32, kind="ExternalInput").ap()
    args["out"] = nc.dram_tensor("out_0", (T, D), F32, kind="ExternalOutput").ap()
    program(nc, **args)
    r = _run(nc, [{f"in_{n}": a for n, a in arrays.items()}], core_ids=[0])
    return r.results[0]["out_0"].reshape(1, T, D)
```
